# Optimizing a Trainium2 kernel written in Bass

```python
import jax
import jax.numpy as jnp
from jax import lax
import numpy as np
import math

D_MODEL = 1024
BATCH = 1
SEQ = 256
DEPTH = 2

HEAD_DIM = 64
ATTN_Q_HEADS = 8
ATTN_KV_HEADS = 2
ATTN_GROUP = ATTN_Q_HEADS // ATTN_KV_HEADS
ATTN_WIDTH = ATTN_Q_HEADS * HEAD_DIM
ATTN_KV_WIDTH = ATTN_KV_HEADS * HEAD_DIM
WINDOW = 128
ATTN_BLOCK = 128
RWKV_HEADS = 8
RWKV_WIDTH = RWKV_HEADS * HEAD_DIM
DECAY_LORA = 64
ICLR_LORA = 64
GATE_LORA = 128
RWKV_SIZES = (RWKV_WIDTH, RWKV_WIDTH, RWKV_WIDTH, DECAY_LORA, ICLR_LORA, GATE_LORA)
RWKV_COLS = sum(RWKV_SIZES)
RWKV_LN_EPS = 64e-5
RET_HEADS = 8
RET_WIDTH = RET_HEADS * HEAD_DIM
RET_CHUNK = 128
ROPE_BASE = 10000.0
N_BRANCH = 3
IN_SIZES = (ATTN_WIDTH, ATTN_KV_WIDTH, ATTN_KV_WIDTH, RWKV_COLS,
            RET_WIDTH, RET_WIDTH, RET_WIDTH, RET_WIDTH, N_BRANCH * D_MODEL)
IN_WIDTH = sum(IN_SIZES)
D_FF = -((-8 * D_MODEL) // (3 * 256)) * 256
NORM_EPS = 1e-6


def _split(t, sizes):
    out, start = [], 0
    for s in sizes:
        out.append(t[..., start:start + s])
        start += s
    return out

def _rms(x, eps=NORM_EPS):
    xf = x.astype(jnp.float32)
    return (xf * lax.rsqrt(jnp.mean(xf * xf, axis=-1, keepdims=True) + eps)).astype(x.dtype)

def sliding_window_attention(q, k, v, sinks):
    B, T = q.shape[0], q.shape[1]
    C = ATTN_BLOCK
    NB = T // C
    qb = q.reshape(B, NB, C, ATTN_KV_HEADS, ATTN_GROUP, HEAD_DIM)

    def band(t):
        tb = t.reshape(B, NB, C, ATTN_KV_HEADS, HEAD_DIM)
        prev = jnp.concatenate([jnp.zeros_like(tb[:, :1]), tb[:, :-1]], axis=1)
        return jnp.concatenate([prev, tb], axis=2)

    kb, vb = band(k), band(v)
    s = jnp.einsum('bnqhgd,bnshd->bnhgqs', qb, kb).astype(jnp.float32) * (HEAD_DIM ** -0.5)
    qi = jnp.arange(C)[:, None]
    si = jnp.arange(2 * C)[None, :]
    rel = qi + C - si
    key_pos = jnp.arange(NB)[:, None, None] * C + si[None] - C
    mask = (rel >= 0) & (rel < WINDOW) & (key_pos >= 0)
    s = jnp.where(mask[None, :, None, None], s, -jnp.inf)
    sink = sinks.astype(jnp.float32).reshape(ATTN_KV_HEADS, ATTN_GROUP)[None, None, :, :, None, None]
    m = jnp.maximum(jnp.max(s, axis=-1, keepdims=True), sink)
    p = jnp.exp(s - m)
    p = p / (jnp.sum(p, axis=-1, keepdims=True) + jnp.exp(sink - m))
    o = jnp.einsum('bnhgqs,bnshd->bnqhgd', p.astype(v.dtype), vb)
    return o.reshape(B, T, ATTN_WIDTH)

def rwkv7_time_mix(h, shift_mu, w0, w2, a0, a2, g2, k_k, k_a, r_k, lnx_g, lnx_b):
    B, T = h.shape[0], h.shape[1]
    H, N = RWKV_HEADS, HEAD_DIM
    h_prev = jnp.pad(h, ((0, 0), (1, 0), (0, 0)))[:, :-1]
    z = h + shift_mu * (h_prev - h)
    r, k, v, wd, ad, gd = _split(z, RWKV_SIZES)
    w_log = -jax.nn.softplus(-(w0 + jnp.tanh(wd) @ w2)) - 0.5
    decay = jnp.exp(-jnp.exp(w_log.astype(jnp.float32)))
    a = jax.nn.sigmoid(a0 + ad @ a2)
    g = jax.nn.sigmoid(gd) @ g2
    kk = (k * k_k).reshape(B, T, H, N).astype(jnp.float32)
    kk = kk / jnp.maximum(jnp.linalg.norm(kk, axis=-1, keepdims=True), 1e-12)
    k = k * (1.0 + (a - 1.0) * k_a)

    def heads(t):
        return t.reshape(B, T, H, N).astype(jnp.float32)

    r_h, k_h, v_h, a_h, w_h = heads(r), heads(k), heads(v), heads(a), heads(decay)
    xs = tuple(t.transpose(1, 0, 2, 3) for t in (r_h, w_h, k_h, v_h, -kk, kk * a_h))

    def step(S, inp):
        r_t, w_t, k_t, v_t, a_t, b_t = inp
        Sa = jnp.einsum('bhvk,bhk->bhv', S, a_t)
        S = S * w_t[:, :, None, :] + Sa[..., None] * b_t[:, :, None, :] + v_t[..., None] * k_t[:, :, None, :]
        return S, jnp.einsum('bhvk,bhk->bhv', S, r_t)

    S0 = jnp.zeros((B, H, N, N), jnp.float32)
    _, y = lax.scan(step, S0, xs)
    y = y.transpose(1, 0, 2, 3)
    mu = jnp.mean(y, axis=-1, keepdims=True)
    var = jnp.mean(jnp.square(y - mu), axis=-1, keepdims=True)
    y = ((y - mu) * lax.rsqrt(var + RWKV_LN_EPS)).reshape(B, T, RWKV_WIDTH)
    y = y * lnx_g.astype(jnp.float32) + lnx_b.astype(jnp.float32)
    bonus = jnp.sum(r_h * k_h * r_k.astype(jnp.float32), axis=-1, keepdims=True) * v_h
    y = (y + bonus.reshape(B, T, RWKV_WIDTH)) * g.astype(jnp.float32)
    return y.astype(h.dtype)

def _rotary(x, pos):
    half = HEAD_DIM // 2
    inv_freq = 1.0 / (ROPE_BASE ** (jnp.arange(half, dtype=jnp.float32) * 2.0 / HEAD_DIM))
    ang = pos.astype(jnp.float32)[:, None] * inv_freq[None, :]
    cos, sin = jnp.cos(ang)[:, None, :], jnp.sin(ang)[:, None, :]
    x1, x2 = x[..., :half], x[..., half:]
    return jnp.concatenate([x1 * cos - x2 * sin, x2 * cos + x1 * sin], axis=-1)

def retention(q, k, v, gate):
    B, T = q.shape[0], q.shape[1]
    H, d, C = RET_HEADS, HEAD_DIM, RET_CHUNK
    NC = T // C
    pos = jnp.arange(T)
    qh = _rotary(q.reshape(B, T, H, d).astype(jnp.float32), pos)
    kh = _rotary(k.reshape(B, T, H, d).astype(jnp.float32), pos) * (d ** -0.5)
    vh = v.reshape(B, T, H, d).astype(jnp.float32)
    log_gamma = jnp.log1p(-jnp.power(2.0, -5.0 - jnp.arange(H, dtype=jnp.float32)))
    idx = jnp.arange(C, dtype=jnp.float32)
    diff = idx[:, None] - idx[None, :]
    dmat = jnp.where(diff >= 0, jnp.exp(log_gamma[:, None, None] * jnp.maximum(diff, 0.0)), 0.0)
    xi = jnp.exp(log_gamma[:, None] * (idx[None, :] + 1.0))
    zeta = jnp.exp(log_gamma[:, None] * (C - 1.0 - idx[None, :]))
    chunk_decay = jnp.exp(log_gamma * C)
    qc = qh.reshape(B, NC, C, H, d)
    kc = kh.reshape(B, NC, C, H, d)
    vc = vh.reshape(B, NC, C, H, d)
    s = jnp.einsum('bnihd,bnjhd->bnhij', qc, kc) * dmat
    inner = jnp.einsum('bnhij,bnjhe->bnihe', s, vc)
    kv = jnp.einsum('bnjhd,bnjhe,hj->nbhde', kc, vc, zeta)

    def step(R, kv_n):
        return R * chunk_decay[None, :, None, None] + kv_n, R

    _, r_prev = lax.scan(step, jnp.zeros((B, H, d, d), jnp.float32), kv)
    cross = jnp.einsum('bnihd,nbhde,hi->bnihe', qc, r_prev, xi)
    o = _rms((inner + cross).reshape(B, T, H, d)).reshape(B, T, RET_WIDTH)
    o = o * jax.nn.silu(gate.astype(jnp.float32))
    return o.astype(q.dtype)

def hybrid_layer(x, norm1_g, w_in, attn_q_norm_g, attn_k_norm_g, attn_sinks, w_attn_o,
                 rwkv_shift_mu, rwkv_w0, rwkv_w2, rwkv_a0, rwkv_a2, rwkv_g2, rwkv_k_k, rwkv_k_a,
                 rwkv_r_k, rwkv_lnx_g, rwkv_lnx_b, w_rwkv_o, w_ret_o, w_out,
                 norm2_g, w_ffn_gate, w_ffn_up, w_ffn_down):
    B, T, D = x.shape
    h = _rms(x) * norm1_g
    proj = h @ w_in
    aq, ak, av, rw, rq, rk, rv, rg, gates = _split(proj, IN_SIZES)
    aq = _rms(aq.reshape(B, T, ATTN_Q_HEADS, HEAD_DIM)) * attn_q_norm_g
    ak = _rms(ak.reshape(B, T, ATTN_KV_HEADS, HEAD_DIM)) * attn_k_norm_g
    av = av.reshape(B, T, ATTN_KV_HEADS, HEAD_DIM)
    o_a = sliding_window_attention(aq, ak, av, attn_sinks) @ w_attn_o
    o_b = rwkv7_time_mix(rw, rwkv_shift_mu, rwkv_w0, rwkv_w2, rwkv_a0, rwkv_a2, rwkv_g2,
                         rwkv_k_k, rwkv_k_a, rwkv_r_k, rwkv_lnx_g, rwkv_lnx_b) @ w_rwkv_o
    o_c = retention(rq, rk, rv, rg) @ w_ret_o
    g = jax.nn.sigmoid(gates).reshape(B, T, N_BRANCH, D)
    mixed = g[:, :, 0] * o_a + g[:, :, 1] * o_b + g[:, :, 2] * o_c
    x = x + mixed @ w_out
    h2 = _rms(x) * norm2_g
    x = x + (jax.nn.silu(h2 @ w_ffn_gate) * (h2 @ w_ffn_up)) @ w_ffn_down
    return x

def first_inputs(seed: int = 0) -> dict:
    key = jax.random.key(seed)
    ks = jax.random.split(key, 25)
    L = DEPTH

    def nrm(k, shape, scale):
        return jax.random.normal(k, shape, jnp.float32) * scale

    return {
        'x': nrm(ks[0], (BATCH, SEQ, D_MODEL), 1.0),
        'norm1_g': 1.0 + nrm(ks[1], (L, D_MODEL), 0.02),
        'w_in': nrm(ks[2], (L, D_MODEL, IN_WIDTH), D_MODEL ** -0.5),
        'attn_q_norm_g': 1.0 + nrm(ks[3], (L, HEAD_DIM), 0.02),
        'attn_k_norm_g': 1.0 + nrm(ks[4], (L, HEAD_DIM), 0.02),
        'attn_sinks': nrm(ks[5], (L, ATTN_Q_HEADS), 0.5),
        'w_attn_o': nrm(ks[6], (L, ATTN_WIDTH, D_MODEL), ATTN_WIDTH ** -0.5),
        'rwkv_shift_mu': jax.random.uniform(ks[7], (L, RWKV_COLS), jnp.float32),
        'rwkv_w0': jax.random.uniform(ks[8], (L, RWKV_WIDTH), jnp.float32, minval=-6.0, maxval=1.0),
        'rwkv_w2': nrm(ks[9], (L, DECAY_LORA, RWKV_WIDTH), 0.1 * DECAY_LORA ** -0.5),
        'rwkv_a0': nrm(ks[10], (L, RWKV_WIDTH), 0.1),
        'rwkv_a2': nrm(ks[11], (L, ICLR_LORA, RWKV_WIDTH), ICLR_LORA ** -0.5),
        'rwkv_g2': nrm(ks[12], (L, GATE_LORA, RWKV_WIDTH), GATE_LORA ** -0.5),
        'rwkv_k_k': 0.85 + nrm(ks[13], (L, RWKV_WIDTH), 0.02),
        'rwkv_k_a': 1.0 + nrm(ks[14], (L, RWKV_WIDTH), 0.02),
        'rwkv_r_k': nrm(ks[15], (L, RWKV_HEADS, HEAD_DIM), 0.1),
        'rwkv_lnx_g': 1.0 + nrm(ks[16], (L, RWKV_WIDTH), 0.02),
        'rwkv_lnx_b': nrm(ks[17], (L, RWKV_WIDTH), 0.02),
        'w_rwkv_o': nrm(ks[18], (L, RWKV_WIDTH, D_MODEL), RWKV_WIDTH ** -0.5),
        'w_ret_o': nrm(ks[19], (L, RET_WIDTH, D_MODEL), RET_WIDTH ** -0.5),
        'w_out': nrm(ks[20], (L, D_MODEL, D_MODEL), D_MODEL ** -0.5),
        'norm2_g': 1.0 + nrm(ks[21], (L, D_MODEL), 0.02),
        'w_ffn_gate': nrm(ks[22], (L, D_MODEL, D_FF), D_MODEL ** -0.5),
        'w_ffn_up': nrm(ks[23], (L, D_MODEL, D_FF), D_MODEL ** -0.5),
        'w_ffn_down': nrm(ks[24], (L, D_FF, D_MODEL), D_FF ** -0.5),
    }

def first_block(x, norm1_g, w_in, attn_q_norm_g, attn_k_norm_g, attn_sinks, w_attn_o,
              rwkv_shift_mu, rwkv_w0, rwkv_w2, rwkv_a0, rwkv_a2, rwkv_g2, rwkv_k_k, rwkv_k_a,
              rwkv_r_k, rwkv_lnx_g, rwkv_lnx_b, w_rwkv_o, w_ret_o, w_out,
              norm2_g, w_ffn_gate, w_ffn_up, w_ffn_down):
    for l in range(DEPTH):
        x = hybrid_layer(x, norm1_g[l], w_in[l], attn_q_norm_g[l], attn_k_norm_g[l], attn_sinks[l],
                         w_attn_o[l], rwkv_shift_mu[l], rwkv_w0[l], rwkv_w2[l], rwkv_a0[l], rwkv_a2[l],
                         rwkv_g2[l], rwkv_k_k[l], rwkv_k_a[l], rwkv_r_k[l], rwkv_lnx_g[l], rwkv_lnx_b[l],
                         w_rwkv_o[l], w_ret_o[l], w_out[l], norm2_g[l], w_ffn_gate[l], w_ffn_up[l],
                         w_ffn_down[l])
    return x


DEPTH_2 = 1

MIX_WIDTH = D_MODEL
MLSTM_WIDTH = MIX_WIDTH // 2
MLSTM_HEADS = 4
MLSTM_HEAD_DIM = MLSTM_WIDTH // MLSTM_HEADS
MLSTM_CHUNK = 128
MLSTM_M_INIT = -1e30
HYENA_WIDTH = MIX_WIDTH - MLSTM_WIDTH
HYENA_GROUPS = 4
HYENA_GROUP_DIM = HYENA_WIDTH // HYENA_GROUPS
HYENA_ORDER = 2
HYENA_DIRS = 2
HYENA_BANDS = 16
HYENA_EMB_DIM = 1 + 2 * HYENA_BANDS
HYENA_FILTER_HIDDEN = 64
HYENA_WINDOW_SHIFT = 0.05
HYENA_SLOW_DECAY = -math.log(1e-2) / 1.5
HYENA_FAST_DECAY = -math.log(1e-2) / 0.3
SHORT_CONV = 3
N_GATE_COLS = 4 * MLSTM_HEADS
PROJ_COLS = 4 * MLSTM_WIDTH + N_GATE_COLS + (HYENA_ORDER + 1) * HYENA_WIDTH
N_EXPERTS = 16
EC_CAPACITY_FACTOR = 2
EXPERT_FF = 2 * D_MODEL
RMS_EPS = 1e-6


def rms_norm(x, g):
    xf = x.astype(jnp.float32)
    y = xf * lax.rsqrt(jnp.mean(xf * xf, axis=-1, keepdims=True) + RMS_EPS)
    return (y * g.astype(jnp.float32)).astype(x.dtype)

def centred_short_conv(u, w, b):
    S = u.shape[1]
    r = SHORT_CONV // 2
    up = jnp.pad(u, ((0, 0), (r, r), (0, 0)))
    y = b
    for j in range(SHORT_CONV):
        y = y + up[:, j:j + S] * w[j]
    return y

def mlstm_scan(q, k, v, i_pre, logf):
    B, H, S, Dh = q.shape
    nc = S // MLSTM_CHUNK
    qc = q.reshape(B, H, nc, MLSTM_CHUNK, Dh)
    kc = k.reshape(B, H, nc, MLSTM_CHUNK, Dh)
    vc = v.reshape(B, H, nc, MLSTM_CHUNK, Dh)
    ic = i_pre.reshape(B, H, nc, MLSTM_CHUNK)
    b = jnp.cumsum(logf.reshape(B, H, nc, MLSTM_CHUNK), axis=-1)
    g = b[..., -1]
    w_end = g[..., None] - b + ic
    a = jnp.max(w_end, axis=-1)
    e_end = jnp.exp(w_end - a[..., None])
    c_loc = jnp.einsum('bhcsv,bhcsk->bhcvk', vc * e_end[..., None], kc)
    n_loc = jnp.einsum('bhcs,bhcsk->bhck', e_end, kc)

    def step(carry, inp):
        c_st, n_st, m_st = carry
        g_j, a_j, c_j, n_j = inp
        m_new = jnp.maximum(g_j + m_st, a_j)
        s_prev = jnp.exp(g_j + m_st - m_new)
        s_loc = jnp.exp(a_j - m_new)
        c_new = s_prev[..., None, None] * c_st + s_loc[..., None, None] * c_j
        n_new = s_prev[..., None] * n_st + s_loc[..., None] * n_j
        return (c_new, n_new, m_new), (c_st, n_st, m_st)

    init = (jnp.zeros((B, H, Dh, Dh), q.dtype), jnp.zeros((B, H, Dh), q.dtype),
            jnp.full((B, H), MLSTM_M_INIT, q.dtype))
    xs = tuple(jnp.moveaxis(t, 2, 0) for t in (g, a, c_loc, n_loc))
    _, (c_in, n_in, m_in) = lax.scan(step, init, xs)
    c_in = jnp.moveaxis(c_in, 0, 2)
    n_in = jnp.moveaxis(n_in, 0, 2)
    m_in = jnp.moveaxis(m_in, 0, 2)

    tri = jnp.tril(jnp.ones((MLSTM_CHUNK, MLSTM_CHUNK), dtype=bool))
    log_d = jnp.where(tri, b[..., :, None] - b[..., None, :] + ic[..., None, :], -jnp.inf)
    log_inter = b + m_in[..., None]
    m_t = jnp.maximum(log_inter, jnp.max(log_d, axis=-1))
    d = jnp.exp(log_d - m_t[..., None])
    e_inter = jnp.exp(log_inter - m_t)
    s = jnp.einsum('bhctd,bhcsd->bhcts', qc, kc) * d
    num = (jnp.einsum('bhcts,bhcsd->bhctd', s, vc)
           + e_inter[..., None] * jnp.einsum('bhcvk,bhctk->bhctv', c_in, qc))
    den = jnp.sum(s, axis=-1) + e_inter * jnp.einsum('bhck,bhctk->bhct', n_in, qc)
    nrm = jnp.maximum(jnp.abs(den), jnp.exp(-m_t))
    return (num / nrm[..., None]).reshape(B, H, S, Dh)

def mlstm_mixer(q, k, v, o, gates, conv_w, conv_b, norm_g):
    B, S, _ = q.shape
    H, Dh = MLSTM_HEADS, MLSTM_HEAD_DIM
    qk = jax.nn.silu(centred_short_conv(jnp.concatenate([q, k], axis=-1), conv_w, conv_b))
    q, k = jnp.split(qk, 2, axis=-1)

    def heads(t):
        return t.reshape(B, S, H, Dh).transpose(0, 2, 1, 3).astype(jnp.float32)

    qh, kh, vh = heads(q), heads(k) * (MLSTM_HEAD_DIM ** -0.5), heads(v)
    g4 = gates.reshape(B, S, 4, H).transpose(2, 0, 3, 1).astype(jnp.float32)
    i_f, f_f, i_b, f_b = g4[0], g4[1], g4[2], g4[3]
    h_f = mlstm_scan(qh, kh, vh, i_f, jax.nn.log_sigmoid(f_f))

    def fl(t):
        return jnp.flip(t, axis=2)

    h_b = fl(mlstm_scan(fl(qh), fl(kh), fl(vh), fl(i_b), fl(jax.nn.log_sigmoid(f_b))))
    hsum = (h_f + h_b).transpose(0, 2, 1, 3)
    hn = rms_norm(hsum, norm_g.reshape(H, Dh)).reshape(B, S, MLSTM_WIDTH)
    return (jax.nn.sigmoid(o.astype(jnp.float32)) * hn).astype(o.dtype)

def hyena_filters(L, w1, b1, w2, b2, w3, freq, deltas):
    f32 = jnp.float32
    t = jnp.linspace(0.0, 1.0, L, dtype=f32)[:, None]
    w = 2.0 * math.pi * jnp.arange(L, dtype=f32)[:, None] / L
    bands = jnp.linspace(1e-4, HYENA_BANDS - 1, HYENA_BANDS, dtype=f32)[None, :]
    z = jnp.concatenate([t, jnp.cos(bands * w), -jnp.sin(bands * w)], axis=-1)
    fr = freq.astype(f32)
    hid = jnp.sin(fr * (z @ w1.astype(f32) + b1.astype(f32)))
    hid = jnp.sin(fr * (hid @ w2.astype(f32) + b2.astype(f32)))
    h = hid @ w3.astype(f32)
    window = jnp.exp(-t * jnp.abs(deltas.astype(f32))) + HYENA_WINDOW_SHIFT
    return (h * window).reshape(L, HYENA_ORDER, HYENA_DIRS, HYENA_WIDTH)

def bidir_long_conv(u, h_fwd, h_bwd, bias):
    L, C = h_fwd.shape
    two_sided = jnp.concatenate([(h_fwd[0] + h_bwd[0])[None], h_fwd[1:],
                                 jnp.zeros((1, C), jnp.float32), jnp.flip(h_bwd[1:], axis=0)], axis=0)
    k_f = jnp.fft.rfft(two_sided, n=2 * L, axis=0)
    uf = u.astype(jnp.float32)
    u_f = jnp.fft.rfft(uf, n=2 * L, axis=1)
    y = jnp.fft.irfft(u_f * k_f[None], n=2 * L, axis=1)[:, :L]
    return (y + uf * bias.astype(jnp.float32)).astype(u.dtype)

def hyena_mixer(hx, conv_w, conv_b, filt, bias, norm_g):
    B, S, _ = hx.shape
    u = centred_short_conv(hx, conv_w, conv_b)
    x1, x2, z = jnp.split(u, HYENA_ORDER + 1, axis=-1)
    z = x1 * bidir_long_conv(z, filt[:, 0, 0], filt[:, 0, 1], bias[0])
    z = x2 * bidir_long_conv(z, filt[:, 1, 0], filt[:, 1, 1], bias[1])
    zg = z.reshape(B, S, HYENA_GROUPS, HYENA_GROUP_DIM)
    return rms_norm(zg, norm_g.reshape(HYENA_GROUPS, HYENA_GROUP_DIM)).reshape(B, S, HYENA_WIDTH)

def expert_choice_moe(xn, w_router, w_gate, w_up, w_down):
    B, T, D = xn.shape
    cap = EC_CAPACITY_FACTOR * T // N_EXPERTS
    aff = jax.nn.softmax((xn @ w_router).astype(jnp.float32), axis=-1)
    g, idx = lax.top_k(jnp.swapaxes(aff, 1, 2), cap)
    bidx = jnp.arange(B)[:, None, None]
    xs = xn[bidx, idx]
    hid = jax.nn.silu(jnp.einsum('becd,edf->becf', xs, w_gate)) * jnp.einsum('becd,edf->becf', xs, w_up)
    y = jnp.einsum('becf,efd->becd', hid, w_down) * g[..., None].astype(xn.dtype)
    return jnp.zeros_like(xn).at[bidx, idx].add(y)

def second_inputs(seed: int = 0) -> dict:
    key = jax.random.key(seed)
    ks = jax.random.split(key, 32)
    f32 = jnp.float32
    D, L = D_MODEL, DEPTH_2

    def nrm(k, shape, scale):
        return jax.random.normal(k, shape, f32) * scale

    gate_off = 4 * MLSTM_WIDTH
    H = MLSTM_HEADS
    f_bias = jnp.linspace(3.0, 6.0, H, dtype=f32)
    b_in = nrm(ks[5], (L, PROJ_COLS), 0.02)
    b_in = b_in.at[:, gate_off + H:gate_off + 2 * H].add(f_bias)
    b_in = b_in.at[:, gate_off + 3 * H:gate_off + 4 * H].add(f_bias)
    n_filt = HYENA_ORDER * HYENA_DIRS * HYENA_WIDTH
    base_delta = jnp.tile(jnp.linspace(HYENA_SLOW_DECAY, HYENA_FAST_DECAY, HYENA_WIDTH, dtype=f32),
                          HYENA_ORDER * HYENA_DIRS)
    return {
        'x': nrm(ks[0], (BATCH, SEQ, D), 1.0),
        'c': nrm(ks[1], (BATCH, D), 1.0),
        'w_ada': nrm(ks[2], (L, D, 6 * D), 0.5 * D ** -0.5),
        'b_ada': nrm(ks[3], (L, 6 * D), 0.02),
        'g_mix': 1.0 + nrm(ks[4], (L, D), 0.02),
        'w_in': nrm(ks[6], (L, D, PROJ_COLS), D ** -0.5),
        'b_in': b_in,
        'conv_qk_w': nrm(ks[7], (L, SHORT_CONV, 2 * MLSTM_WIDTH), SHORT_CONV ** -0.5),
        'conv_qk_b': nrm(ks[8], (L, 2 * MLSTM_WIDTH), 0.02),
        'mlstm_norm_g': 1.0 + nrm(ks[9], (L, MLSTM_WIDTH), 0.02),
        'conv_hy_w': nrm(ks[10], (L, SHORT_CONV, (HYENA_ORDER + 1) * HYENA_WIDTH), SHORT_CONV ** -0.5),
        'conv_hy_b': nrm(ks[11], (L, (HYENA_ORDER + 1) * HYENA_WIDTH), 0.02),
        'hy_w1': nrm(ks[12], (L, HYENA_EMB_DIM, HYENA_FILTER_HIDDEN), HYENA_EMB_DIM ** -0.5),
        'hy_b1': nrm(ks[13], (L, HYENA_FILTER_HIDDEN), 0.1),
        'hy_w2': nrm(ks[14], (L, HYENA_FILTER_HIDDEN, HYENA_FILTER_HIDDEN), HYENA_FILTER_HIDDEN ** -0.5),
        'hy_b2': nrm(ks[15], (L, HYENA_FILTER_HIDDEN), 0.1),
        'hy_w3': nrm(ks[16], (L, HYENA_FILTER_HIDDEN, n_filt), 0.1 * HYENA_FILTER_HIDDEN ** -0.5),
        'hy_freq': 1.0 + nrm(ks[17], (L, HYENA_FILTER_HIDDEN), 0.02),
        'hy_deltas': base_delta[None] * (1.0 + nrm(ks[18], (L, n_filt), 0.02)),
        'hy_bias': nrm(ks[19], (L, HYENA_ORDER, HYENA_WIDTH), 0.1),
        'hyena_norm_g': 1.0 + nrm(ks[20], (L, HYENA_WIDTH), 0.02),
        'w_out': nrm(ks[21], (L, MIX_WIDTH, D), MIX_WIDTH ** -0.5),
        'g_ffn': 1.0 + nrm(ks[22], (L, D), 0.02),
        'w_router': nrm(ks[23], (L, D, N_EXPERTS), D ** -0.5),
        'w_gate': nrm(ks[24], (L, N_EXPERTS, D, EXPERT_FF), D ** -0.5),
        'w_up': nrm(ks[25], (L, N_EXPERTS, D, EXPERT_FF), D ** -0.5),
        'w_down': nrm(ks[26], (L, N_EXPERTS, EXPERT_FF, D), EXPERT_FF ** -0.5),
        'g_final': 1.0 + nrm(ks[27], (D,), 0.02),
    }

def second_block(x, c, w_ada, b_ada, g_mix, w_in, b_in, conv_qk_w, conv_qk_b, mlstm_norm_g,
              conv_hy_w, conv_hy_b, hy_w1, hy_b1, hy_w2, hy_b2, hy_w3, hy_freq, hy_deltas, hy_bias,
              hyena_norm_g, w_out, g_ffn, w_router, w_gate, w_up, w_down, g_final):
    W = MLSTM_WIDTH
    split_pts = [W, 2 * W, 3 * W, 4 * W, 4 * W + N_GATE_COLS]
    seq_len = x.shape[1]
    for l in range(DEPTH_2):
        mod = (c @ w_ada[l] + b_ada[l])[:, None, :]
        sh1, sc1, gt1, sh2, sc2, gt2 = jnp.split(mod, 6, axis=-1)
        h = rms_norm(x, g_mix[l]) * (1 + sc1) + sh1
        p = h @ w_in[l] + b_in[l]
        q, k, v, o, gates, hx = jnp.split(p, split_pts, axis=-1)
        y_m = mlstm_mixer(q, k, v, o, gates, conv_qk_w[l], conv_qk_b[l], mlstm_norm_g[l])
        filt = hyena_filters(seq_len, hy_w1[l], hy_b1[l], hy_w2[l], hy_b2[l], hy_w3[l], hy_freq[l], hy_deltas[l])
        y_h = hyena_mixer(hx, conv_hy_w[l], conv_hy_b[l], filt, hy_bias[l], hyena_norm_g[l])
        mixed = jnp.concatenate([y_m, y_h], axis=-1) @ w_out[l]
        x = x + gt1 * mixed
        hf = rms_norm(x, g_ffn[l]) * (1 + sc2) + sh2
        x = x + gt2 * expert_choice_moe(hf, w_router[l], w_gate[l], w_up[l], w_down[l])
    return rms_norm(x, g_final)


def setup_inputs(seed=0):
    out = dict(first_inputs(seed))
    for name, value in second_inputs(seed + 1).items():
        if name != "x":
            out[name + "_2"] = value
    return out


def reference(
    x, norm1_g, w_in, attn_q_norm_g, attn_k_norm_g, attn_sinks, w_attn_o, rwkv_shift_mu,
    rwkv_w0, rwkv_w2, rwkv_a0, rwkv_a2, rwkv_g2, rwkv_k_k, rwkv_k_a, rwkv_r_k, rwkv_lnx_g,
    rwkv_lnx_b, w_rwkv_o, w_ret_o, w_out, norm2_g, w_ffn_gate, w_ffn_up, w_ffn_down, c_2,
    w_ada_2, b_ada_2, g_mix_2, w_in_2, b_in_2, conv_qk_w_2, conv_qk_b_2, mlstm_norm_g_2,
    conv_hy_w_2, conv_hy_b_2, hy_w1_2, hy_b1_2, hy_w2_2, hy_b2_2, hy_w3_2, hy_freq_2,
    hy_deltas_2, hy_bias_2, hyena_norm_g_2, w_out_2, g_ffn_2, w_router_2, w_gate_2, w_up_2,
    w_down_2, g_final_2,
):
    x = first_block(
        x, norm1_g, w_in, attn_q_norm_g, attn_k_norm_g, attn_sinks, w_attn_o, rwkv_shift_mu,
        rwkv_w0, rwkv_w2, rwkv_a0, rwkv_a2, rwkv_g2, rwkv_k_k, rwkv_k_a, rwkv_r_k, rwkv_lnx_g,
        rwkv_lnx_b, w_rwkv_o, w_ret_o, w_out, norm2_g, w_ffn_gate, w_ffn_up, w_ffn_down,
    )
    return second_block(
        x, c_2, w_ada_2, b_ada_2, g_mix_2, w_in_2, b_in_2, conv_qk_w_2, conv_qk_b_2,
        mlstm_norm_g_2, conv_hy_w_2, conv_hy_b_2, hy_w1_2, hy_b1_2, hy_w2_2, hy_b2_2, hy_w3_2,
        hy_freq_2, hy_deltas_2, hy_bias_2, hyena_norm_g_2, w_out_2, g_ffn_2, w_router_2,
        w_gate_2, w_up_2, w_down_2, g_final_2,
    )


_drawn_inputs = setup_inputs


def setup_inputs(seed=0):
    import zlib

    import numpy as np

    out = dict(_drawn_inputs(seed))
    spreads = {}
    factors = {'attn_q_norm_g': 8.0,
     'attn_k_norm_g': 8.0,
     'attn_sinks': 29.424,
     'rwkv_w2': 8.0,
     'rwkv_k_k': 7.343,
     'rwkv_k_a': 4.51,
     'rwkv_lnx_g': 4.644,
     'rwkv_lnx_b': 4.991,
     'b_ada_2': 2.696,
     'g_mix_2': 5.49,
     'conv_qk_b_2': 34.292,
     'mlstm_norm_g_2': 8.0,
     'conv_hy_b_2': 3.012,
     'hy_freq_2': 5.851,
     'hyena_norm_g_2': 8.0,
     'g_ffn_2': 5.645,
     'g_final_2': 8.007}
    for name, (base, spread) in spreads.items():
        noise = np.random.default_rng([zlib.crc32(name.encode()), seed]).standard_normal(out[name].shape)
        drawn = base * np.exp(spread * noise) if base else spread * noise
        out[name] = jnp.asarray(drawn.astype(out[name].dtype))
    for name, factor in factors.items():
        out[name] = (out[name] * factor).astype(out[name].dtype)
    return out
```

```python
import math
from contextlib import ExitStack

import numpy as np

import concourse.bass as bass
import concourse.mybir as mybir
from concourse.alu_op_type import AluOpType as ALU

F32 = mybir.dt.float32
U32 = mybir.dt.uint32
ACT = mybir.ActivationFunctionType
AX = mybir.AxisListType.X

P = 128
T = 256
TT = T // P
D = 1024
KD = D // P
LAYERS = 2
HD = 64
HEADS = 8
HB = HEADS * HD // P
F_FF = 2816
FB = F_FF // P
W_IN = 7680
EPS = 1e-6
LNX_EPS = 64e-5
KAPPA = math.exp(-0.5)
NEG = -1e30

QKV, RW, RET0, GATE0 = 0, 768, 2560, 4608
IN_ORDER = [512, 1024, 1536, 2048, 0] + list(range(2560, W_IN, 512))
B_AK, B_AV, B_R, B_K, B_V, B_LORA, B_GD, B_AQ, B_RQ, B_RK, B_RV, B_RG, B_GATE = (
    0, 1, 2, 6, 10, 14, 15, 16, 20, 24, 28, 32, 36)
RW_BLOCKS = 14

H2, DH2 = 4, 128
EXPERTS, CAP, F_E = 16, 32, 2048
IN2 = 3600

RING, SLOT = 3, 4096
ADA_SLOTS, LAYER_SLOTS, TWO_SLOTS, EXPERT_SLOTS = 12, 39, 12, 12
ADA_BLOCKS, TWO_BLOCKS = 12, 20
N_PROJ, N_MIX, N_OUT, N_FFN, N_DOWN = 30, 12, 4, 22, 8
Q_MIX = N_PROJ
Q_OUT = Q_MIX + N_MIX
Q_FFN = Q_OUT + N_OUT
Q_DOWN = Q_FFN + N_FFN
LAYER_BLOCKS = Q_DOWN + N_DOWN
S_MIX, S_OUT, S_FFN, S_DOWN = 15, 18, 20, 31
SLOT_BLOCKS = [2] * 15 + [4] * 3 + [2] * 2 + [2] * 11 + [1] * 8

C_ID, C_ONES, C_BD, C_PERM, C_DUP, C_COS, C_SIN = 0, 128, 256, 384, 512, 768, 1024
C_LVL = 1280
LEVELS = 7
C_GRAM = C_LVL + LEVELS * P
C_CAUSAL = C_GRAM + 512
C_BAND = C_CAUSAL + P
C_N = C_BAND + 2 * P
PL_G1, PL_G2, PL_QN, PL_KN, PL_MU, PL_W0, PL_A0, PL_KK, PL_KA, PL_RK, PL_LG, PL_LB, PL_SINK = (
    0, 8, 16, 17, 18, 32, 36, 40, 44, 48, 52, 56, 60)
PL_N = PL_SINK + 16
D_CS, D_CI, D_MASK, D_IOTA, D_Z, D_SEL, D_TOK, D_NT = 0, 1024, 2048, 3072, 3328, 3584, 4096, 4098
D_N = 4100
P2_GMIX, P2_GFFN, P2_GFIN, P2_BIN, P2_BG, P2_CQW, P2_CQB, P2_CHW, P2_CHB, P2_MN, P2_HBIAS, P2_HN, P2_HY = (
    0, 8, 16, 24, 52, 56, 80, 88, 124, 136, 140, 148, 152)
P2_N = 155

ROUNDS = [(0, [0, 2, 4, 6, 1, 3, 5, 7]), (1, [0, 2, 1, 3]), (1, [4, 6, 5, 7])]


def layer_constants():
    c = np.zeros((P, C_N), np.float32)
    p, f = np.arange(P)[:, None], np.arange(P)[None, :]
    c[:, C_ID:C_ID + P] = p == f
    c[:, C_ONES:C_ONES + P] = 1
    c[:, C_BD:C_BD + P] = p // HD == f // HD
    half = HD // 2
    same = p // HD == f // HD
    c[:, C_PERM:C_PERM + P] = np.where(same & (p == f + half), -1.0, 0) + np.where(same & (p == f - half), 1.0, 0)
    for kv in range(2):
        c[:, C_DUP + kv * P:C_DUP + (kv + 1) * P] = p == kv * HD + f % HD
    inv = (1.0 / (np.float32(10000.0) ** (np.arange(half, dtype=np.float32) * np.float32(2.0) / HD))).astype(np.float32)
    ang = np.arange(T, dtype=np.float32)[None, :] * inv[:, None]
    c[:, C_COS:C_COS + T] = np.tile(np.cos(ang), (P // half, 1))
    c[:, C_SIN:C_SIN + T] = np.tile(np.sin(ang), (P // half, 1))
    for n in range(LEVELS):
        m = 1 << n
        c[:, C_LVL + n * P:C_LVL + (n + 1) * P] = (p // (2 * m) == f // (2 * m)) & (p // m % 2 == 0) & (f // m % 2 == 1)
    for n, keep in enumerate([p > f, p <= f, p < f, p <= f]):
        c[:, C_GRAM + n * P:C_GRAM + (n + 1) * P] = keep
    c[:, C_CAUSAL:C_CAUSAL + P] = np.where(f <= p, 0, NEG)
    c[:, C_BAND:C_BAND + P] = np.where(f > p, 0, NEG)
    c[:, C_BAND + P:C_BAND + 2 * P] = np.where(f <= p, 0, NEG)
    gamma = np.log1p(-np.power(2.0, -5.0 - np.arange(HEADS, dtype=np.float64)))[None, :, None]
    diff = np.arange(T)[None, None, :] - np.arange(P)[:, None, None]
    dec = np.where(diff >= 0, np.exp(gamma * np.maximum(diff, 0)), 0) * HD ** -0.5
    decay = np.concatenate([dec, dec[:, :, :P]], axis=2).astype(np.float32)
    return c, decay.reshape(P, HEADS * 3 * P)


def second_constants():
    c = np.zeros((P, D_N), np.float32)
    t, k = np.arange(T, dtype=np.float64), np.arange(T, dtype=np.float64) + 0.5
    ang = 2 * np.pi * t[:, None] * k[None, :] / (2 * T)
    fwd = np.stack([np.cos(ang), np.sin(ang)], axis=1)
    c[:, D_CS:D_CS + 1024] = fwd.reshape(TT, P, 512).transpose(1, 0, 2).reshape(P, 1024)
    inv = np.stack([np.cos(ang.T), np.sin(ang.T)], axis=1) / T
    c[:, D_CI:D_CI + 1024] = inv.reshape(TT, P, 512).transpose(1, 0, 2).reshape(P, 1024)
    s, q = np.arange(T)[:, None], np.arange(T)[None, :]
    masks = np.stack([s <= q, s >= q], axis=1).astype(np.float32)
    c[:, D_MASK:D_MASK + 1024] = masks.reshape(TT, P, 2, T).transpose(1, 2, 0, 3).reshape(P, 1024)
    c[:, D_IOTA:D_IOTA + T] = np.arange(T)
    f32 = np.float32
    tl = np.linspace(0.0, 1.0, T, dtype=f32)[:, None]
    w = (f32(2.0 * math.pi) * np.arange(T, dtype=f32)[:, None] / f32(T)).astype(f32)
    bands = np.linspace(1e-4, 15, 16, dtype=f32)[None, :]
    z = np.concatenate([tl, np.cos(bands * w), -np.sin(bands * w)], axis=-1)
    c[:33, D_Z:D_Z + T] = z.T
    for h in range(H2):
        c[h, D_SEL + h * P:D_SEL + (h + 1) * P] = 1
    c[:, D_TOK:D_TOK + TT] = np.arange(T).reshape(TT, P).T
    c[:, D_NT:D_NT + TT] = -tl[:, 0].reshape(TT, P).T
    return c


def columns(v):
    return np.ascontiguousarray(v).reshape(-1, P).T


def pack_layer(a, l):
    dup = lambda g: np.concatenate([g, g])[:, None]
    order = [h for _, heads in ROUNDS for h in heads]
    parts = [columns(a["norm1_g"][l]), columns(a["norm2_g"][l]), dup(a["attn_q_norm_g"][l]), dup(a["attn_k_norm_g"][l]),
             columns(a["rwkv_shift_mu"][l]), columns(a["rwkv_w0"][l]), columns(a["rwkv_a0"][l]), columns(a["rwkv_k_k"][l]),
             columns(a["rwkv_k_a"][l]), columns(a["rwkv_r_k"][l]), columns(a["rwkv_lnx_g"][l]), columns(a["rwkv_lnx_b"][l]),
             np.broadcast_to(a["attn_sinks"][l][order][None, :], (P, 16))]
    return np.concatenate(parts, axis=1)


def pack_lora(a, l):
    return np.concatenate([np.concatenate([a["rwkv_w2"][l], a["rwkv_a2"][l]], axis=0), a["rwkv_g2"][l]], axis=1)


def pack_second(a):
    rows = lambda v: np.concatenate([v, np.zeros((P - v.shape[0],) + v.shape[1:], v.dtype)], axis=0)
    b = a["b_in_2"][0]
    bias = np.concatenate([b[:2048], b[2064:]])
    parts = [columns(a["g_mix_2"][0]), columns(a["g_ffn_2"][0]), columns(a["g_final_2"]), columns(bias),
             rows(b[2048:2064].reshape(4, H2).T),
             columns(a["conv_qk_w_2"][0]), columns(a["conv_qk_b_2"][0]), columns(a["conv_hy_w_2"][0]), columns(a["conv_hy_b_2"][0]),
             columns(a["mlstm_norm_g_2"][0]), columns(a["hy_bias_2"][0]), columns(a["hyena_norm_g_2"][0]),
             rows(a["hy_b1_2"][0][:, None]), rows(a["hy_b2_2"][0][:, None]), rows(a["hy_freq_2"][0][:, None])]
    return np.concatenate(parts, axis=1)


def build(nc, io):
    ctx = ExitStack()
    with ctx:
        def sb(name, shape):
            return ctx.enter_context(nc.sbuf_tensor(name, shape, F32))

        def sem(name):
            return ctx.enter_context(nc.semaphore(name))

        ring = sb("ring", [P, RING, SLOT])
        xT = sb("xT", [P, KD, T])
        hT = sb("hT", [P, KD, T])
        con = sb("con", [P, C_N])
        par = sb("par", [P, PL_N])
        lora = sb("lora", [P, 1024])
        proj = sb("proj", [P, 60, T])
        work = sb("work", [P, 16640])
        small = sb("small", [P, 64])
        mod = sb("mod", [P, 48])
        bias = sb("bias", [P, 4])
        PS = ctx.enter_context(nc.psum_tensor("PS", [P, 8, 512], F32))

        def w_(at, *dims):
            n = 1
            for d in dims:
                n *= d
            v = work[:, at:at + n]
            if len(dims) == 2:
                v = v.rearrange("p (a b) -> p a b", b=dims[1])
            if len(dims) == 3:
                v = v.rearrange("p (a b c) -> p a b c", b=dims[1], c=dims[2])
            if len(dims) == 4:
                v = v.rearrange("p (a b c d) -> p a b c d", b=dims[1], c=dims[2], d=dims[3])
            return v

        def banks(at, n, *dims):
            v = PS[:, at:at + n, :].rearrange("p a b -> p (a b)")
            if dims:
                m = 1
                for d in dims:
                    m *= d
                v = v[:, 0:m]
            if len(dims) == 2:
                v = v.rearrange("p (a b) -> p a b", b=dims[1])
            if len(dims) == 3:
                v = v.rearrange("p (a b c) -> p a b c", b=dims[1], c=dims[2])
            return v

        ident, ones, bd = con[:, C_ID:C_ID + P], con[:, C_ONES:C_ONES + P], con[:, C_BD:C_BD + P]
        perm = con[:, C_PERM:C_PERM + P]
        epsc, lnxc, onec = bias[:, 0:1], bias[:, 1:2], bias[:, 2:3]

        X1, X2, X3 = (w_(n * 1024, HB, T) for n in range(3))
        QT, W1S = w_(0, HEADS, 2, P), w_(2048, HEADS, P)
        KK, AT = w_(3072, HB, T), w_(4096, HB, T)
        AR = w_(5120, HB, TT, 2, P)
        GT, Y = w_(7168, HB, T), w_(8192, HB, T)
        GM = w_(9216, HEADS, 4 * P)
        SHIFT = w_(9216, RW_BLOCKS, T)
        VTOK, BKT = w_(13312, TT, 512), w_(14336, 2, 512)
        RHS, U, ST = w_(15360, HEADS, HD), w_(15872, HEADS, HD), w_(16384, HB, HD)
        MID, SC, MIDE = small[:, 0:8].rearrange("p (a b) -> p a b", b=TT), small[:, 8:12], small[:, 12:16]
        MX, MM, SK, SUM = small[:, 16:24], small[:, 24:32], small[:, 32:40], small[:, 40:48]
        ATS, SCO, PT = w_(9216, 5, T), w_(9216 + 1280, 1024), w_(9216 + 2304, HEADS, P)
        KDUP, VATT = w_(9216 + 3328, 2, T), w_(9216 + 3840, TT, P)
        DEC, SM = w_(0, HEADS, 3 * P), w_(3072, HEADS, 3 * P)
        VRET, XR = w_(13312, TT, 512), w_(14336, HB, T)
        SQ, STD, RSTD = w_(5120, KD, T), w_(0, T), w_(256, T)
        HID = proj[:, 0:FB, :]
        SILU = proj[:, 24:28, :].rearrange("p a b -> p (a b)").rearrange("p (a b) -> p a b", b=512)
        CT, MROW, BROW = w_(0, KD), w_(512, 3, 512), w_(2560, 3, 512)

        ring_full = [sem(f"ring_full{n}") for n in range(RING)]
        block_done = sem("block_done")
        const_loaded, cond_loaded = sem("const_loaded"), sem("cond_loaded")
        bias_set, slot_freed = sem("bias_set"), sem("slot_freed")
        mod_rows, mod_cols, mod_ready = sem("mod_rows"), sem("mod_cols"), sem("mod_ready")
        layer_go, layer_joined = sem("layer_go"), sem("layer_joined")

        names = """par_loaded sq_ready ss_ready std_ready h_ready act_taken dve_taken
            z_ready lora_in lora_done lora_out kk_sq kk_ss kk_std cum_ready exps_ready gram_in bonus_in bonus_ss
            bonus_out tok_ready tok_out gm_zero gram_ready gram_taken qt_ready w1_ready w1_masked dq_ready
            rhs_ready rhs_out u_ready u_out y_ready y_out s_ready st_ready ln_in ln_ss ln_std ob_ready
            att_sq att_ss att_std att_qk att_tr att_kv sc_ready sc_max sc_exp p_ready pt_ready pt_out oa_ready oa_out
            rot_ready rot_out vr_ready vr_out dec_loaded rs_ready rs_out oc_psum oc_out oc_sq oc_ss oc_std oc_ready
            vec_order layer_fin""".split()
        L = {n: sem(n) for n in names}
        (par_loaded, sq_ready, ss_ready, std_ready, h_ready, act_taken, dve_taken,
         z_ready, lora_in, lora_done, lora_out, kk_sq, kk_ss, kk_std, cum_ready, exps_ready, gram_in, bonus_in, bonus_ss,
         bonus_out, tok_ready, tok_out, gm_zero, gram_ready, gram_taken, qt_ready, w1_ready, w1_masked, dq_ready,
         rhs_ready, rhs_out, u_ready, u_out, y_ready, y_out, s_ready, st_ready, ln_in, ln_ss, ln_std, ob_ready,
         att_sq, att_ss, att_std, att_qk, att_tr, att_kv, sc_ready, sc_max, sc_exp, p_ready, pt_ready, pt_out, oa_ready, oa_out,
         rot_ready, rot_out, vr_ready, vr_out, dec_loaded, rs_ready, rs_out, oc_psum, oc_out, oc_sq, oc_ss, oc_std, oc_ready,
         vec_order, layer_fin) = (L[n] for n in names)
        layer_sems = range(par_loaded.num, layer_fin.num + 1)
        assert sorted(s.num for s in L.values()) == list(layer_sems)

        def done(l, q):
            return ADA_BLOCKS + LAYER_BLOCKS * l + q + 1

        def full(l, n):
            return 32 * (ADA_SLOTS // RING + LAYER_SLOTS // RING * l + n // RING + 1)

        def hrow(h):
            return slice(HD * (h % 2), HD * (h % 2) + HD)

        c2 = w_(12288, D_N)
        p2 = lora[:, 0:P2_N]
        wrt = lora[:, 256:384].rearrange("p (k e) -> p k e", e=EXPERTS)
        hyw1, hyw2 = lora[0:33, 384:448], lora[0:64, 448:512]
        ARG, TRN = lora[0:64, 512:768], lora[0:64, 768:1024]
        CS, CI = (c2[:, c:c + 1024].rearrange("p (a s n) -> p a s n", s=2, n=T) for c in (D_CS, D_CI))
        MASK2 = c2[:, D_MASK:D_MASK + 1024]
        FILT, KF = w_(0, TT, 4, 512), w_(4096, TT, 2, 2, 512)
        HYW3, DELTA = w_(8192, 2048), w_(10240, 2048)
        YF = w_(10240, TT, 2, 512)
        TMP1, TMP2 = w_(8192, 512), w_(8704, 512)
        WIN = proj[:, 56:60, :].rearrange("p a b -> p (a b)").rearrange("p (a b) -> p a b", b=512)
        ZTOK = WIN
        E2, EMS, NUM = w_(0, 2, TT, T), w_(1024, 2, T), w_(1536, 2, T)
        HS2, LF, BB = w_(2048, H2, T), w_(3072, 2, T), w_(3584, 2, T)
        VT2 = proj[:, 48:52, :].rearrange("p a b -> p (a b)").rearrange("p (a b) -> p a b", b=512)
        G4 = proj[:, 52:56, :]
        AA, NM, EMR, ZER = (proj[:, b:b + 2, :] for b in (16, 18, 20, 22))
        ACOL = small[:, 0:16].rearrange("p (d t h) -> p d t h", t=TT, h=H2)
        gs1, gs2 = small[:, 16:24], small[:, 24:32]
        QK2, HX2 = proj[:, 28:36, :], proj[:, 36:48, :]
        HTOK = proj[:, 0:8, :].rearrange("p a b -> p (a b)").rearrange("p (a b) -> p a b", b=D)
        XS = proj[:, 8:24, :].rearrange("p e (k s) -> p e k s", s=CAP)
        XSE = proj[:, 24, :].rearrange("p (k s) -> p k s", s=CAP)
        PICK = proj[:, 25:29, :].rearrange("p a b -> p (a b)").rearrange("p (a b) -> p a b", b=512)
        GE = proj[:, 29, :]
        flat = lambda a: proj[:, a:a + 2, :].rearrange("p a b -> p (a b)")
        HSE, HE, HTE, YE = flat(32), flat(34), flat(36), flat(38)
        AFF = proj[0:EXPERTS, 40, :]
        DIAG = flat(42)
        LOG = proj[:, 44, 0:32].rearrange("p (t e) -> p t e", e=EXPERTS)
        VAL, IDXU, IDXF = proj[0:EXPERTS, 45, 0:32], proj[0:EXPERTS, 45, 32:64], proj[0:EXPERTS, 45, 64:96]
        REP = proj[0:EXPERTS, 46, :].rearrange("p (a r s) -> p a r s", r=4, s=CAP)
        IG = proj[:, 47, 0:32].rearrange("p (a e) -> p a e", e=EXPERTS)
        ST4 = proj[:, 47, 32:64]
        ZERO = proj[:, 48, 0:P]

        SQ2, STD2, RSTD2 = w_(8192, KD, T), w_(10240, T), w_(10496, T)
        E2F = w_(0, 4, T)

        names2 = """two_loaded f_hid f_arg f_sin f_abs f_win f_h f_filt f_sum kf_ready kf_out
            sq2 ss2 std2 h2_ready act2 dve2 conv_ready conv_act gate_rows abs_rows ln_rows rows_ready em_rows zero_set
            m_tr m_out m_s m_em m_emo m_arg m_exp m_w m_num m_h
            z_tr z_out u2_ready yf_ready yt_ready z_ready2 r_sq r_ss r_std cat_ready
            tok2 tok2_out rt_logit rt_max rt_exp rt_prob rt_tr topk_done ix_ready ix_out diag_ready row_ready pick_ready xs_psum xs_out
            expert_slots xs_staged ge_ready hs_ready he_ready ht_ready ht_out ye_ready scattered
            moe_sum zero_e vec2 out_done""".split()
        S = {n: sem(n) for n in names2}
        (two_loaded, f_hid, f_arg, f_sin, f_abs, f_win, f_h, f_filt, f_sum, kf_ready, kf_out,
         sq2, ss2, std2, h2_ready, act2, dve2, conv_ready, conv_act, gate_rows, abs_rows, ln_rows, rows_ready, em_rows, zero_set,
         m_tr, m_out, m_s, m_em, m_emo, m_arg, m_exp, m_w, m_num, m_h,
         z_tr, z_out, u2_ready, yf_ready, yt_ready, z_ready2, r_sq, r_ss, r_std, cat_ready,
         tok2, tok2_out, rt_logit, rt_max, rt_exp, rt_prob, rt_tr, topk_done, ix_ready, ix_out, diag_ready, row_ready, pick_ready, xs_psum, xs_out,
         expert_slots, xs_staged, ge_ready, hs_ready, he_ready, ht_ready, ht_out, ye_ready, scattered,
         moe_sum, zero_e, vec2, out_done) = (S[n] for n in names2)
        BASE2 = ADA_BLOCKS + LAYERS * LAYER_BLOCKS
        FULL2 = 32 * (ADA_SLOTS + LAYERS * LAYER_SLOTS) // RING
        FULLE = FULL2 + 32 * TWO_SLOTS // RING
        IN2_ORDER = [0, 512, 1024, 1536, 2064, 2576, 3088]

        def second_sync(sp, load, by_rows):
            for n in range(TWO_SLOTS):
                if n < RING:
                    sp.wait_ge(block_done, BASE2 - (RING - 1 - n))
                else:
                    m = n - RING + 1
                    sp.wait_ge(block_done, BASE2 + (2 * m if m <= 8 else 16 + m - 8))
                s = n % RING
                if n < 7:
                    by_rows(io["w_in_2"][0][:, IN2_ORDER[n]:IN2_ORDER[n] + 512], s, 512)
                elif n == 7:
                    by_rows(io["w_in_2"][0][:, 2048:2064], s, 16)
                else:
                    by_rows(io["w_out_2"][0][:, 256 * (n - 8):256 * (n - 7)], s, 256)
            sp.wait_ge(block_done, BASE2 + TWO_BLOCKS)
            with sp.Fori(0, EXPERTS) as e:
                for n in range(EXPERT_SLOTS):
                    s = n % RING
                    sp.wait_ge(expert_slots, EXPERT_SLOTS * e + EXPERT_SLOTS + n - RING + 1)
                    sp.sem_inc(slot_freed, 1)
                    if n < 8:
                        w = io[("w_gate_2", "w_up_2")[n // 4]][0][e]
                        rows, cols = 2 * P, F_E
                        w = w[rows * (n % 4):rows * (n % 4 + 1), :]
                    else:
                        cols = D
                        w = io["w_down_2"][0][e][4 * P * (n - 8):4 * P * (n - 7), :]
                    by_rows(w, s, cols)
            sp.wait_ge(h2_ready, 3)
            sp.dma_start(io["yT"].rearrange("(k p) t -> p k t", p=P), hT[:, :, :]).then_inc(out_done, 16)
            sp.wait_ge(out_done, 16)

        def second_pool(pool):
            pool.wait_ge(layer_go, LAYERS)

        def second_tensor(pe):
            nt = nc.tensor

            def norm_sums(n):
                pe.wait_ge(sq2, n)
                for k in range(KD):
                    mm = nt.matmul(PS[:, 2, 0:T], ones, SQ2[:, k, :], start=(k == 0), stop=(k == KD - 1))
                mm.then_inc(ss2, 1)

            def four_sums(bank, src, signal):
                for n in range(2):
                    mm = nt.matmul(PS[:, bank + n, :], ones, src[:, 2 * n:2 * n + 2, :].rearrange("p a b -> p (a b)"), start=True, stop=True)
                mm.then_inc(signal, 1)

            def product(q, weight, moving, kn, n_blocks=2, m=P):
                if q >= 2:
                    if q - 2 < 16:
                        pe.wait_ge(act2, q - 1)
                    else:
                        pe.wait_ge(dve2, q - 17)
                for b in range(n_blocks):
                    for k in range(kn):
                        mm = nt.matmul(PS[0:m, q % 2, T * b:T * (b + 1)], weight(b, k), moving(k), start=(k == 0), stop=(k == kn - 1))
                mm.then_inc(block_done, 1)

            def filters():
                pe.wait_ge(two_loaded, 7 * 16)
                nt.matmul(PS[0:64, 2, 0:T], hyw1, c2[0:33, D_Z:D_Z + T], start=True, stop=True).then_inc(f_hid, 1)
                pe.wait_ge(f_sin, 1)
                nt.matmul(PS[0:64, 3, 0:T], hyw2, ARG, start=True, stop=True).then_inc(f_hid, 1)
                pe.wait_ge(f_sin, 2)
                for i in range(8):
                    c, t = i // 2, i % 2
                    if i >= 2:
                        pe.wait_ge(f_filt, i - 1)
                    nt.matmul(PS[:, 4 + i % 2, :], ARG[:, P * t:P * (t + 1)], HYW3[0:64, 512 * c:512 * (c + 1)], start=True, stop=True)\
                        .then_inc(f_h, 1)
                pe.wait_ge(f_sum, 2)
                for i in range(8):
                    o, s, kt = i // 4, i // 2 % 2, i % 2
                    if i >= 4:
                        pe.wait_ge(kf_out, i - 3)
                    for t in range(TT):
                        mm = nt.matmul(PS[:, 4 + i % 4, :], CS[:, t, s, P * kt:P * (kt + 1)], FILT[:, t, 2 * o + s, :], start=(t == 0), stop=(t == 1))
                    mm.then_inc(kf_ready, 1)

            def project():
                for n in range(7):
                    s = n % RING
                    pe.wait_ge(ring_full[s], FULL2 + 32 * (n // RING + 1))
                    for half in range(2):
                        product(2 * n + half, lambda b, k: ring[:, s, 512 * k + P * (2 * half + b):512 * k + P * (2 * half + b + 1)],
                                lambda k: hT[:, k, :], KD)
                s = 7 % RING
                pe.wait_ge(ring_full[s], FULL2 + 32 * (7 // RING + 1))
                for half in range(2):
                    product(14 + half, lambda b, k: ring[:, s, 16 * k + 4 * (2 * half + b):16 * k + 4 * (2 * half + b + 1)],
                            lambda k: hT[:, k, :], KD, 2, H2)

            def mlstm():
                pe.wait_ge(act2, 16)
                pe.wait_ge(kf_out, 8)
                for t in range(TT):
                    for b in range(H2):
                        mm = nt.transpose(PS[:, 6 + t, P * b:P * (b + 1)], proj[:, 8 + b, P * t:P * (t + 1)], ident)
                mm.then_inc(m_tr, 1)
                pe.wait_ge(rows_ready, 2)
                for d in range(2):
                    for t in range(TT):
                        at = 4 * (2 * d + t)
                        mm = nt.transpose(PS[:, 5, at:at + 4], AA[0:H2, d, P * t:P * (t + 1)], ident[0:H2, 0:H2])
                mm.then_inc(m_tr, 1)
                pe.wait_ge(em_rows, 1)
                pe.wait_ge(conv_act, 1)
                pe.wait_ge(m_out, 3)
                for h in range(H2):
                    if h:
                        pe.wait_ge(m_h, h)
                    sel = c2[0:H2, D_SEL + P * h:D_SEL + P * (h + 1)]
                    nt.matmul(PS[:, 3, :], sel, NM[0:H2, :, :].rearrange("p a b -> p (a b)"), start=True, stop=True)
                    nt.matmul(PS[:, 4, :], sel, EMR[0:H2, :, :].rearrange("p a b -> p (a b)"), start=True, stop=True).then_inc(m_em, 1)
                    for j in range(TT):
                        mm = nt.matmul(PS[:, 2, T * j:T * (j + 1)], QK2[:, 4 + h, P * j:P * (j + 1)], QK2[:, h, :], start=True, stop=True)
                    mm.then_inc(m_s, 1)
                    pe.wait_ge(m_w, h + 1)
                    for d in range(2):
                        for j in range(TT):
                            nt.matmul(PS[:, 5, T * d:T * (d + 1)], VT2[:, j, P * h:P * (h + 1)], E2[:, d, j, :], start=(j == 0), stop=(j == 1))
                    for d in range(2):
                        for j in range(TT):
                            mm = nt.matmul(PS[:, 6, T * d:T * (d + 1)], ones, E2[:, d, j, :], start=(j == 0), stop=(j == 1))
                    mm.then_inc(m_num, 1)
                pe.wait_ge(r_sq, 1)
                four_sums(2, E2F, r_ss)

            def hyena():
                pe.wait_ge(r_std, 1)
                for o in range(2):
                    if o:
                        pe.wait_ge(z_ready2, 1)
                    for t in range(TT):
                        for b in range(4):
                            mm = nt.transpose(PS[:, 6 + t, P * b:P * (b + 1)], HX2[:, 8 + b, P * t:P * (t + 1)], ident)
                    mm.then_inc(z_tr, 1)
                    pe.wait_ge(z_out, 2 * (o + 1))
                    for kt in range(TT):
                        for s in range(2):
                            for t in range(TT):
                                mm = nt.matmul(PS[:, 2 + 2 * kt + s, :], CS[:, t, s, P * kt:P * (kt + 1)], ZTOK[:, t, :], start=(t == 0), stop=(t == 1))
                    mm.then_inc(u2_ready, 1)
                    pe.wait_ge(yf_ready, o + 1)
                    for b in range(4):
                        for n in range(4):
                            mm = nt.matmul(PS[:, 6 + b // 2, T * (b % 2):T * (b % 2 + 1)], YF[:, n // 2, n % 2, P * b:P * (b + 1)],
                                           CI[:, n // 2, n % 2, :], start=(n == 0), stop=(n == 3))
                    mm.then_inc(yt_ready, 1)
                pe.wait_ge(r_sq, 2)
                four_sums(2, E2F, r_ss)

            def out():
                pe.wait_ge(cat_ready, 2)
                for n in range(4):
                    s = (8 + n) % RING
                    pe.wait_ge(ring_full[s], FULL2 + 32 * ((8 + n) // RING + 1))
                    product(16 + n, lambda b, k: ring[:, s, 256 * k + P * b:256 * k + P * (b + 1)], lambda k: hT[:, k, :], KD)

            def route():
                pe.wait_ge(h2_ready, 2)
                for t in range(TT):
                    for k in range(KD):
                        mm = nt.matmul(PS[:, 2, EXPERTS * t:EXPERTS * (t + 1)], hT[:, k, P * t:P * (t + 1)], wrt[:, k, :],
                                       start=(k == 0), stop=(k == KD - 1))
                mm.then_inc(rt_logit, 1)
                for i in range(4):
                    t, g = i // 2, i % 2
                    for b in range(4):
                        mm = nt.transpose(PS[:, 4 + i, P * b:P * (b + 1)], hT[:, 4 * g + b, P * t:P * (t + 1)], ident)
                    mm.then_inc(tok2, 1)
                pe.wait_ge(rt_prob, 1)
                for t in range(TT):
                    mm = nt.transpose(PS[0:EXPERTS, 3, P * t:P * (t + 1)], LOG[:, t, :], ident)
                mm.then_inc(rt_tr, 1)
                pe.wait_ge(topk_done, 1)
                for a in range(2):
                    mm = nt.matmul(PS[:, 2, EXPERTS * a:EXPERTS * (a + 1)], REP[:, a, :, :].rearrange("p a b -> p (a b)"),
                                   ident[0:EXPERTS, 0:EXPERTS], start=True, stop=True)
                mm.then_inc(ix_ready, 1)
                pe.wait_ge(diag_ready, 1)
                nt.matmul(PS[:, 3, :], ones[0:EXPERTS, :], DIAG[0:EXPERTS, :], start=True, stop=True).then_inc(row_ready, 1)
                pe.wait_ge(pick_ready, 1)
                pe.wait_ge(tok2_out, 4)
                for k in range(KD):
                    if k >= 4:
                        pe.wait_ge(xs_out, k - 3)
                    for t in range(TT):
                        mm = nt.matmul(PS[:, 4 + k % 4, :], HTOK[:, t, P * k:P * (k + 1)], PICK[:, t, :], start=(t == 0), stop=(t == 1))
                    mm.then_inc(xs_psum, 1)

            def experts():
                pe.wait_ge(xs_out, KD)
                pe.wait_ge(zero_e, 1)
                pe.wait_ge(dve2, 4)
                YB = [6, 7, 0, 1]
                for b in YB:
                    nt.matmul(PS[:, b, :], ZERO, con[:, 0:512], start=True, stop=False, skip_group_check=True)
                pe.sem_inc(expert_slots, EXPERT_SLOTS)
                pe.sem_inc(scattered, 1)
                with pe.Fori(0, EXPERTS) as e:
                    pe.wait_ge(xs_staged, e + 1)
                    for n in range(8):
                        s = n % RING
                        pe.wait_ge(ring_full[s], FULLE + 32 * (EXPERT_SLOTS // RING) * e + 32 * (n // RING + 1))
                        for kk in range(2):
                            k = 2 * (n % 4) + kk
                            for j in range(4):
                                mm = nt.matmul(PS[32 * j:32 * j + 32, 2 + n // 4, :], XSE[:, k, :],
                                               ring[:, s, F_E * kk + 512 * j:F_E * kk + 512 * (j + 1)], start=(k == 0), stop=(k == KD - 1))
                        mm.then_inc(expert_slots, 1)
                    pe.wait_ge(he_ready, e + 1)
                    for c in range(4):
                        mm = nt.transpose(PS[:, 4, P * c:P * (c + 1)], HE[:, P * c:P * (c + 1)], ident)
                    mm.then_inc(ht_ready, 1)
                    pe.wait_ge(ht_out, e + 1)
                    for n in range(8, 12):
                        s, d = n % RING, n - 8
                        pe.wait_ge(ring_full[s], FULLE + 32 * (EXPERT_SLOTS // RING) * e + 32 * (n // RING + 1))
                        for c in range(4):
                            for dh in range(2):
                                g = 2 * dh + c % 2
                                mm = nt.matmul(PS[32 * g:32 * g + 32, 5, :], HTE[:, P * c + 32 * d:P * c + 32 * (d + 1)],
                                               ring[:, s, D * c + 512 * dh:D * c + 512 * (dh + 1)],
                                               start=(d == 0 and c < 2), stop=(d == 3 and c >= 2))
                        mm.then_inc(expert_slots, 1)
                    pe.wait_ge(ye_ready, e + 1)
                    for b in range(KD):
                        o = slice(64 * (b // 4), 64 * (b // 4) + 64)
                        mm = nt.matmul(PS[:, YB[b // 2], T * (b % 2):T * (b % 2 + 1)], YE[o, P * (b % 4):P * (b % 4 + 1)], GE[o, :],
                                       start=False, stop=False, skip_group_check=True)
                    mm.then_inc(scattered, 1)

            filters()
            norm_sums(1)
            pe.wait_ge(h2_ready, 1)
            project()
            mlstm()
            hyena()
            out()
            norm_sums(2)
            route()
            experts()
            norm_sums(3)

        def second_scalar(act):
            na = nc.scalar

            def root(n):
                act.wait_ge(ss2, n)
                na.activation(STD2, PS[:, 2, 0:T], ACT.Sqrt, bias=epsc, scale=1.0 / D).then_inc(std2, 1)

            def four_roots(n):
                act.wait_ge(r_ss, n)
                na.activation(E2F.rearrange("p a b -> p (a b)"), banks(2, 2), ACT.Sqrt, bias=epsc, scale=1.0 / P).then_inc(r_std, 1)

            act.dma_start(c2, io["constants_2"]).then_inc(two_loaded, 16)
            act.dma_start(p2, io["params_2"]).then_inc(two_loaded, 16)
            act.dma_start(wrt, io["router"]).then_inc(two_loaded, 16)
            act.dma_start(hyw1, io["hy_w1_2"][0]).then_inc(two_loaded, 16)
            act.dma_start(hyw2, io["hy_w2_2"][0]).then_inc(two_loaded, 16)
            act.dma_start(HYW3[0:64, :], io["hy_w3_2"][0]).then_inc(two_loaded, 16)
            act.dma_start(DELTA, io["hy_deltas_2"].partition_broadcast(P).rearrange("p o n -> p (o n)")).then_inc(two_loaded, 16)
            for n in range(2):
                act.wait_ge(f_arg, n + 1)
                na.activation(ARG, ARG, ACT.Sin).then_inc(f_sin, 1)
            act.wait_ge(f_abs, 1)
            for i in range(8):
                c, t = i // 2, i % 2
                if i >= 2:
                    act.wait_ge(f_filt, i - 1)
                na.activation(WIN[:, i % 2, :], DELTA[:, 512 * c:512 * (c + 1)], ACT.Exp, scale=c2[:, D_NT + t:D_NT + t + 1]).then_inc(f_win, 1)
            for i in range(8):
                o, s, kt = i // 4, i // 2 % 2, i % 2
                act.wait_ge(kf_ready, i + 1)
                na.activation(KF[:, kt, o, s, :], PS[:, 4 + i % 4, :], ACT.Copy).then_inc(kf_out, 1)
            root(1)
            for q in range(14):
                act.wait_ge(block_done, BASE2 + q + 1)
                f = ACT.Sigmoid if q in (6, 7) else ACT.Identity
                for b in range(2):
                    n = 2 * q + b
                    ins = na.activation(proj[:, n, :], PS[:, q % 2, T * b:T * (b + 1)], f, bias=p2[:, P2_BIN + n:P2_BIN + n + 1])
                ins.then_inc(act2, 1)
            for q in (14, 15):
                act.wait_ge(block_done, BASE2 + q + 1)
                for b in range(2):
                    n = 2 * (q - 14) + b
                    ins = na.activation(G4[0:H2, n, :], PS[0:H2, q % 2, T * b:T * (b + 1)], ACT.Identity, bias=p2[0:H2, P2_BG + n:P2_BG + n + 1])
                ins.then_inc(act2, 1)
            act.wait_ge(conv_ready, 1)
            na.activation(QK2, QK2, ACT.Silu).then_inc(conv_act, 1)
            act.wait_ge(gate_rows, 1)
            na.activation(LF[0:H2], LF[0:H2], ACT.Exp, scale=-1.0).then_inc(abs_rows, 1)
            act.wait_ge(abs_rows, 1)
            na.activation(LF[0:H2], LF[0:H2], ACT.Ln, bias=onec[0:H2, :]).then_inc(ln_rows, 1)
            act.wait_ge(m_tr, 1)
            for t in range(TT):
                na.activation(VT2[:, t, :], PS[:, 6 + t, :], ACT.Copy).then_inc(m_out, 1)
            act.wait_ge(m_tr, 2)
            na.activation(small[:, 0:16], PS[:, 5, 0:16], ACT.Copy).then_inc(m_out, 1)
            act.wait_ge(rows_ready, 2)
            na.activation(EMR[0:H2], EMR[0:H2], ACT.Exp, scale=-1.0).then_inc(em_rows, 1)
            for h in range(H2):
                act.wait_ge(m_em, h + 1)
                na.activation(EMS.rearrange("p a b -> p (a b)"), PS[:, 4, :], ACT.Copy).then_inc(m_emo, 1)
                act.wait_ge(m_arg, h + 1)
                na.activation(E2, E2, ACT.Exp).then_inc(m_exp, 1)
            four_roots(1)
            for o in range(2):
                act.wait_ge(z_tr, o + 1)
                for t in range(TT):
                    na.activation(ZTOK[:, t, :], PS[:, 6 + t, :], ACT.Copy).then_inc(z_out, 1)
            four_roots(2)
            root(2)
            for i in range(4):
                t, g = i // 2, i % 2
                act.wait_ge(tok2, i + 1)
                na.activation(HTOK[:, t, 512 * g:512 * (g + 1)], PS[:, 4 + i, :], ACT.Copy).then_inc(tok2_out, 1)
            act.wait_ge(rt_max, 1)
            na.activation(LOG, LOG, ACT.Exp).then_inc(rt_exp, 1)
            act.wait_ge(ix_ready, 1)
            na.activation(IG.rearrange("p a b -> p (a b)"), PS[:, 2, 0:32], ACT.Copy).then_inc(ix_out, 1)
            for k in range(KD):
                act.wait_ge(xs_psum, k + 1)
                na.activation(XS[:, :, k, :], banks(4 + k % 4, 1, EXPERTS, CAP), ACT.Copy).then_inc(xs_out, 1)
            with act.Fori(0, EXPERTS) as e:
                act.wait_ge(expert_slots, EXPERT_SLOTS * e + EXPERT_SLOTS + 4)
                na.activation(HSE, PS[:, 2, :], ACT.Silu).then_inc(hs_ready, 1)
                act.wait_ge(ht_ready, e + 1)
                na.activation(HTE, PS[:, 4, :], ACT.Copy).then_inc(ht_out, 1)
            root(3)

        def second_vector(dve):
            nv = nc.vector
            count = [0]

            def link(ins):
                count[0] += 1
                ins.then_inc(vec2, 1)
                dve.wait_ge(vec2, count[0])

            def square(n):
                nv.tensor_tensor(SQ2, xT[:, :, :], xT[:, :, :], ALU.mult).then_inc(sq2, 1)
                dve.wait_ge(std2, n)
                link(nv.reciprocal(RSTD2, STD2))

            def norm(n, gain, shift):
                square(n)
                for k in range(KD):
                    link(nv.scalar_tensor_tensor(hT[:, k, :], xT[:, k, :], gain[:, k:k + 1], RSTD2, ALU.mult, ALU.mult))
                    ins = nv.tensor_scalar(hT[:, k, :], hT[:, k, :], mod[:, shift + k:shift + k + 1], None, ALU.add)
                    if k < KD - 1:
                        link(ins)
                ins.then_inc(h2_ready, 1)

            def sine_argument(n):
                dve.wait_ge(f_hid, n + 1)
                link(nv.tensor_scalar(ARG, PS[0:64, 2 + n, 0:T], p2[0:64, P2_HY + n:P2_HY + n + 1], p2[0:64, P2_HY + 2:P2_HY + 3], ALU.add, ALU.mult))
                big = 1.5 * 2.0 ** 23
                two_pi = 2 * math.pi
                c1 = 6.28125
                link(nv.tensor_scalar(TRN, ARG, 1 / two_pi, None, ALU.mult))
                link(nv.tensor_scalar(TRN, TRN, big, None, ALU.add))
                link(nv.tensor_scalar(TRN, TRN, -big, None, ALU.add))
                link(nv.scalar_tensor_tensor(ARG, TRN, -c1, ARG, ALU.mult, ALU.add))
                link(nv.scalar_tensor_tensor(ARG, TRN, -(two_pi - c1), ARG, ALU.mult, ALU.add))
                pi = float(np.nextafter(np.float32(math.pi), np.float32(0)))
                nv.tensor_scalar(ARG, ARG, pi, -pi, ALU.min, ALU.max).then_inc(f_arg, 1)

            def filters():
                dve.wait_ge(two_loaded, 7 * 16)
                nv.scalar_tensor_tensor(DELTA, DELTA, -1.0, DELTA, ALU.mult, ALU.max).then_inc(f_abs, 1)
                sine_argument(0)
                sine_argument(1)
                for i in range(8):
                    c, t = i // 2, i % 2
                    dve.wait_ge(f_h, i + 1)
                    dve.wait_ge(f_win, i + 1)
                    nv.scalar_tensor_tensor(FILT[:, t, c, :], WIN[:, i % 2, :], 0.05, PS[:, 4 + i % 2, :], ALU.add, ALU.mult).then_inc(f_filt, 1)
                dve.wait_ge(f_filt, 8)
                for o in range(2):
                    f, b = FILT[:, :, 2 * o, :], FILT[:, :, 2 * o + 1, :]
                    link(nv.tensor_tensor(f, f, b, ALU.add))
                    nv.scalar_tensor_tensor(b, b, -2.0, f, ALU.mult, ALU.add).then_inc(f_sum, 1)

            def conv(dst, src, w, b, n, blocks):
                for i in range(n):
                    y, u = dst[:, i, :], proj[:, src + i, :]
                    tap = lambda j: p2[:, w + blocks * j + i:w + blocks * j + i + 1]
                    link(nv.tensor_scalar(y, u, tap(1), p2[:, b + i:b + i + 1], ALU.mult, ALU.add))
                    link(nv.scalar_tensor_tensor(y[:, 1:T], u[:, 0:T - 1], tap(0), y[:, 1:T], ALU.mult, ALU.add))
                    ins = nv.scalar_tensor_tensor(y[:, 0:T - 1], u[:, 1:T], tap(2), y[:, 0:T - 1], ALU.mult, ALU.add)
                    if i < n - 1:
                        link(ins)
                ins.then_inc(conv_ready, 1)

            def mlstm():
                f = G4[0:H2, 1::2, :]
                i_ = G4[0:H2, 0::2, :]
                lf, bb, aa, nm, emr, zer = (a[0:H2] for a in (LF, BB, AA, NM, EMR, ZER))
                dve.wait_ge(act2, 16)
                nv.scalar_tensor_tensor(lf, f, -1.0, f, ALU.mult, ALU.max).then_inc(gate_rows, 1)
                conv(QK2, 0, P2_CQW, P2_CQB, 8, 8)
                conv(HX2, 16, P2_CHW, P2_CHB, 12, 12)
                dve.wait_ge(conv_ready, 2)
                link(nv.memset(zer, 0.0))
                dve.wait_ge(ln_rows, 1)
                link(nv.scalar_tensor_tensor(lf, f, 0.0, lf, ALU.min, ALU.subtract))
                link(nv.tensor_tensor_scan(bb[:, 0, :], zer[:, 0, :], lf[:, 0, :], 0.0, ALU.add, ALU.add))
                link(nv.tensor_tensor_scan(bb[:, 1, ::-1], zer[:, 0, :], lf[:, 1, ::-1], 0.0, ALU.add, ALU.add))
                link(nv.tensor_tensor(aa, i_, bb, ALU.subtract))
                link(nv.tensor_tensor_scan(nm[:, 0, :], zer[:, 0, :], aa[:, 0, :], NEG, ALU.add, ALU.max))
                nv.tensor_tensor_scan(nm[:, 1, ::-1], zer[:, 0, :], aa[:, 1, ::-1], NEG, ALU.add, ALU.max).then_inc(rows_ready, 1)
                dve.wait_ge(rows_ready, 1)
                link(nv.tensor_tensor(emr, bb, nm, ALU.add))
                nv.tensor_scalar(nm, nm, -1.0, None, ALU.mult).then_inc(rows_ready, 1)
                dve.wait_ge(rows_ready, 2)
                dve.wait_ge(m_out, 3)
                e1 = E2.rearrange("p d j t -> p (d j t)")
                for h in range(H2):
                    dve.wait_ge(m_em, h + 1)
                    for d in range(2):
                        for j in range(TT):
                            ins = nv.tensor_scalar(E2[:, d, j, :], PS[:, 3, T * d:T * (d + 1)], ACOL[:, d, j, h:h + 1], 0.0, ALU.add, ALU.min)
                            if d + j < 2:
                                link(ins)
                    ins.then_inc(m_arg, 1)
                    dve.wait_ge(m_exp, h + 1)
                    link(nv.tensor_tensor(e1, e1, MASK2, ALU.mult))
                    dve.wait_ge(m_s, h + 1)
                    e3 = E2.rearrange("p d j t -> p d (j t)")
                    nv.scalar_tensor_tensor(e3, PS[:, 2, :].unsqueeze(1).broadcast_to([P, 2, 512]), DH2 ** -0.5, e3, ALU.mult, ALU.mult)\
                        .then_inc(m_w, 1)
                    dve.wait_ge(m_num, h + 1)
                    dve.wait_ge(m_emo, h + 1)
                    ems = EMS.rearrange("p a b -> p (a b)")
                    num = NUM.rearrange("p a b -> p (a b)")
                    link(nv.scalar_tensor_tensor(num, PS[:, 6, :], -1.0, ems, ALU.mult, ALU.max))
                    link(nv.tensor_tensor(num, PS[:, 6, :], num, ALU.max))
                    link(nv.reciprocal(num, num))
                    link(nv.tensor_tensor(num, PS[:, 5, :], num, ALU.mult))
                    nv.tensor_tensor(HS2[:, h, :], NUM[:, 0, :], NUM[:, 1, :], ALU.add).then_inc(m_h, 1)
                dve.wait_ge(m_h, H2)
                group_norm(1, HS2, P2_MN, 0, proj[:, 12:16, :])

            def group_norm(n, x, gain, at, gate):
                nv.tensor_tensor(E2F, x, x, ALU.mult).then_inc(r_sq, 1)
                dve.wait_ge(r_std, n)
                link(nv.reciprocal(E2F, E2F))
                for b in range(4):
                    ins = nv.scalar_tensor_tensor(hT[:, at + b, :], x[:, b, :], p2[:, gain + b:gain + b + 1], E2F[:, b, :], ALU.mult, ALU.mult)
                    if b < 3 or gate is not None:
                        link(ins)
                if gate is not None:
                    ins = nv.tensor_tensor(hT[:, at:at + 4, :], hT[:, at:at + 4, :], gate, ALU.mult)
                ins.then_inc(cat_ready, 1)

            def hyena():
                z = HX2[:, 8:12, :]
                for o in range(2):
                    dve.wait_ge(u2_ready, o + 1)
                    for kt in range(TT):
                        a, b = PS[:, 2 + 2 * kt, :], PS[:, 3 + 2 * kt, :]
                        c, d = KF[:, kt, o, 0, :], KF[:, kt, o, 1, :]
                        link(nv.tensor_tensor(TMP1, a, c, ALU.mult))
                        link(nv.tensor_tensor(TMP2, b, d, ALU.mult))
                        link(nv.tensor_tensor(YF[:, kt, 0, :], TMP1, TMP2, ALU.subtract))
                        link(nv.tensor_tensor(TMP1, a, d, ALU.mult))
                        link(nv.tensor_tensor(TMP2, b, c, ALU.mult))
                        ins = nv.tensor_tensor(YF[:, kt, 1, :], TMP1, TMP2, ALU.add)
                        if kt == 0:
                            link(ins)
                    ins.then_inc(yf_ready, 1)
                    dve.wait_ge(yt_ready, o + 1)
                    for b in range(4):
                        link(nv.scalar_tensor_tensor(z[:, b, :], z[:, b, :], p2[:, P2_HBIAS + 4 * o + b:P2_HBIAS + 4 * o + b + 1],
                                                     PS[:, 6 + b // 2, T * (b % 2):T * (b % 2 + 1)], ALU.mult, ALU.add))
                    nv.tensor_tensor(z, z, HX2[:, 4 * o:4 * o + 4, :], ALU.mult).then_inc(z_ready2, 1)
                    dve.wait_ge(z_ready2, o + 1)
                group_norm(2, z, P2_HN, 4, None)

            def residual(n, base, signal, gate, bank):
                for b in range(2):
                    k = 2 * n + b
                    ins = nv.scalar_tensor_tensor(xT[:, k, :], PS[:, bank, T * b:T * (b + 1)], mod[:, gate + k:gate + k + 1], xT[:, k, :],
                                                  ALU.mult, ALU.add)
                ins.then_inc(signal, 1)

            def route():
                m, s = ST4[:, 0:TT], ST4[:, TT:2 * TT]
                wide = lambda a: a.unsqueeze(2).broadcast_to([P, TT, EXPERTS])
                dve.wait_ge(rt_logit, 1)
                lg = banks(2, 1, TT, EXPERTS)
                link(nv.tensor_reduce(m, lg, AX, ALU.max))
                nv.tensor_tensor(LOG, lg, wide(m), ALU.subtract).then_inc(rt_max, 1)
                dve.wait_ge(rt_exp, 1)
                link(nv.tensor_reduce(s, LOG, AX, ALU.add))
                link(nv.reciprocal(s, s))
                nv.tensor_tensor(LOG, LOG, wide(s), ALU.mult).then_inc(rt_prob, 1)
                dve.wait_ge(rt_tr, 1)
                link(nv.tensor_copy(AFF, PS[0:EXPERTS, 3, 0:T]))
                for g in range(CAP // 8):
                    v, ix = VAL[:, 8 * g:8 * g + 8], IDXU[:, 8 * g:8 * g + 8].bitcast(U32)
                    link(nv.max(v, AFF))
                    link(nv.max_index(ix, v, AFF))
                    link(nv.match_replace(AFF, v, AFF, -1.0))
                link(nv.tensor_copy(IDXF, IDXU.bitcast(U32)))
                for a, src in enumerate((IDXF, VAL)):
                    ins = nv.tensor_copy(REP[:, a, :, :], src.unsqueeze(1).broadcast_to([EXPERTS, 4, CAP]))
                    if a == 0:
                        link(ins)
                ins.then_inc(topk_done, 1)
                eye = ident[0:EXPERTS, 0:EXPERTS].unsqueeze(2).broadcast_to([EXPERTS, EXPERTS, CAP])
                nv.tensor_tensor(DIAG[0:EXPERTS, :].rearrange("p (e s) -> p e s", s=CAP), eye,
                                 IDXF.unsqueeze(1).broadcast_to([EXPERTS, EXPERTS, CAP]), ALU.mult).then_inc(diag_ready, 1)
                dve.wait_ge(row_ready, 1)
                for t in range(TT):
                    ins = nv.tensor_scalar(PICK[:, t, :], PS[:, 3, :], c2[:, D_TOK + t:D_TOK + t + 1], None, ALU.is_equal)
                    if t == 0:
                        link(ins)
                ins.then_inc(pick_ready, 1)
                nv.memset(ZERO, 0.0).then_inc(zero_e, 1)
                dve.wait_ge(xs_out, KD)
                dve.wait_ge(ix_out, 1)

            def experts():
                iota = c2[:, D_IOTA:D_IOTA + T]
                with dve.Fori(0, EXPERTS) as e:
                    dve.wait_ge(expert_slots, EXPERT_SLOTS * e + 8)
                    nv.tensor_scalar(XSE.rearrange("p k s -> p (k s)"), XS[:, e, :, :].rearrange("p k s -> p (k s)"), 1.0, None, ALU.mult)\
                        .then_inc(xs_staged, 1)
                    dve.wait_ge(scattered, e + 1)
                    nv.tensor_scalar(GE, iota, IG[:, 0, bass.ts(e, 1)], IG[:, 1, bass.ts(e, 1)], ALU.is_equal, ALU.mult).then_inc(ge_ready, 1)
                    dve.wait_ge(expert_slots, EXPERT_SLOTS * e + EXPERT_SLOTS + 8)
                    dve.wait_ge(hs_ready, e + 1)
                    nv.tensor_tensor(HE, HSE, PS[:, 3, :], ALU.mult).then_inc(he_ready, 1)
                    dve.wait_ge(expert_slots, EXPERT_SLOTS * e + EXPERT_SLOTS + 12)
                    nv.tensor_copy(YE, PS[:, 5, :]).then_inc(ye_ready, 1)

            filters()
            link(nv.scalar_tensor_tensor(gs1, mod[:, 8:16], 1.0, p2[:, P2_GMIX:P2_GMIX + KD], ALU.add, ALU.mult))
            link(nv.scalar_tensor_tensor(gs2, mod[:, 32:40], 1.0, p2[:, P2_GFFN:P2_GFFN + KD], ALU.add, ALU.mult))
            norm(1, gs1, 0)
            mlstm()
            hyena()
            for n in range(4):
                dve.wait_ge(block_done, BASE2 + 16 + n + 1)
                residual(n, 0, dve2, 16, (16 + n) % 2)
            dve.wait_ge(dve2, 4)
            norm(2, gs2, 24)
            route()
            experts()
            dve.wait_ge(scattered, EXPERTS + 1)
            for n, b in enumerate((6, 7, 0, 1)):
                residual(n, 0, moe_sum, 40, b)
            dve.wait_ge(moe_sum, 4)
            square(3)
            for k in range(KD):
                ins = nv.scalar_tensor_tensor(hT[:, k, :], xT[:, k, :], p2[:, P2_GFIN + k:P2_GFIN + k + 1], RSTD2, ALU.mult, ALU.mult)
                if k < KD - 1:
                    link(ins)
            ins.then_inc(h2_ready, 1)

        block = ctx.enter_context(nc.Block())

        @block.sync
        def _(sp):
            def load(slot, pieces):
                for dst, src in pieces:
                    sp.dma_start(dst, src).then_inc(ring_full[slot], 16)

            def by_rows(w, slot, cols):
                n = w.shape[0] // P
                c = w.shape[1]
                v = w.rearrange("(k p) n -> p k n", p=P)
                r = ring[:, slot, 0:n * c].rearrange("p (k n) -> p k n", n=c)
                load(slot, [(r[:, 0:n // 2], v[:, 0:n // 2]), (r[:, n // 2:n], v[:, n // 2:n])])

            for n in range(ADA_SLOTS):
                if n >= RING:
                    sp.wait_ge(block_done, n - RING + 1)
                by_rows(io["w_ada_2"][0][:, 512 * n:512 * (n + 1)], n % RING, 512)

            before = [sum(SLOT_BLOCKS[:n + 1]) for n in range(LAYER_SLOTS)]
            with sp.Fori(0, LAYERS) as l:
                for n in range(LAYER_SLOTS):
                    if n >= RING:
                        sp.wait_ge(block_done, ADA_BLOCKS + LAYER_BLOCKS * l + before[n - RING])
                    else:
                        sp.wait_ge(block_done, ADA_BLOCKS + LAYER_BLOCKS * l - (RING - 1 - n))
                    sp.sem_inc(slot_freed, 1)
                    s = n % RING
                    if n < S_MIX:
                        by_rows(io["w_in"][l][:, IN_ORDER[n]:IN_ORDER[n] + 512], s, 512)
                    elif n < S_OUT:
                        by_rows(io[("w_attn_o", "w_rwkv_o", "w_ret_o")[n - S_MIX]][l], s, D)
                    elif n < S_FFN:
                        by_rows(io["w_out"][l][:, 512 * (n - S_OUT):512 * (n - S_OUT + 1)], s, 512)
                    elif n < S_DOWN:
                        c = 256 * (n - S_FFN)
                        load(s, [(ring[:, s, 2048 * g:2048 * (g + 1)].rearrange("p (k n) -> p k n", n=256),
                                  io[("w_ffn_gate", "w_ffn_up")[g]][l][:, c:c + 256].rearrange("(k p) n -> p k n", p=P))
                                 for g in range(2)])
                    else:
                        c = P * (n - S_DOWN)
                        by_rows(io["w_ffn_down"][l][:, c:c + P], s, P)
            second_sync(sp, load, by_rows)

        @block.gpsimd
        def _(pool):
            pool.memset(bias[:, 0:1], EPS).then_inc(bias_set, 1)
            pool.memset(bias[:, 1:2], LNX_EPS).then_inc(bias_set, 1)
            pool.memset(bias[:, 2:3], 1.0).then_inc(bias_set, 1)
            with pool.Fori(0, LAYERS) as l:
                pool.wait_ge(z_ready, 1)
                pool.memset(w_(9216, 4096), 0.0).then_inc(gm_zero, 1)
                pool.wait_ge(layer_fin, 3)
                pool.sem_clear(layer_sems)
                pool.sem_inc(layer_go, 1)
            second_pool(pool)

        @block.tensor
        def _(pe):
            nt = nc.tensor

            def ada():
                pe.wait_ge(cond_loaded, 5 * 16)
                for n in range(ADA_SLOTS):
                    pe.wait_ge(ring_full[n % RING], 32 * (n // RING + 1))
                    j = 32 * (n % 4)
                    for k in range(KD):
                        mm = nt.matmul(PS[j:j + 1, 2 + n // 4, :], CT[:, k:k + 1], ring[:, n % RING, 512 * k:512 * (k + 1)],
                                       start=(k == 0), stop=(k == KD - 1))
                    mm.then_inc(block_done, 1)
                pe.wait_ge(mod_rows, 4)
                for n in range(48):
                    j = 32 * (n // 4 % 4)
                    mm = nt.matmul(PS[:, 4 + n // 4 % 4, n:n + 1], MROW[j:j + 1, n // 16, P * (n % 4):P * (n % 4 + 1)],
                                   con[j:j + 1, C_ONES:C_ONES + 1], start=True, stop=True)
                mm.then_inc(mod_cols, 1)

            def taken(q):
                q -= 2
                if q < 0:
                    return
                if q < Q_MIX:
                    pe.wait_ge(act_taken, q + 1)
                elif q < Q_FFN:
                    pe.wait_ge(dve_taken, q - Q_MIX + 1)
                elif q < Q_DOWN:
                    if (q - Q_FFN) % 2 == 0:
                        pe.wait_ge(act_taken, N_PROJ + (q - Q_FFN) // 2 + 1)
                    else:
                        pe.wait_ge(dve_taken, N_MIX + N_OUT + (q - Q_FFN) // 2 + 1)
                else:
                    pe.wait_ge(dve_taken, N_MIX + N_OUT + N_FFN // 2 + q - Q_DOWN + 1)

            def product(q, weight, moving, kn, n_blocks=2):
                taken(q)
                for b in range(n_blocks):
                    for k in range(kn):
                        mm = nt.matmul(PS[:, q % 2, T * b:T * (b + 1)], weight(b, k), moving(k), start=(k == 0), stop=(k == kn - 1))
                mm.then_inc(block_done, 1)

            def norm_sums(n):
                pe.wait_ge(sq_ready, n)
                for k in range(KD):
                    mm = nt.matmul(PS[:, 2, 0:T], ones, SQ[:, k, :], start=(k == 0), stop=(k == KD - 1))
                mm.then_inc(ss_ready, 1)

            def proj_slot(l, n):
                s = n % RING
                pe.wait_ge(ring_full[s], full(l, n))
                for half in range(2):
                    product(2 * n + half, lambda b, k: ring[:, s, 512 * k + P * (2 * half + b):512 * k + P * (2 * half + b + 1)],
                            lambda k: hT[:, k, :], KD)

            def head_sums(bank, src, signal):
                for n in range(2):
                    mm = nt.matmul(PS[:, bank + n, :], bd, src[:, 2 * n:2 * n + 2, :].rearrange("p a b -> p (a b)"), start=True, stop=True)
                mm.then_inc(signal, 1)

            def lora_products():
                pe.wait_ge(lora_in, 2)
                for b in range(HB):
                    mm = nt.matmul(PS[:, 2 + b // 2, T * (b % 2):T * (b % 2 + 1)], lora[0:64, P * b:P * (b + 1)],
                                   proj[0:64, B_LORA, :], start=True, stop=True)
                mm.then_inc(lora_done, 1)
                for b in range(HB):
                    mm = nt.matmul(PS[:, 4 + b // 2, T * (b % 2):T * (b % 2 + 1)], lora[64:128, P * b:P * (b + 1)],
                                   proj[64:128, B_LORA, :], start=True, stop=True)
                mm.then_inc(lora_done, 1)
                for b in range(HB):
                    mm = nt.matmul(PS[:, 6 + b // 2, T * (b % 2):T * (b % 2 + 1)], lora[:, 512 + P * b:512 + P * (b + 1)],
                                   proj[:, B_GD, :], start=True, stop=True)
                mm.then_inc(lora_done, 1)

            def rwkv_prep():
                pe.wait_ge(kk_sq, 1)
                pe.wait_ge(lora_out, 4)
                head_sums(2, X3, kk_ss)
                pe.wait_ge(lora_out, 10)
                for t in range(TT):
                    for b in range(HB):
                        mm = nt.transpose(PS[:, 4 + t, P * b:P * (b + 1)], proj[:, B_V + b, P * t:P * (t + 1)], ident)
                mm.then_inc(tok_ready, 1)
                pe.wait_ge(gram_in, 1)
                for n, src in enumerate((AT, KK)):
                    for b in range(HB):
                        mm = nt.transpose(PS[:, 6 + n, P * b:P * (b + 1)], src[:, b, 0:P], ident)
                mm.then_inc(tok_ready, 1)
                pe.wait_ge(kk_std, 1)
                pe.wait_ge(bonus_in, 1)
                head_sums(2, Y, bonus_ss)

            def rwkv_chunk(t):
                cols = slice(P * t, P * (t + 1))
                if t == 0:
                    pe.wait_ge(tok_out, 4)
                    pe.wait_ge(bonus_out, 1)
                else:
                    pe.wait_ge(y_out, 1)
                    pe.wait_ge(st_ready, 1)
                for h in range(HEADS):
                    bk = 2 + h % 2 + 2 * (h // 2 % 2)
                    if h >= 4:
                        pe.wait_ge(gram_taken, 8 * t + h - 3)
                    o, b = hrow(h), h // 2
                    nt.matmul(PS[:, bk, 0:P], AR[o, b, t, 0, :], AT[o, b, cols], start=True, stop=True)
                    nt.matmul(PS[:, bk, P:2 * P], AT[o, b, cols], AR[o, b, t, 1, :], start=True, stop=True)
                    nt.matmul(PS[:, bk, 2 * P:4 * P], KK[o, b, cols], AR[o, b, t, :, :].rearrange("p a b -> p (a b)"),
                              start=True, stop=True).then_inc(gram_ready, 1)
                for lev in range(LEVELS):
                    for half in range(2):
                        pe.wait_ge(qt_ready, t * (2 * LEVELS + 1) + (2 * lev + half if lev else 1))
                        if lev == 0:
                            pe.wait_ge(gram_taken, 8 * t + 4 * (half + 1))
                        for u in range(4 * half, 4 * half + 4):
                            mm = nt.matmul(PS[:, 6 + half, P * (u % 4):P * (u % 4 + 1)], GM[:, u, 0:P], QT[:, u, 0, :],
                                           start=True, stop=True)
                        mm.then_inc(w1_ready, 1)
                    for half in range(2):
                        i = (t * LEVELS + lev) * 2 + half
                        pe.wait_ge(w1_masked, i + 1)
                        for u in range(4 * half, 4 * half + 4):
                            bk, c = 2 + 2 * half + u % 4 // 2, 2 * P * (u % 2)
                            nt.matmul(PS[:, bk, c:c + P], QT[:, u, 1, :], W1S[:, u, :], start=True, stop=True)
                            mm = nt.matmul(PS[:, bk, c + P:c + 2 * P], W1S[:, u, :], QT[:, u, 1, :], start=True, stop=True)
                        mm.then_inc(dq_ready, 1)
                pe.wait_ge(qt_ready, (t + 1) * (2 * LEVELS + 1))
                for h in [0, 2, 4, 6, 1, 3, 5, 7]:
                    out = PS[:, 6 + h % 2, HD * (h // 2):HD * (h // 2 + 1)]
                    if t:
                        nt.matmul(out, AR[hrow(h), h // 2, t, 0, :], ST[hrow(h), h // 2, :], start=True, stop=False)
                    mm = nt.matmul(out, GM[:, h, 2 * P:3 * P], VTOK[:, t, HD * h:HD * (h + 1)], start=(t == 0), stop=True)
                mm.then_inc(rhs_ready, 1)
                pe.wait_ge(rhs_out, 2 * (t + 1))
                for h in range(HEADS):
                    mm = nt.matmul(PS[:, 2, HD * h:HD * (h + 1)], QT[:, h, 0, :], RHS[:, h, :], start=True, stop=True)
                mm.then_inc(u_ready, 1)
                pe.wait_ge(u_out, t + 1)
                for h in range(HEADS):
                    out = PS[hrow(h), 3, P * (h // 2):P * (h // 2 + 1)]
                    nt.matmul(out, U[:, h, :], GM[:, h, P:2 * P], start=True, stop=False)
                    mm = nt.matmul(out, VTOK[:, t, HD * h:HD * (h + 1)], GM[:, h, 3 * P:4 * P], start=False, stop=(t == 0))
                    if t:
                        mm = nt.matmul(out, ST[hrow(h), h // 2, :], AR[hrow(h), h // 2, t, 1, :], start=False, stop=True)
                mm.then_inc(y_ready, 1)
                if t == 0:
                    for h in range(HEADS):
                        out = PS[hrow(h), 5, HD * (h // 2):HD * (h // 2 + 1)]
                        nt.matmul(out, BKT[:, 0, HD * h:HD * (h + 1)], U[:, h, :], start=True, stop=False)
                        mm = nt.matmul(out, BKT[:, 1, HD * h:HD * (h + 1)], VTOK[:, 0, HD * h:HD * (h + 1)], start=False, stop=True)
                    mm.then_inc(s_ready, 1)

            def rwkv_norm():
                pe.wait_ge(y_out, 2)
                head_sums(4, Y, ln_ss)
                pe.wait_ge(ln_in, 1)
                head_sums(6, X1, ln_ss)

            def attention():
                pe.wait_ge(att_sq, 2)
                pe.wait_ge(ln_std, 1)
                head_sums(2, ATS[:, 0:HB, :], att_ss)
                nt.matmul(PS[:, 4, 0:T], bd, ATS[:, HB, :], start=True, stop=True).then_inc(att_ss, 1)
                for t in range(TT):
                    mm = nt.transpose(PS[:, 6, P * t:P * (t + 1)], proj[:, B_AV, P * t:P * (t + 1)], ident)
                mm.then_inc(att_tr, 1)
                pe.wait_ge(att_qk, 2)
                for kv in range(2):
                    mm = nt.matmul(PS[:, 5, T * kv:T * (kv + 1)], con[:, C_DUP + P * kv:C_DUP + P * (kv + 1)], proj[:, B_AK, :],
                                   start=True, stop=True)
                mm.then_inc(att_tr, 1)
                pe.wait_ge(att_kv, 2)
                for r, (t, heads) in enumerate(ROUNDS):
                    w = P * (t + 1)
                    if r:
                        pe.wait_ge(oa_out, r)
                    for n, h in enumerate(heads):
                        at = n * w
                        mm = nt.matmul(PS[:, 2 + at // 512, at % 512:at % 512 + w], proj[hrow(h), B_AQ + h // 2, P * t:P * (t + 1)],
                                       KDUP[hrow(h), h // 4, 0:w], start=True, stop=True)
                    mm.then_inc(sc_ready, 1)
                    pe.wait_ge(p_ready, r + 1)
                    for n in range(8):
                        mm = nt.transpose(PS[:, 6 + n // 4, P * (n % 4):P * (n % 4 + 1)], SCO[:, P * n:P * (n + 1)], ident)
                    mm.then_inc(pt_ready, 1)
                    pe.wait_ge(pt_out, r + 1)
                    for n, h in enumerate(heads):
                        kv = h // 4
                        for j in range(t + 1):
                            mm = nt.matmul(PS[hrow(h), 4, P * (h // 2):P * (h // 2 + 1)], VATT[:, j, HD * kv:HD * (kv + 1)],
                                           PT[:, n * (t + 1) + j, :], start=(j == 0), stop=(j == t))
                    mm.then_inc(oa_ready, 1)

            def retention():
                pe.wait_ge(oa_out, 3)
                for n, at in enumerate((B_RQ, B_RK)):
                    for b in range(2):
                        mm = nt.matmul(PS[:, 2 + 2 * n + b, :], perm, proj[:, at + 2 * b:at + 2 * b + 2, :].rearrange("p a b -> p (a b)"),
                                       start=True, stop=True)
                    mm.then_inc(rot_ready, 1)
                for t in range(TT):
                    for b in range(HB):
                        mm = nt.transpose(PS[:, 6 + t, P * b:P * (b + 1)], proj[:, B_RV + b, P * t:P * (t + 1)], ident)
                mm.then_inc(vr_ready, 1)
                pe.wait_ge(rot_out, 2)
                for h in range(HEADS):
                    o, b, bk = hrow(h), h // 2, 2 + h % 2 + 2 * (h // 2 % 2)
                    if h >= 4:
                        pe.wait_ge(rs_out, h - 3)
                    nt.matmul(PS[:, bk, 0:T], proj[o, B_RK + b, 0:P], proj[o, B_RQ + b, :], start=True, stop=True)
                    nt.matmul(PS[:, bk, T:T + P], proj[o, B_RK + b, P:T], proj[o, B_RQ + b, P:T], start=True, stop=True)\
                        .then_inc(rs_ready, 1)
                pe.wait_ge(vr_out, 2)
                for h in range(HEADS):
                    pe.wait_ge(rs_out, h + 1)
                    o, b = hrow(h), h // 2
                    bk, c = 6 + b // 2, T * (b % 2)
                    nt.matmul(PS[o, bk, c:c + T], VRET[:, 0, HD * h:HD * (h + 1)], SM[:, h, 0:T], start=True, stop=False)
                    mm = nt.matmul(PS[o, bk, c + P:c + T], VRET[:, 1, HD * h:HD * (h + 1)], SM[:, h, T:T + P], start=False, stop=True)
                mm.then_inc(oc_psum, 1)
                pe.wait_ge(oc_sq, 1)
                head_sums(2, XR, oc_ss)

            def mix(l):
                for br, (src, at, ready) in enumerate(((proj, B_AQ, oa_out), (Y, 0, ob_ready), (proj, B_RQ, oc_ready))):
                    n = S_MIX + br
                    pe.wait_ge(ready, 3 if br == 0 else 1)
                    pe.wait_ge(ring_full[n % RING], full(l, n))
                    for i in range(4):
                        product(Q_MIX + 4 * br + i, lambda b, k: ring[:, n % RING, D * k + P * (2 * i + b):D * k + P * (2 * i + b + 1)],
                                lambda k: src[:, at + k, :], HB)

            def out(l):
                pe.wait_ge(dve_taken, N_MIX)
                for n in range(2):
                    s = (S_OUT + n) % RING
                    pe.wait_ge(ring_full[s], full(l, S_OUT + n))
                    for i in range(2):
                        product(Q_OUT + 2 * n + i, lambda b, k: ring[:, s, 512 * k + P * (2 * i + b):512 * k + P * (2 * i + b + 1)],
                                lambda k: hT[:, k, :], KD)

            def ffn(l):
                pe.wait_ge(h_ready, 2)
                for n in range(N_FFN // 2):
                    s = (S_FFN + n) % RING
                    pe.wait_ge(ring_full[s], full(l, S_FFN + n))
                    for g in range(2):
                        product(Q_FFN + 2 * n + g, lambda b, k: ring[:, s, 2048 * g + 256 * k + P * b:2048 * g + 256 * k + P * (b + 1)],
                                lambda k: hT[:, k, :], KD)
                pe.wait_ge(dve_taken, N_MIX + N_OUT + N_FFN // 2)
                for n in range(N_DOWN):
                    s = (S_DOWN + n) % RING
                    pe.wait_ge(ring_full[s], full(l, S_DOWN + n))
                    product(Q_DOWN + n, lambda b, k: ring[:, s, P * k:P * (k + 1)], lambda k: HID[:, k, :], FB, 1)

            pe.wait_ge(const_loaded, 32)
            ada()
            with pe.Fori(0, LAYERS) as l:
                pe.wait_ge(par_loaded, 32)
                norm_sums(1)
                pe.wait_ge(h_ready, 1)
                for n in range(5):
                    proj_slot(l, n)
                lora_products()
                for n in range(5, 9):
                    proj_slot(l, n)
                rwkv_prep()
                for n in range(9, S_MIX):
                    proj_slot(l, n)
                rwkv_chunk(0)
                rwkv_chunk(1)
                rwkv_norm()
                attention()
                retention()
                mix(l)
                out(l)
                norm_sums(2)
                ffn(l)
                pe.wait_ge(dve_taken, N_MIX + N_OUT + N_FFN // 2 + N_DOWN)
                pe.sem_inc(layer_fin, 1)
                pe.wait_ge(layer_go, l + 1)
                pe.sem_inc(layer_joined, 1)
            second_tensor(pe)

        @block.scalar
        def _(act):
            na = nc.scalar
            def proj_out(l, lo, hi):
                for q in range(lo, hi):
                    act.wait_ge(block_done, done(l, q))
                    f = ACT.Copy
                    if 2 * q >= B_GATE:
                        f = ACT.Sigmoid
                    elif 2 * q >= B_RG:
                        f = ACT.Silu
                    na.activation(proj[:, 2 * q:2 * q + 2, :].rearrange("p a b -> p (a b)"), PS[:, q % 2, :], f).then_inc(act_taken, 1)

            def norm_root(n):
                act.wait_ge(ss_ready, n)
                na.activation(STD, PS[:, 2, 0:T], ACT.Sqrt, bias=epsc, scale=1.0 / D).then_inc(std_ready, 1)

            def lora_inputs():
                act.wait_ge(z_ready, 1)
                na.activation(proj[0:64, B_LORA, :], proj[0:64, B_LORA, :], ACT.Tanh).then_inc(lora_in, 1)
                na.activation(proj[:, B_GD, :], proj[:, B_GD, :], ACT.Sigmoid).then_inc(lora_in, 1)

            def lora_outputs():
                for n, (dst, col) in enumerate(((X1, PL_W0), (AT, PL_A0))):
                    act.wait_ge(lora_done, n + 1)
                    for b in range(HB):
                        na.activation(dst[:, b, :], PS[:, 2 + 2 * n + b // 2, T * (b % 2):T * (b % 2 + 1)], ACT.Sigmoid,
                                      bias=par[:, col + b:col + b + 1]).then_inc(lora_out, 1)
                act.wait_ge(lora_done, 3)
                for n in range(2):
                    na.activation(GT[:, 2 * n:2 * n + 2, :].rearrange("p a b -> p (a b)"), PS[:, 6 + n, :], ACT.Copy).then_inc(lora_out, 1)

            def rwkv_prep():
                act.wait_ge(tok_ready, 1)
                for t in range(TT):
                    na.activation(VTOK[:, t, :], PS[:, 4 + t, :], ACT.Copy).then_inc(tok_out, 1)
                act.wait_ge(kk_ss, 1)
                na.activation(Y[:, :, :].rearrange("p a b -> p (a b)"), banks(2, 2), ACT.Sqrt).then_inc(kk_std, 1)
                act.wait_ge(cum_ready, 2)
                na.activation(X1[:, :, :], X1[:, :, :], ACT.Exp, scale=-KAPPA).then_inc(exps_ready, 1)
                na.activation(X3[:, :, :], X2[:, :, :], ACT.Exp, scale=-KAPPA).then_inc(exps_ready, 1)
                act.wait_ge(exps_ready, 2)
                na.activation(X2[:, :, :], X2[:, :, :], ACT.Exp, scale=KAPPA).then_inc(exps_ready, 1)
                na.activation(MIDE, MID[:, :, 1], ACT.Exp, scale=-KAPPA).then_inc(exps_ready, 1)
                act.wait_ge(tok_ready, 2)
                for n in range(2):
                    na.activation(BKT[:, n, :], PS[:, 6 + n, :], ACT.Copy).then_inc(tok_out, 1)

            def rwkv_chunk(t):
                act.wait_ge(rhs_ready, t + 1)
                for odd in range(2):
                    na.activation(RHS[:, odd::2, :], banks(6 + odd, 1, HB, HD), ACT.Copy).then_inc(rhs_out, 1)
                act.wait_ge(u_ready, t + 1)
                na.activation(U[:, :, :].rearrange("p a b -> p (a b)"), PS[:, 2, :], ACT.Copy).then_inc(u_out, 1)
                act.wait_ge(y_ready, t + 1)
                na.activation(Y[:, :, P * t:P * (t + 1)], banks(3, 1, HB, P), ACT.Copy).then_inc(y_out, 1)

            def rwkv_norm():
                act.wait_ge(ln_ss, 2)
                na.activation(X2[:, :, :].rearrange("p a b -> p (a b)"), banks(6, 2), ACT.Sqrt, bias=lnxc, scale=1.0 / HD).then_inc(ln_std, 1)

            def attention():
                act.wait_ge(att_ss, 2)
                na.activation(ATS[:, 0:HB, :].rearrange("p a b -> p (a b)"), banks(2, 2), ACT.Sqrt, bias=epsc, scale=1.0 / HD).then_inc(att_std, 1)
                na.activation(ATS[:, HB, :], PS[:, 4, 0:T], ACT.Sqrt, bias=epsc, scale=1.0 / HD).then_inc(att_std, 1)
                act.wait_ge(att_tr, 1)
                na.activation(VATT[:, :, :].rearrange("p a b -> p (a b)"), PS[:, 6, 0:T], ACT.Copy).then_inc(att_kv, 1)
                act.wait_ge(att_tr, 2)
                na.activation(KDUP[:, :, :].rearrange("p a b -> p (a b)"), PS[:, 5, :], ACT.Copy).then_inc(att_kv, 1)
                for r, (t, heads) in enumerate(ROUNDS):
                    act.wait_ge(sc_max, r + 1)
                    na.activation(SCO, SCO, ACT.Exp).then_inc(sc_exp, 1)
                    na.activation(SK[:, 0:len(heads)], SK[:, 0:len(heads)], ACT.Exp).then_inc(sc_exp, 1)
                    act.wait_ge(pt_ready, r + 1)
                    na.activation(PT[:, :, :].rearrange("p a b -> p (a b)"), banks(6, 2), ACT.Copy).then_inc(pt_out, 1)
                    act.wait_ge(oa_ready, r + 1)
                    b0, b1 = (0, 4) if t == 0 else (2 * (r - 1), 2 * r)
                    na.activation(proj[:, B_AQ + b0:B_AQ + b1, P * t:P * (t + 1)],
                                  PS[:, 4, P * b0:P * b1].rearrange("p (a b) -> p a b", b=P), ACT.Copy).then_inc(oa_out, 1)

            def retention():
                act.wait_ge(ob_ready, 1)
                act.dma_start(w_(0, HEADS * 3 * P), io["decay"]).then_inc(dec_loaded, 16)
                act.wait_ge(vr_ready, 1)
                for t in range(TT):
                    na.activation(VRET[:, t, :], PS[:, 6 + t, :], ACT.Copy).then_inc(vr_out, 1)
                act.wait_ge(oc_psum, 1)
                na.activation(proj[:, B_RQ:B_RQ + HB, :].rearrange("p a b -> p (a b)"), banks(6, 2), ACT.Copy).then_inc(oc_out, 1)
                act.wait_ge(oc_ss, 1)
                na.activation(XR[:, :, :].rearrange("p a b -> p (a b)"), banks(2, 2), ACT.Sqrt, bias=epsc, scale=1.0 / HD).then_inc(oc_std, 1)

            def ffn(l):
                for n in range(N_FFN // 2):
                    act.wait_ge(block_done, done(l, Q_FFN + 2 * n))
                    if n >= 2:
                        act.wait_ge(dve_taken, N_MIX + N_OUT + n - 1)
                    na.activation(SILU[:, n % 2, :], PS[:, 0, :], ACT.Silu).then_inc(act_taken, 1)

            act.dma_start(con[:, :], io["constants"]).then_inc(const_loaded, 16)
            act.dma_start(xT[:, :, :], io["xT"]).then_inc(const_loaded, 16)
            act.dma_start(CT, io["cT"]).then_inc(cond_loaded, 16)
            for j in range(4):
                act.dma_start(BROW[32 * j:32 * j + 1, :, :], io["b_ada_2"].rearrange("o (b j n) -> o j b n", j=4, n=512)[:, j])\
                    .then_inc(cond_loaded, 16)
            act.wait_ge(bias_set, 3)
            with act.Fori(0, LAYERS) as l:
                act.dma_start(par[:, :], io["layer_params"][l]).then_inc(par_loaded, 16)
                act.dma_start(lora[:, :], io["layer_lora"][l]).then_inc(par_loaded, 16)
                norm_root(1)
                proj_out(l, 0, 8)
                lora_inputs()
                proj_out(l, 8, 10)
                lora_outputs()
                proj_out(l, 10, 18)
                rwkv_prep()
                proj_out(l, 18, N_PROJ)
                rwkv_chunk(0)
                rwkv_chunk(1)
                rwkv_norm()
                attention()
                retention()
                norm_root(2)
                ffn(l)
                act.wait_ge(act_taken, N_PROJ + N_FFN // 2)
                act.sem_inc(layer_fin, 1)
                act.wait_ge(layer_go, l + 1)
                act.sem_inc(layer_joined, 1)
            second_scalar(act)

        @block.vector
        def _(dve):
            nv = nc.vector
            count = [0]

            def link(ins):
                count[0] += 1
                ins.then_inc(vec_order, 1)
                dve.wait_ge(vec_order, count[0])

            def norm(n, gain):
                nv.tensor_tensor(SQ, xT[:, :, :], xT[:, :, :], ALU.mult).then_inc(sq_ready, 1)
                dve.wait_ge(std_ready, n)
                link(nv.reciprocal(RSTD, STD))
                for k in range(KD):
                    ins = nv.scalar_tensor_tensor(hT[:, k, :], xT[:, k, :], par[:, gain + k:gain + k + 1], RSTD, ALU.mult, ALU.mult)
                    if k < KD - 1:
                        link(ins)
                ins.then_inc(h_ready, 1)

            def rwkv_mix():
                dve.wait_ge(act_taken, 8)
                raw = proj[:, B_R:B_R + RW_BLOCKS, :]
                link(nv.tensor_tensor(SHIFT[:, :, 1:T], raw[:, :, 0:T - 1], raw[:, :, 1:T], ALU.subtract))
                link(nv.tensor_scalar(SHIFT[:, :, 0:1], raw[:, :, 0:1], -1.0, None, ALU.mult))
                for b in range(RW_BLOCKS):
                    ins = nv.scalar_tensor_tensor(raw[:, b, :], SHIFT[:, b, :], par[:, PL_MU + b:PL_MU + b + 1], raw[:, b, :],
                                                  ALU.mult, ALU.add)
                    if b < RW_BLOCKS - 1:
                        link(ins)
                ins.then_inc(z_ready, 1)

            r, k, v = (proj[:, b:b + HB, :] for b in (B_R, B_K, B_V))

            def rwkv_prep():
                dve.wait_ge(z_ready, 1)
                for b in range(HB):
                    link(nv.tensor_scalar(KK[:, b, :], k[:, b, :], par[:, PL_KK + b:PL_KK + b + 1], None, ALU.mult))
                nv.tensor_tensor(X3, KK, KK, ALU.mult).then_inc(kk_sq, 1)
                dve.wait_ge(lora_out, 8)
                for b in range(HB):
                    for t in range(TT):
                        c = slice(P * t, P * (t + 1))
                        link(nv.tensor_tensor_scan(X2[:, b, c], ones, X1[:, b, c], 0.0, ALU.mult, ALU.add))
                by_chunk = lambda a: a.rearrange("p b (t n) -> p (b t) n", n=P)
                x2c = by_chunk(X2)
                mid = small[:, 0:8]
                link(nv.tensor_copy(mid, x2c[:, :, P // 2 - 1]))
                nv.tensor_tensor(x2c, x2c, mid.unsqueeze(2).broadcast_to([P, 8, P]), ALU.subtract).then_inc(cum_ready, 1)
                dve.wait_ge(cum_ready, 1)
                nv.tensor_tensor(X1, X2, X1, ALU.subtract).then_inc(cum_ready, 1)
                dve.wait_ge(kk_std, 1)
                link(nv.tensor_scalar(Y, Y, 1e-12, None, ALU.max))
                link(nv.reciprocal(Y, Y))
                link(nv.tensor_tensor(KK, KK, Y, ALU.mult))
                for b in range(HB):
                    link(nv.tensor_scalar(Y[:, b, :], AT[:, b, :], -1.0, par[:, PL_KA + b:PL_KA + b + 1], ALU.add, ALU.mult))
                link(nv.scalar_tensor_tensor(k, Y, 1.0, k, ALU.add, ALU.mult))
                link(nv.tensor_tensor(AT, KK, AT, ALU.mult))
                dve.wait_ge(exps_ready, 4)
                arv = AR.rearrange("p b t s n -> p (b t) s n")
                link(nv.tensor_tensor(arv[:, :, 1, :], by_chunk(r), by_chunk(X3), ALU.mult))
                link(nv.scalar_tensor_tensor(arv[:, :, 0, :], by_chunk(KK), -1.0, by_chunk(X1), ALU.mult, ALU.mult))
                link(nv.tensor_tensor(AT, AT, X2, ALU.mult))
                link(nv.tensor_tensor(SC, X3[:, :, P - 1], MIDE, ALU.mult))
                nv.tensor_tensor(KK, k, X2, ALU.mult).then_inc(gram_in, 1)
                for b in range(HB):
                    ins = nv.scalar_tensor_tensor(Y[:, b, :], r[:, b, :], par[:, PL_RK + b:PL_RK + b + 1], k[:, b, :], ALU.mult, ALU.mult)
                    if b < HB - 1:
                        link(ins)
                ins.then_inc(bonus_in, 1)
                dve.wait_ge(bonus_ss, 1)
                nv.tensor_tensor(r, banks(2, 2, HB, T), v, ALU.mult).then_inc(bonus_out, 1)

            def rwkv_chunk(t):
                dve.wait_ge(gm_zero, 1)
                dve.wait_ge(gram_in, 1)
                if t:
                    dve.wait_ge(y_ready, 1)
                    dve.wait_ge(s_ready, 1)
                else:
                    dve.wait_ge(bonus_in, 1)
                nv.tensor_copy(QT.rearrange("p h s n -> p (h s) n"), ident.unsqueeze(1).broadcast_to([P, 2 * HEADS, P])).then_inc(qt_ready, 1)
                mask = con[:, C_GRAM:C_GRAM + 512].bitcast(U32)
                for h in range(HEADS):
                    dve.wait_ge(gram_ready, 8 * t + h + 1)
                    nv.copy_predicated(GM[:, h, :], mask, PS[:, 2 + h % 2 + 2 * (h // 2 % 2), :]).then_inc(gram_taken, 1)
                dve.wait_ge(qt_ready, t * (2 * LEVELS + 1) + 1)
                for lev in range(LEVELS):
                    lm = con[:, C_LVL + P * lev:C_LVL + P * (lev + 1)]
                    for half in range(2):
                        i = (t * LEVELS + lev) * 2 + half
                        u = slice(4 * half, 4 * half + 4)
                        dve.wait_ge(w1_ready, i + 1)
                        nv.tensor_tensor(W1S[:, u, :], banks(6 + half, 1, 4, P), lm.unsqueeze(1).broadcast_to([P, 4, P]), ALU.mult)\
                            .then_inc(w1_masked, 1)
                    for half in range(2):
                        i = (t * LEVELS + lev) * 2 + half
                        u = slice(4 * half, 4 * half + 4)
                        dve.wait_ge(dq_ready, i + 1)
                        q = QT[:, u, :, :].rearrange("p a b c -> p (a b c)")
                        nv.tensor_tensor(q, q, banks(2 + 2 * half, 2), ALU.add).then_inc(qt_ready, 1)
                if t == 0:
                    dve.wait_ge(s_ready, 1)
                    nv.tensor_tensor(ST, banks(5, 1, HB, HD), SC.unsqueeze(2).broadcast_to([P, HB, HD]), ALU.mult).then_inc(st_ready, 1)

            def rwkv_norm():
                dve.wait_ge(ln_ss, 1)
                dve.wait_ge(y_out, 2)
                link(nv.scalar_tensor_tensor(Y, banks(4, 2, HB, T), -1.0 / HD, Y, ALU.mult, ALU.add))
                nv.tensor_tensor(X1, Y, Y, ALU.mult).then_inc(ln_in, 1)
                dve.wait_ge(ln_std, 1)
                link(nv.reciprocal(X2, X2))
                link(nv.tensor_tensor(Y, Y, X2, ALU.mult))
                for b in range(HB):
                    link(nv.tensor_scalar(Y[:, b, :], Y[:, b, :], par[:, PL_LG + b:PL_LG + b + 1], par[:, PL_LB + b:PL_LB + b + 1],
                                          ALU.mult, ALU.add))
                link(nv.tensor_tensor(Y, Y, r, ALU.add))
                nv.tensor_tensor(Y, Y, GT, ALU.mult).then_inc(ob_ready, 1)

            def attention():
                q, kk = proj[:, B_AQ:B_AQ + HB, :], proj[:, B_AK, :]
                dve.wait_ge(y_ready, 2)
                dve.wait_ge(act_taken, 10)
                nv.tensor_tensor(ATS[:, 0:HB, :], q, q, ALU.mult).then_inc(att_sq, 1)
                nv.tensor_tensor(ATS[:, HB, :], kk, kk, ALU.mult).then_inc(att_sq, 1)
                dve.wait_ge(att_std, 2)
                link(nv.reciprocal(ATS, ATS))
                nv.scalar_tensor_tensor(q, q, par[:, PL_QN:PL_QN + 1], ATS[:, 0:HB, :], ALU.mult, ALU.mult).then_inc(att_qk, 1)
                nv.scalar_tensor_tensor(kk, kk, par[:, PL_KN:PL_KN + 1], ATS[:, HB, :], ALU.mult, ALU.mult).then_inc(att_qk, 1)
                at = 0
                for rnd, (t, heads) in enumerate(ROUNDS):
                    n, w = len(heads), P * (t + 1)
                    s = SCO.rearrange("p (a b) -> p a b", b=w)
                    wide = lambda a: a[:, 0:n].unsqueeze(2).broadcast_to([P, n, w])
                    mask = con[:, C_BAND:C_BAND + w] if t else con[:, C_CAUSAL:C_CAUSAL + P]
                    sink = par[:, PL_SINK + at:PL_SINK + at + n]
                    at += n
                    dve.wait_ge(sc_ready, rnd + 1)
                    if rnd:
                        dve.wait_ge(pt_ready, rnd)
                    link(nv.scalar_tensor_tensor(s, banks(2, 2, n, w), HD ** -0.5, mask.unsqueeze(1).broadcast_to([P, n, w]), ALU.mult, ALU.add))
                    link(nv.tensor_reduce(MX[:, 0:n], s, AX, ALU.max))
                    link(nv.tensor_tensor(MM[:, 0:n], MX[:, 0:n], sink, ALU.max))
                    link(nv.tensor_tensor(s, s, wide(MM), ALU.subtract))
                    nv.tensor_tensor(SK[:, 0:n], sink, MM[:, 0:n], ALU.subtract).then_inc(sc_max, 1)
                    dve.wait_ge(sc_exp, 2 * (rnd + 1))
                    link(nv.tensor_reduce(SUM[:, 0:n], s, AX, ALU.add))
                    link(nv.tensor_tensor(SUM[:, 0:n], SUM[:, 0:n], SK[:, 0:n], ALU.add))
                    link(nv.reciprocal(SUM[:, 0:n], SUM[:, 0:n]))
                    nv.tensor_tensor(s, s, wide(SUM), ALU.mult).then_inc(p_ready, 1)

            def retention():
                cos, sin = (con[:, c:c + T].unsqueeze(1).broadcast_to([P, HB, T]) for c in (C_COS, C_SIN))
                dve.wait_ge(act_taken, 18)
                for n, at in enumerate((B_RQ, B_RK)):
                    x = proj[:, at:at + HB, :]
                    dve.wait_ge(rot_ready, n + 1)
                    link(nv.tensor_tensor(XR, banks(2 + 2 * n, 2, HB, T), sin, ALU.mult))
                    link(nv.tensor_tensor(x, x, cos, ALU.mult))
                    ins = nv.tensor_tensor(x, x, XR, ALU.add)
                    ins.then_inc(rot_out, 1)
                    dve.wait_ge(rot_out, n + 1)
                dve.wait_ge(dec_loaded, 16)
                for h in range(HEADS):
                    dve.wait_ge(rs_ready, h + 1)
                    nv.tensor_tensor(SM[:, h, :], PS[:, 2 + h % 2 + 2 * (h // 2 % 2), 0:3 * P], DEC[:, h, :], ALU.mult).then_inc(rs_out, 1)
                o, g = proj[:, B_RQ:B_RQ + HB, :], proj[:, B_RG:B_RG + HB, :]
                dve.wait_ge(oc_out, 1)
                nv.tensor_tensor(XR, o, o, ALU.mult).then_inc(oc_sq, 1)
                dve.wait_ge(oc_std, 1)
                link(nv.reciprocal(XR, XR))
                link(nv.tensor_tensor(o, o, XR, ALU.mult))
                nv.tensor_tensor(o, o, g, ALU.mult).then_inc(oc_ready, 1)

            def mix(l):
                for br in range(3):
                    for i in range(4):
                        q = Q_MIX + 4 * br + i
                        gate = proj[:, B_GATE + KD * br + 2 * i:B_GATE + KD * br + 2 * i + 2, :]
                        out = hT[:, 2 * i:2 * i + 2, :]
                        dve.wait_ge(block_done, done(l, q))
                        ps = banks(q % 2, 1, 2, T)
                        if br == 0:
                            nv.tensor_tensor(out, ps, gate, ALU.mult).then_inc(dve_taken, 1)
                        else:
                            link(nv.tensor_tensor(gate, ps, gate, ALU.mult))
                            if i == 0:
                                dve.wait_ge(dve_taken, 4 * br)
                            nv.tensor_tensor(out, out, gate, ALU.add).then_inc(dve_taken, 1)

            def residual(l, q0, n, blocks, base):
                for i in range(n):
                    dve.wait_ge(block_done, done(l, q0 + i))
                    x = xT[:, blocks * i:blocks * (i + 1), :]
                    nv.tensor_tensor(x, x, banks((q0 + i) % 2, 1, blocks, T), ALU.add).then_inc(dve_taken, 1)
                dve.wait_ge(dve_taken, base + n)

            def ffn(l):
                for n in range(N_FFN // 2):
                    dve.wait_ge(block_done, done(l, Q_FFN + 2 * n + 1))
                    dve.wait_ge(act_taken, N_PROJ + n + 1)
                    nv.tensor_tensor(HID[:, 2 * n:2 * n + 2, :], banks(1, 1, 2, T), SILU[:, n % 2, :].rearrange("p (a b) -> p a b", b=T),
                                     ALU.mult).then_inc(dve_taken, 1)

            dve.wait_ge(const_loaded, 32)
            dve.wait_ge(cond_loaded, 5 * 16)
            dve.wait_ge(block_done, ADA_BLOCKS)
            for j in range(4):
                nv.tensor_tensor(MROW[32 * j:32 * j + 1, :, :], PS[32 * j:32 * j + 1, 2:5, :], BROW[32 * j:32 * j + 1, :, :], ALU.add)\
                    .then_inc(mod_rows, 1)
            dve.wait_ge(mod_cols, 1)
            for j in range(4):
                by_group = lambda a: a.rearrange("p (b j i) -> p j b i", j=4, i=4)[:, j]
                nv.tensor_copy(by_group(mod[:, :]), by_group(PS[:, 4 + j, 0:48])).then_inc(mod_ready, 1)
            dve.wait_ge(mod_ready, 4)
            with dve.Fori(0, LAYERS) as l:
                dve.wait_ge(par_loaded, 32)
                norm(1, PL_G1)
                rwkv_mix()
                rwkv_prep()
                rwkv_chunk(0)
                rwkv_chunk(1)
                rwkv_norm()
                attention()
                retention()
                mix(l)
                residual(l, Q_OUT, N_OUT, 2, N_MIX)
                norm(2, PL_G2)
                ffn(l)
                residual(l, Q_DOWN, N_DOWN, 1, N_MIX + N_OUT + N_FFN // 2)
                dve.sem_inc(layer_fin, 1)
                dve.wait_ge(layer_go, l + 1)
                dve.sem_inc(layer_joined, 1)
            second_vector(dve)


_NATURAL = ["w_ada_2", "b_ada_2", "w_in", "w_attn_o", "w_rwkv_o", "w_ret_o", "w_out", "w_ffn_gate", "w_ffn_up", "w_ffn_down",
            "w_in_2", "w_out_2", "hy_w1_2", "hy_w2_2", "hy_w3_2", "hy_deltas_2", "w_gate_2", "w_up_2", "w_down_2"]


def kernel(**inputs):
    import concourse.bacc as bacc
    from concourse.bass_utils import run_bass_kernel_spmd

    a = {n: np.asarray(v) for n, v in inputs.items()}
    arrays = {n: np.ascontiguousarray(a[n]) for n in _NATURAL}
    blocks = lambda m: np.ascontiguousarray(m.reshape(KD, P, -1).transpose(1, 0, 2))
    arrays["xT"] = blocks(a["x"][0].T)
    arrays["cT"] = np.ascontiguousarray(a["c_2"].reshape(KD, P).T)
    arrays["router"] = blocks(a["w_router_2"][0])
    arrays["layer_params"] = np.stack([pack_layer(a, l) for l in range(LAYERS)])
    arrays["layer_lora"] = np.stack([pack_lora(a, l) for l in range(LAYERS)])
    arrays["params_2"] = pack_second(a)
    arrays["constants"], arrays["decay"] = layer_constants()
    arrays["constants_2"] = second_constants()

    nc = bacc.Bacc("TRN2", target_bir_lowering=False, num_devices=1)
    io = {}
    for n, v in arrays.items():
        v = arrays[n] = np.ascontiguousarray(v)
        io[n] = nc.dram_tensor(f"in_{n}", v.shape, mybir.dt.from_np(v.dtype), kind="ExternalInput").ap()
    io["yT"] = nc.dram_tensor("out_yT", (D, T), F32, kind="ExternalOutput").ap()
    build(nc, io)
    r = run_bass_kernel_spmd(nc, [{f"in_{n}": v for n, v in arrays.items()}], core_ids=[0])
    return np.ascontiguousarray(r.results[0]["out_yT"].T)[None]
```

```python
import math
from contextlib import ExitStack

import numpy as np

import concourse.bass as bass
import concourse.mybir as mybir
from concourse.alu_op_type import AluOpType as ALU

F32 = mybir.dt.float32
U32 = mybir.dt.uint32
ACT = mybir.ActivationFunctionType
AX = mybir.AxisListType.X

P = 128
T = 256
TT = T // P
D = 1024
KD = D // P
LAYERS = 2
HD = 64
HEADS = 8
HB = HEADS * HD // P
F_FF = 2816
FB = F_FF // P
W_IN = 7680
EPS = 1e-6
LNX_EPS = 64e-5
KAPPA = math.exp(-0.5)
NEG = -1e30

QKV, RW, RET0, GATE0 = 0, 768, 2560, 4608
IN_ORDER = [512, 1024, 1536, 2048, 0] + list(range(2560, W_IN, 512))
B_AK, B_AV, B_R, B_K, B_V, B_LORA, B_GD, B_AQ, B_RQ, B_RK, B_RV, B_RG, B_GATE = (
    0, 1, 2, 6, 10, 14, 15, 16, 20, 24, 28, 32, 36)
RW_BLOCKS = 14

H2, DH2 = 4, 128
EXPERTS, CAP, F_E = 16, 32, 2048
IN2 = 3600

RING, SLOT = 3, 4096
LAYER_SLOTS, TWO_SLOTS, EXPERT_SLOTS = 45, 12, 12
START, TWO_BLOCKS = RING, 20
N_PROJ, N_ADA, N_MIX, N_OUT, N_FFN, N_DOWN = 30, 6, 12, 4, 22, 8
Q_ADA = [30, 31, 32, 33, 36, 37]
Q_COLS = 38
Q_MIX = [[34, 35, 39, 40], [41, 42, 43, 44], [45, 46, 47, 48]]
Q_OUT = N_PROJ + N_ADA + 1 + N_MIX
Q_FFN = Q_OUT + N_OUT
Q_DOWN = Q_FFN + N_FFN
LAYER_BLOCKS = Q_DOWN + N_DOWN
S_ADA, S_MIX, S_OUT, S_FFN, S_DOWN = [15, 16, 17, 18, 20, 21], [19, 22, 23], 24, 26, 37
SLOT_DONE = [0] * LAYER_SLOTS
for _n in range(15):
    SLOT_DONE[_n] = 2 * _n + 2
for _s, _q in list(zip(S_ADA, Q_ADA)) + [(_s, _q[-1]) for _s, _q in zip(S_MIX, Q_MIX)]:
    SLOT_DONE[_s] = _q + 1
for _n in range(N_OUT // 2):
    SLOT_DONE[S_OUT + _n] = Q_OUT + 2 * _n + 2
for _n in range(N_FFN // 2):
    SLOT_DONE[S_FFN + _n] = Q_FFN + 2 * _n + 2
for _n in range(N_DOWN):
    SLOT_DONE[S_DOWN + _n] = Q_DOWN + _n + 1
BY_ACT = [q < N_PROJ or (Q_FFN <= q < Q_DOWN and (q - Q_FFN) % 2 == 0) for q in range(LAYER_BLOCKS)]
TAKEN = [sum(b == BY_ACT[q] for b in BY_ACT[:q + 1]) for q in range(LAYER_BLOCKS)]
ADA_AT = [{2: 0, 3: 1, 4: 2, 6: 3}, {1: 4, 4: 5}]
COLS_AT = [None, 6]

C_ID, C_ONES, C_BD, C_PERM, C_DUP, C_COS, C_SIN = 0, 128, 256, 384, 512, 768, 1024
C_LVL = 1280
LEVELS = 7
C_GRAM = C_LVL + LEVELS * P
C_CAUSAL = C_GRAM + 512
C_BAND = C_CAUSAL + P
C_SEL = C_BAND + 2 * P
C_N = C_SEL + N_ADA
PL_G1, PL_G2, PL_QN, PL_KN, PL_MU, PL_W0, PL_A0, PL_KK, PL_KA, PL_RK, PL_LG, PL_LB, PL_SINK = (
    0, 8, 16, 17, 18, 32, 36, 40, 44, 48, 52, 56, 60)
PL_N = PL_SINK + 16
D_CS, D_CI, D_MASK, D_IOTA, D_Z, D_SEL, D_TOK, D_NT = 0, 1024, 2048, 3072, 3328, 3584, 4096, 4098
D_N = 4100
P2_GMIX, P2_GFFN, P2_GFIN, P2_BIN, P2_BG, P2_CQW, P2_CQB, P2_CHW, P2_CHB, P2_MN, P2_HBIAS, P2_HN, P2_HY = (
    0, 8, 16, 24, 52, 56, 80, 88, 124, 136, 140, 148, 152)
P2_N = 155

BESIDE_SOFTMAX = [(22, 24), (25, 26), (27, 28)]
BESIDE_COPY = [(24, 25), (26, 27), (28, 29)]

ROUNDS = [(0, [0, 2, 4, 6, 1, 3, 5, 7]), (1, [0, 2, 1, 3]), (1, [4, 6, 5, 7])]


def layer_constants():
    c = np.zeros((P, C_N), np.float32)
    p, f = np.arange(P)[:, None], np.arange(P)[None, :]
    c[:, C_ID:C_ID + P] = p == f
    c[:, C_ONES:C_ONES + P] = 1
    c[:, C_BD:C_BD + P] = p // HD == f // HD
    half = HD // 2
    same = p // HD == f // HD
    c[:, C_PERM:C_PERM + P] = np.where(same & (p == f + half), -1.0, 0) + np.where(same & (p == f - half), 1.0, 0)
    for kv in range(2):
        c[:, C_DUP + kv * P:C_DUP + (kv + 1) * P] = p == kv * HD + f % HD
    inv = (1.0 / (np.float32(10000.0) ** (np.arange(half, dtype=np.float32) * np.float32(2.0) / HD))).astype(np.float32)
    ang = np.arange(T, dtype=np.float32)[None, :] * inv[:, None]
    c[:, C_COS:C_COS + T] = np.tile(np.cos(ang), (P // half, 1))
    c[:, C_SIN:C_SIN + T] = np.tile(np.sin(ang), (P // half, 1))
    for n in range(LEVELS):
        m = 1 << n
        c[:, C_LVL + n * P:C_LVL + (n + 1) * P] = (p // (2 * m) == f // (2 * m)) & (p // m % 2 == 0) & (f // m % 2 == 1)
    for n, keep in enumerate([p > f, p <= f, p < f, p <= f]):
        c[:, C_GRAM + n * P:C_GRAM + (n + 1) * P] = keep
    c[:, C_CAUSAL:C_CAUSAL + P] = np.where(f <= p, 0, NEG)
    c[:, C_BAND:C_BAND + P] = np.where(f > p, 0, NEG)
    c[:, C_BAND + P:C_BAND + 2 * P] = np.where(f <= p, 0, NEG)
    c[:, C_SEL:C_SEL + N_ADA] = p % 32 == np.arange(N_ADA)[None, :]
    gamma = np.log1p(-np.power(2.0, -5.0 - np.arange(HEADS, dtype=np.float64)))[None, :, None]
    diff = np.arange(T)[None, None, :] - np.arange(P)[:, None, None]
    dec = np.where(diff >= 0, np.exp(gamma * np.maximum(diff, 0)), 0) * HD ** -0.5
    decay = np.concatenate([dec, dec[:, :, :P]], axis=2).astype(np.float32)
    return c, decay.reshape(P, HEADS * 3 * P)


def second_constants():
    c = np.zeros((P, D_N), np.float32)
    t, k = np.arange(T, dtype=np.float64), np.arange(T, dtype=np.float64) + 0.5
    ang = 2 * np.pi * t[:, None] * k[None, :] / (2 * T)
    fwd = np.stack([np.cos(ang), np.sin(ang)], axis=1)
    c[:, D_CS:D_CS + 1024] = fwd.reshape(TT, P, 512).transpose(1, 0, 2).reshape(P, 1024)
    inv = np.stack([np.cos(ang.T), np.sin(ang.T)], axis=1) / T
    c[:, D_CI:D_CI + 1024] = inv.reshape(TT, P, 512).transpose(1, 0, 2).reshape(P, 1024)
    s, q = np.arange(T)[:, None], np.arange(T)[None, :]
    masks = np.stack([s <= q, s >= q], axis=1).astype(np.float32)
    c[:, D_MASK:D_MASK + 1024] = masks.reshape(TT, P, 2, T).transpose(1, 2, 0, 3).reshape(P, 1024)
    c[:, D_IOTA:D_IOTA + T] = np.arange(T)
    f32 = np.float32
    tl = np.linspace(0.0, 1.0, T, dtype=f32)[:, None]
    w = (f32(2.0 * math.pi) * np.arange(T, dtype=f32)[:, None] / f32(T)).astype(f32)
    bands = np.linspace(1e-4, 15, 16, dtype=f32)[None, :]
    z = np.concatenate([tl, np.cos(bands * w), -np.sin(bands * w)], axis=-1)
    c[:33, D_Z:D_Z + T] = z.T
    for h in range(H2):
        c[h, D_SEL + h * P:D_SEL + (h + 1) * P] = 1
    c[:, D_TOK:D_TOK + TT] = np.arange(T).reshape(TT, P).T
    c[:, D_NT:D_NT + TT] = -tl[:, 0].reshape(TT, P).T
    return c


def columns(v):
    return np.ascontiguousarray(v).reshape(-1, P).T


def pack_layer(a, l):
    dup = lambda g: np.concatenate([g, g])[:, None]
    order = [h for _, heads in ROUNDS for h in heads]
    parts = [columns(a["norm1_g"][l]), columns(a["norm2_g"][l]), dup(a["attn_q_norm_g"][l]), dup(a["attn_k_norm_g"][l]),
             columns(a["rwkv_shift_mu"][l]), columns(a["rwkv_w0"][l]), columns(a["rwkv_a0"][l]), columns(a["rwkv_k_k"][l]),
             columns(a["rwkv_k_a"][l]), columns(a["rwkv_r_k"][l]), columns(a["rwkv_lnx_g"][l]), columns(a["rwkv_lnx_b"][l]),
             np.broadcast_to(a["attn_sinks"][l][order][None, :], (P, 16))]
    return np.concatenate(parts, axis=1)


def pack_lora(a, l):
    return np.concatenate([np.concatenate([a["rwkv_w2"][l], a["rwkv_a2"][l]], axis=0), a["rwkv_g2"][l]], axis=1)


def pack_second(a):
    rows = lambda v: np.concatenate([v, np.zeros((P - v.shape[0],) + v.shape[1:], v.dtype)], axis=0)
    b = a["b_in_2"][0]
    bias = np.concatenate([b[:2048], b[2064:]])
    parts = [columns(a["g_mix_2"][0]), columns(a["g_ffn_2"][0]), columns(a["g_final_2"]), columns(bias),
             rows(b[2048:2064].reshape(4, H2).T),
             columns(a["conv_qk_w_2"][0]), columns(a["conv_qk_b_2"][0]), columns(a["conv_hy_w_2"][0]), columns(a["conv_hy_b_2"][0]),
             columns(a["mlstm_norm_g_2"][0]), columns(a["hy_bias_2"][0]), columns(a["hyena_norm_g_2"][0]),
             rows(a["hy_b1_2"][0][:, None]), rows(a["hy_b2_2"][0][:, None]), rows(a["hy_freq_2"][0][:, None])]
    return np.concatenate(parts, axis=1)


def build(nc, io):
    ctx = ExitStack()
    with ctx:
        def sb(name, shape):
            return ctx.enter_context(nc.sbuf_tensor(name, shape, F32))

        def sem(name):
            return ctx.enter_context(nc.semaphore(name))

        ring = sb("ring", [P, RING, SLOT])
        xT = sb("xT", [P, KD, T])
        hT = sb("hT", [P, KD, T])
        con = sb("con", [P, C_N])
        par = sb("par", [P, PL_N])
        lora = sb("lora", [P, 1024])
        proj = sb("proj", [P, 60, T])
        work = sb("work", [P, 16640])
        small = sb("small", [P, 64])
        cond = sb("cond", [P, KD, 64])
        mod = sb("mod", [P, 48])
        bias = sb("bias", [P, 4])
        PS = ctx.enter_context(nc.psum_tensor("PS", [P, 8, 512], F32))

        def w_(at, *dims):
            n = 1
            for d in dims:
                n *= d
            v = work[:, at:at + n]
            if len(dims) == 2:
                v = v.rearrange("p (a b) -> p a b", b=dims[1])
            if len(dims) == 3:
                v = v.rearrange("p (a b c) -> p a b c", b=dims[1], c=dims[2])
            if len(dims) == 4:
                v = v.rearrange("p (a b c d) -> p a b c d", b=dims[1], c=dims[2], d=dims[3])
            return v

        def banks(at, n, *dims):
            v = PS[:, at:at + n, :].rearrange("p a b -> p (a b)")
            if dims:
                m = 1
                for d in dims:
                    m *= d
                v = v[:, 0:m]
            if len(dims) == 2:
                v = v.rearrange("p (a b) -> p a b", b=dims[1])
            if len(dims) == 3:
                v = v.rearrange("p (a b c) -> p a b c", b=dims[1], c=dims[2])
            return v

        ident, ones, bd = con[:, C_ID:C_ID + P], con[:, C_ONES:C_ONES + P], con[:, C_BD:C_BD + P]
        perm = con[:, C_PERM:C_PERM + P]
        epsc, lnxc, onec = bias[:, 0:1], bias[:, 1:2], bias[:, 2:3]

        X1, X2, X3 = (w_(n * 1024, HB, T) for n in range(3))
        QT, W1S = w_(0, HEADS, 2, P), w_(2048, HEADS, P)
        KK, AT = w_(3072, HB, T), w_(4096, HB, T)
        AR = w_(5120, HB, TT, 2, P)
        GT, Y = w_(7168, HB, T), w_(8192, HB, T)
        GM = w_(9216, HEADS, 4 * P)
        SHIFT = w_(9216, RW_BLOCKS, T)
        VTOK, BKT = w_(13312, TT, 512), w_(14336, 2, 512)
        RHS, U, ST = w_(2048, HEADS, HD), w_(2560, HEADS, HD), w_(15872, HB, HD)
        MID, SC, MIDE = small[:, 0:8].rearrange("p (a b) -> p a b", b=TT), small[:, 8:12], small[:, 12:16]
        MX, MM, SK, SUM = small[:, 16:24], small[:, 24:32], small[:, 32:40], small[:, 40:48]
        ATS, SCO, PT = w_(9216, 5, T), w_(9216 + 1280, 1024), w_(9216 + 2304, HEADS, P)
        KDUP, VATT = w_(9216 + 3328, 2, T), w_(9216 + 3840, TT, P)
        DEC, SM = w_(9216, HEADS, 3 * P), w_(3072, HEADS, 3 * P)
        VRET, XR = w_(13312, TT, 512), w_(14336, HB, T)
        SQ, STD, RSTD = w_(5120, KD, T), w_(0, T), w_(256, T)
        HID = proj[:, 0:FB, :]
        SILU = proj[:, 24:28, :].rearrange("p a b -> p (a b)").rearrange("p (a b) -> p a b", b=512)
        mod_rows = w_(15360, 512)
        MOD2 = mod[:, :].rearrange("p (l b n) -> p l n b", l=LAYERS, n=4)

        ring_full = [sem(f"ring_full{n}") for n in range(RING)]
        block_done = sem("block_done")
        const_loaded = sem("const_loaded")
        bias_set, slot_freed = sem("bias_set"), sem("slot_freed")
        layer_go, layer_joined = sem("layer_go"), sem("layer_joined")

        names = """par_loaded sq_ready ss_ready std_ready h_ready act_taken dve_taken
            z_ready lora_in lora_done lora_out kk_sq kk_ss kk_std cum_ready exps_ready gram_in bonus_in bonus_ss
            bonus_out tok_ready tok_out gm_zero gram_ready gram_taken qt_ready w1_ready w1_masked dq_ready
            rhs_ready rhs_out u_ready u_out y_ready y_out s_ready st_ready ln_in ln_ss ln_std ob_ready
            att_sq att_ss att_std att_qk att_tr att_kv sc_ready sc_max sc_exp p_ready pt_ready pt_out oa_ready oa_out
            rot_ready rot_out vr_ready vr_out dec_loaded rs_ready rs_out oc_psum oc_out oc_sq oc_ss oc_std oc_ready
            vec_order layer_fin""".split()
        L = {n: sem(n) for n in names}
        (par_loaded, sq_ready, ss_ready, std_ready, h_ready, act_taken, dve_taken,
         z_ready, lora_in, lora_done, lora_out, kk_sq, kk_ss, kk_std, cum_ready, exps_ready, gram_in, bonus_in, bonus_ss,
         bonus_out, tok_ready, tok_out, gm_zero, gram_ready, gram_taken, qt_ready, w1_ready, w1_masked, dq_ready,
         rhs_ready, rhs_out, u_ready, u_out, y_ready, y_out, s_ready, st_ready, ln_in, ln_ss, ln_std, ob_ready,
         att_sq, att_ss, att_std, att_qk, att_tr, att_kv, sc_ready, sc_max, sc_exp, p_ready, pt_ready, pt_out, oa_ready, oa_out,
         rot_ready, rot_out, vr_ready, vr_out, dec_loaded, rs_ready, rs_out, oc_psum, oc_out, oc_sq, oc_ss, oc_std, oc_ready,
         vec_order, layer_fin) = (L[n] for n in names)
        layer_sems = range(par_loaded.num, layer_fin.num + 1)
        assert sorted(s.num for s in L.values()) == list(layer_sems)

        def done(l, q):
            return START + LAYER_BLOCKS * l + q + 1

        def full(l, n):
            return 32 * (LAYER_SLOTS // RING * l + n // RING + 1)

        def hrow(h):
            return slice(HD * (h % 2), HD * (h % 2) + HD)

        c2 = w_(12288, D_N)
        p2 = lora[:, 0:P2_N]
        wrt = lora[:, 256:384].rearrange("p (k e) -> p k e", e=EXPERTS)
        hyw1, hyw2 = lora[0:33, 384:448], lora[0:64, 448:512]
        ARG, TRN = lora[0:64, 512:768], lora[0:64, 768:1024]
        CS, CI = (c2[:, c:c + 1024].rearrange("p (a s n) -> p a s n", s=2, n=T) for c in (D_CS, D_CI))
        MASK2 = c2[:, D_MASK:D_MASK + 1024]
        FILT, KF = w_(0, TT, 4, 512), w_(4096, TT, 2, 2, 512)
        HYW3, DELTA = w_(8192, 2048), w_(10240, 2048)
        YF = w_(10240, TT, 2, 512)
        TMP1, TMP2 = w_(8192, 512), w_(8704, 512)
        WIN = proj[:, 56:60, :].rearrange("p a b -> p (a b)").rearrange("p (a b) -> p a b", b=512)
        ZTOK = WIN
        E2, EMS, NUM = w_(0, 2, TT, T), w_(1024, 2, T), w_(1536, 2, T)
        HS2, LF, BB = w_(2048, H2, T), w_(3072, 2, T), w_(3584, 2, T)
        VT2 = proj[:, 48:52, :].rearrange("p a b -> p (a b)").rearrange("p (a b) -> p a b", b=512)
        G4 = proj[:, 52:56, :]
        AA, NM, EMR, ZER = (proj[:, b:b + 2, :] for b in (0, 2, 4, 6))
        ACOL = small[:, 0:16].rearrange("p (d t h) -> p d t h", t=TT, h=H2)
        gs1, gs2 = small[:, 16:24], small[:, 24:32]
        QK2, HX2 = proj[:, 28:36, :], proj[:, 36:48, :]
        HTOK = proj[:, 0:8, :].rearrange("p a b -> p (a b)").rearrange("p (a b) -> p a b", b=D)
        XS = proj[:, 8:24, :].rearrange("p e (k s) -> p e k s", s=CAP)
        XSE = proj[:, 24, :].rearrange("p (k s) -> p k s", s=CAP)
        PICK = proj[:, 25:29, :].rearrange("p a b -> p (a b)").rearrange("p (a b) -> p a b", b=512)
        GE = proj[:, 29, :]
        flat = lambda a: proj[:, a:a + 2, :].rearrange("p a b -> p (a b)")
        HSE, HE, HTE, YE = flat(32), flat(34), flat(36), flat(38)
        AFF = proj[0:EXPERTS, 40, :]
        DIAG = flat(42)
        LOG = proj[:, 44, 0:32].rearrange("p (t e) -> p t e", e=EXPERTS)
        VAL, IDXU, IDXF = proj[0:EXPERTS, 45, 0:32], proj[0:EXPERTS, 45, 32:64], proj[0:EXPERTS, 45, 64:96]
        REP = proj[0:EXPERTS, 46, :].rearrange("p (a r s) -> p a r s", r=4, s=CAP)
        IG = proj[:, 47, 0:32].rearrange("p (a e) -> p a e", e=EXPERTS)
        ST4 = proj[:, 47, 32:64]
        ZERO = proj[:, 48, 0:P]

        SQ2, STD2, RSTD2 = proj[:, 48:56, :], proj[:, 40, :], proj[:, 41, :]
        E2F = w_(0, 4, T)

        names2 = """two_loaded f_hid f_arg f_sin f_abs f_win f_h f_filt f_sum kf_ready kf_out
            sq2 ss2 std2 h2_ready act2 dve2 conv_ready conv_act gate_rows abs_rows ln_rows rows_ready em_rows zero_set
            m_tr m_out m_s m_em m_emo m_arg m_exp m_w m_num m_h
            z_tr z_out u2_ready yf_ready yt_ready z_ready2 r_sq r_ss r_std cat_ready
            tok2 tok2_out rt_logit rt_max rt_exp rt_prob rt_tr topk_done ix_ready ix_out diag_ready row_ready pick_ready xs_psum xs_out
            expert_slots xs_staged ge_ready hs_ready he_ready ht_ready ht_out ye_ready scattered
            moe_sum zero_e vec2 out_done""".split()
        S = {n: sem(n) for n in names2}
        (two_loaded, f_hid, f_arg, f_sin, f_abs, f_win, f_h, f_filt, f_sum, kf_ready, kf_out,
         sq2, ss2, std2, h2_ready, act2, dve2, conv_ready, conv_act, gate_rows, abs_rows, ln_rows, rows_ready, em_rows, zero_set,
         m_tr, m_out, m_s, m_em, m_emo, m_arg, m_exp, m_w, m_num, m_h,
         z_tr, z_out, u2_ready, yf_ready, yt_ready, z_ready2, r_sq, r_ss, r_std, cat_ready,
         tok2, tok2_out, rt_logit, rt_max, rt_exp, rt_prob, rt_tr, topk_done, ix_ready, ix_out, diag_ready, row_ready, pick_ready, xs_psum, xs_out,
         expert_slots, xs_staged, ge_ready, hs_ready, he_ready, ht_ready, ht_out, ye_ready, scattered,
         moe_sum, zero_e, vec2, out_done) = (S[n] for n in names2)
        BASE2 = START + LAYERS * LAYER_BLOCKS
        FULL2 = 32 * LAYERS * LAYER_SLOTS // RING
        FULLE = FULL2 + 32 * TWO_SLOTS // RING
        IN2_ORDER = [(0, 512), (512, 512), (2048, 16), (1024, 512), (2064, 512), (2576, 512), (3088, 512), (1536, 512)]
        IN2_BLOCKS = [0, 4, None, 8, 16, 20, 24, 12]

        def second_sync(sp, load, by_rows):
            for n in range(TWO_SLOTS):
                if n < RING:
                    sp.wait_ge(block_done, BASE2 - (RING - 1 - n))
                else:
                    m = n - RING + 1
                    sp.wait_ge(block_done, BASE2 + (2 * m if m <= 8 else 16 + m - 8))
                s = n % RING
                if n < 8:
                    at, cols = IN2_ORDER[n]
                    by_rows(io["w_in_2"][0][:, at:at + cols], s, cols)
                else:
                    by_rows(io["w_out_2"][0][:, 256 * (n - 8):256 * (n - 7)], s, 256)
            sp.wait_ge(block_done, BASE2 + TWO_BLOCKS)
            with sp.Fori(0, EXPERTS) as e:
                for n in range(EXPERT_SLOTS):
                    s = n % RING
                    sp.wait_ge(expert_slots, EXPERT_SLOTS * e + EXPERT_SLOTS + n - RING + 1)
                    sp.sem_inc(slot_freed, 1)
                    if n < 8:
                        w = io[("w_gate_2", "w_up_2")[n // 4]][0][e]
                        rows, cols = 2 * P, F_E
                        w = w[rows * (n % 4):rows * (n % 4 + 1), :]
                    else:
                        cols = D
                        w = io["w_down_2"][0][e][4 * P * (n - 8):4 * P * (n - 7), :]
                    by_rows(w, s, cols)
            sp.wait_ge(h2_ready, 3)
            sp.dma_start(io["yT"].rearrange("(k p) t -> p k t", p=P), hT[:, :, :]).then_inc(out_done, 16)
            sp.wait_ge(out_done, 16)

        def second_pool(pool):
            pool.wait_ge(layer_go, LAYERS)

        def second_tensor(pe):
            nt = nc.tensor

            def norm_sums(n):
                pe.wait_ge(sq2, n)
                for k in range(KD):
                    mm = nt.matmul(PS[:, 2, 0:T], ones, SQ2[:, k, :], start=(k == 0), stop=(k == KD - 1))
                mm.then_inc(ss2, 1)

            def four_sums(bank, src, signal):
                for n in range(2):
                    mm = nt.matmul(PS[:, bank + n, :], ones, src[:, 2 * n:2 * n + 2, :].rearrange("p a b -> p (a b)"), start=True, stop=True)
                mm.then_inc(signal, 1)

            def product(q, weight, moving, kn, n_blocks=2, m=P):
                if q >= 2:
                    if q - 2 < 16:
                        pe.wait_ge(act2, q - 1)
                    else:
                        pe.wait_ge(dve2, q - 17)
                for b in range(n_blocks):
                    for k in range(kn):
                        mm = nt.matmul(PS[0:m, q % 2, T * b:T * (b + 1)], weight(b, k), moving(k), start=(k == 0), stop=(k == kn - 1))
                mm.then_inc(block_done, 1)

            def project(lo, hi):
                for q in range(lo, hi):
                    n, half = q // 2, q % 2
                    s, cols = n % RING, IN2_ORDER[n][1]
                    if half == 0:
                        pe.wait_ge(ring_full[s], FULL2 + 32 * (n // RING + 1))
                    m = cols // 4
                    product(q, lambda b, k: ring[:, s, cols * k + m * (2 * half + b):cols * k + m * (2 * half + b + 1)],
                            lambda k: hT[:, k, :], KD, 2, m)

            def filter_tiles(lo, hi):
                for i in range(lo, hi):
                    c, t = i // 2, i % 2
                    if i >= 2:
                        pe.wait_ge(f_filt, i - 1)
                    nt.matmul(PS[:, 4 + i % 2, :], ARG[:, P * t:P * (t + 1)], HYW3[0:64, 512 * c:512 * (c + 1)], start=True, stop=True)\
                        .then_inc(f_h, 1)

            def filter_spectra(lo, hi):
                for i in range(lo, hi):
                    o, s, kt = i // 4, i // 2 % 2, i % 2
                    if i >= 4:
                        pe.wait_ge(kf_out, i - 3)
                    for t in range(TT):
                        mm = nt.matmul(PS[:, 4 + i % 4, :], CS[:, t, s, P * kt:P * (kt + 1)], FILT[:, t, 2 * o + s, :], start=(t == 0), stop=(t == 1))
                    mm.then_inc(kf_ready, 1)

            def project_beside_filters():
                pe.wait_ge(two_loaded, 7 * 16)
                nt.matmul(PS[0:64, 3, 0:T], hyw1, c2[0:33, D_Z:D_Z + T], start=True, stop=True).then_inc(f_hid, 1)
                pe.wait_ge(h2_ready, 1)
                project(0, 1)
                pe.wait_ge(f_sin, 1)
                nt.matmul(PS[0:64, 3, T:2 * T], hyw2, ARG, start=True, stop=True).then_inc(f_hid, 1)
                project(1, 2)
                pe.wait_ge(f_sin, 2)
                for n in range(4):
                    filter_tiles(2 * n, 2 * n + 2)
                    project(2 + n, 3 + n)
                project(6, 7)
                pe.wait_ge(f_sum, 2)
                filter_spectra(0, 4)
                project(7, 8)
                filter_spectra(4, 8)

            def mlstm():
                pe.wait_ge(act2, 8)
                pe.wait_ge(kf_out, 8)
                for t in range(TT):
                    for b in range(H2):
                        mm = nt.transpose(PS[:, 6 + t, P * b:P * (b + 1)], proj[:, 8 + b, P * t:P * (t + 1)], ident)
                mm.then_inc(m_tr, 1)
                project(8, 9)
                pe.wait_ge(rows_ready, 2)
                for d in range(2):
                    for t in range(TT):
                        at = 4 * (2 * d + t)
                        mm = nt.transpose(PS[:, 5, at:at + 4], AA[0:H2, d, P * t:P * (t + 1)], ident[0:H2, 0:H2])
                mm.then_inc(m_tr, 1)
                pe.wait_ge(em_rows, 1)
                pe.wait_ge(conv_act, 1)
                pe.wait_ge(m_out, 3)
                for h in range(H2):
                    if h:
                        pe.wait_ge(m_h, h)
                    sel = c2[0:H2, D_SEL + P * h:D_SEL + P * (h + 1)]
                    nt.matmul(PS[:, 3, :], sel, NM[0:H2, :, :].rearrange("p a b -> p (a b)"), start=True, stop=True)
                    nt.matmul(PS[:, 4, :], sel, EMR[0:H2, :, :].rearrange("p a b -> p (a b)"), start=True, stop=True).then_inc(m_em, 1)
                    for j in range(TT):
                        mm = nt.matmul(PS[:, 2, T * j:T * (j + 1)], QK2[:, 4 + h, P * j:P * (j + 1)], QK2[:, h, :], start=True, stop=True)
                    mm.then_inc(m_s, 1)
                    project(9 + 2 * h, 10 + 2 * h)
                    pe.wait_ge(m_w, h + 1)
                    for d in range(2):
                        for j in range(TT):
                            nt.matmul(PS[:, 5, T * d:T * (d + 1)], VT2[:, j, P * h:P * (h + 1)], E2[:, d, j, :], start=(j == 0), stop=(j == 1))
                    for d in range(2):
                        for j in range(TT):
                            mm = nt.matmul(PS[:, 6, T * d:T * (d + 1)], ones, E2[:, d, j, :], start=(j == 0), stop=(j == 1))
                    mm.then_inc(m_num, 1)
                    if h < H2 - 1:
                        project(10 + 2 * h, 11 + 2 * h)
                pe.wait_ge(r_sq, 1)
                four_sums(2, E2F, r_ss)

            def hyena():
                pe.wait_ge(r_std, 1)
                for o in range(2):
                    if o:
                        pe.wait_ge(z_ready2, 1)
                    for t in range(TT):
                        for b in range(4):
                            mm = nt.transpose(PS[:, 6 + t, P * b:P * (b + 1)], HX2[:, 8 + b, P * t:P * (t + 1)], ident)
                    mm.then_inc(z_tr, 1)
                    pe.wait_ge(z_out, 2 * (o + 1))
                    for kt in range(TT):
                        for s in range(2):
                            for t in range(TT):
                                mm = nt.matmul(PS[:, 2 + 2 * kt + s, :], CS[:, t, s, P * kt:P * (kt + 1)], ZTOK[:, t, :], start=(t == 0), stop=(t == 1))
                    mm.then_inc(u2_ready, 1)
                    pe.wait_ge(yf_ready, o + 1)
                    for b in range(4):
                        for n in range(4):
                            mm = nt.matmul(PS[:, 6 + b // 2, T * (b % 2):T * (b % 2 + 1)], YF[:, n // 2, n % 2, P * b:P * (b + 1)],
                                           CI[:, n // 2, n % 2, :], start=(n == 0), stop=(n == 3))
                    mm.then_inc(yt_ready, 1)
                pe.wait_ge(r_sq, 2)
                four_sums(2, E2F, r_ss)

            def out():
                pe.wait_ge(cat_ready, 2)
                for n in range(4):
                    s = (8 + n) % RING
                    pe.wait_ge(ring_full[s], FULL2 + 32 * ((8 + n) // RING + 1))
                    product(16 + n, lambda b, k: ring[:, s, 256 * k + P * b:256 * k + P * (b + 1)], lambda k: hT[:, k, :], KD)

            def route():
                pe.wait_ge(h2_ready, 2)
                for t in range(TT):
                    for k in range(KD):
                        mm = nt.matmul(PS[:, 2, EXPERTS * t:EXPERTS * (t + 1)], hT[:, k, P * t:P * (t + 1)], wrt[:, k, :],
                                       start=(k == 0), stop=(k == KD - 1))
                mm.then_inc(rt_logit, 1)
                for i in range(4):
                    t, g = i // 2, i % 2
                    for b in range(4):
                        mm = nt.transpose(PS[:, 4 + i, P * b:P * (b + 1)], hT[:, 4 * g + b, P * t:P * (t + 1)], ident)
                    mm.then_inc(tok2, 1)
                pe.wait_ge(rt_prob, 1)
                for t in range(TT):
                    mm = nt.transpose(PS[0:EXPERTS, 3, P * t:P * (t + 1)], LOG[:, t, :], ident)
                mm.then_inc(rt_tr, 1)
                pe.wait_ge(topk_done, 1)
                for a in range(2):
                    mm = nt.matmul(PS[:, 2, EXPERTS * a:EXPERTS * (a + 1)], REP[:, a, :, :].rearrange("p a b -> p (a b)"),
                                   ident[0:EXPERTS, 0:EXPERTS], start=True, stop=True)
                mm.then_inc(ix_ready, 1)
                pe.wait_ge(diag_ready, 1)
                nt.matmul(PS[:, 3, :], ones[0:EXPERTS, :], DIAG[0:EXPERTS, :], start=True, stop=True).then_inc(row_ready, 1)
                pe.wait_ge(pick_ready, 1)
                pe.wait_ge(tok2_out, 4)
                for k in range(KD):
                    if k >= 4:
                        pe.wait_ge(xs_out, k - 3)
                    for t in range(TT):
                        mm = nt.matmul(PS[:, 4 + k % 4, :], HTOK[:, t, P * k:P * (k + 1)], PICK[:, t, :], start=(t == 0), stop=(t == 1))
                    mm.then_inc(xs_psum, 1)

            def experts():
                pe.wait_ge(xs_out, KD)
                pe.wait_ge(zero_e, 1)
                pe.wait_ge(dve2, 4)
                YB = [6, 7, 0, 1]
                for b in YB:
                    nt.matmul(PS[:, b, :], ZERO, con[:, 0:512], start=True, stop=False, skip_group_check=True)
                pe.sem_inc(expert_slots, EXPERT_SLOTS)
                pe.sem_inc(scattered, 1)
                with pe.Fori(0, EXPERTS) as e:
                    pe.wait_ge(xs_staged, e + 1)
                    for n in range(8):
                        s = n % RING
                        pe.wait_ge(ring_full[s], FULLE + 32 * (EXPERT_SLOTS // RING) * e + 32 * (n // RING + 1))
                        for kk in range(2):
                            k = 2 * (n % 4) + kk
                            for j in range(4):
                                mm = nt.matmul(PS[32 * j:32 * j + 32, 2 + n // 4, :], XSE[:, k, :],
                                               ring[:, s, F_E * kk + 512 * j:F_E * kk + 512 * (j + 1)], start=(k == 0), stop=(k == KD - 1))
                        mm.then_inc(expert_slots, 1)
                    pe.wait_ge(he_ready, e + 1)
                    for c in range(4):
                        mm = nt.transpose(PS[:, 4, P * c:P * (c + 1)], HE[:, P * c:P * (c + 1)], ident)
                    mm.then_inc(ht_ready, 1)
                    pe.wait_ge(ht_out, e + 1)
                    for n in range(8, 12):
                        s, d = n % RING, n - 8
                        pe.wait_ge(ring_full[s], FULLE + 32 * (EXPERT_SLOTS // RING) * e + 32 * (n // RING + 1))
                        for c in range(4):
                            for dh in range(2):
                                g = 2 * dh + c % 2
                                mm = nt.matmul(PS[32 * g:32 * g + 32, 5, :], HTE[:, P * c + 32 * d:P * c + 32 * (d + 1)],
                                               ring[:, s, D * c + 512 * dh:D * c + 512 * (dh + 1)],
                                               start=(d == 0 and c < 2), stop=(d == 3 and c >= 2))
                        mm.then_inc(expert_slots, 1)
                    pe.wait_ge(ye_ready, e + 1)
                    for b in range(KD):
                        o = slice(64 * (b // 4), 64 * (b // 4) + 64)
                        mm = nt.matmul(PS[:, YB[b // 2], T * (b % 2):T * (b % 2 + 1)], YE[o, P * (b % 4):P * (b % 4 + 1)], GE[o, :],
                                       start=False, stop=False, skip_group_check=True)
                    mm.then_inc(scattered, 1)

            norm_sums(1)
            project_beside_filters()
            mlstm()
            hyena()
            out()
            norm_sums(2)
            route()
            experts()
            norm_sums(3)

        def second_scalar(act):
            na = nc.scalar

            def root(n):
                act.wait_ge(ss2, n)
                na.activation(STD2, PS[:, 2, 0:T], ACT.Sqrt, bias=epsc, scale=1.0 / D).then_inc(std2, 1)

            def four_roots(n):
                act.wait_ge(r_ss, n)
                na.activation(E2F.rearrange("p a b -> p (a b)"), banks(2, 2), ACT.Sqrt, bias=epsc, scale=1.0 / P).then_inc(r_std, 1)

            act.dma_start(c2, io["constants_2"]).then_inc(two_loaded, 16)
            act.dma_start(p2, io["params_2"]).then_inc(two_loaded, 16)
            act.dma_start(wrt, io["router"]).then_inc(two_loaded, 16)
            act.dma_start(hyw1, io["hy_w1_2"][0]).then_inc(two_loaded, 16)
            act.dma_start(hyw2, io["hy_w2_2"][0]).then_inc(two_loaded, 16)
            act.dma_start(HYW3[0:64, :], io["hy_w3_2"][0]).then_inc(two_loaded, 16)
            act.dma_start(DELTA, io["hy_deltas_2"].partition_broadcast(P).rearrange("p o n -> p (o n)")).then_inc(two_loaded, 16)

            def proj_out(lo, hi):
                for q in range(lo, hi):
                    act.wait_ge(block_done, BASE2 + q + 1)
                    at = IN2_BLOCKS[q // 2]
                    for b in range(2):
                        if at is None:
                            n = 2 * (q % 2) + b
                            ins = na.activation(G4[0:H2, n, :], PS[0:H2, q % 2, T * b:T * (b + 1)], ACT.Identity,
                                                bias=p2[0:H2, P2_BG + n:P2_BG + n + 1])
                        else:
                            n = at + 2 * (q % 2) + b
                            ins = na.activation(proj[:, n, :], PS[:, q % 2, T * b:T * (b + 1)], ACT.Sigmoid if at == 12 else ACT.Identity,
                                                bias=p2[:, P2_BIN + n:P2_BIN + n + 1])
                    ins.then_inc(act2, 1)

            def filter_windows(lo, hi):
                for i in range(lo, hi):
                    c, t = i // 2, i % 2
                    if i >= 2:
                        act.wait_ge(f_filt, i - 1)
                    na.activation(WIN[:, i % 2, :], DELTA[:, 512 * c:512 * (c + 1)], ACT.Exp, scale=c2[:, D_NT + t:D_NT + t + 1]).then_inc(f_win, 1)

            def filter_spectra(lo, hi):
                for i in range(lo, hi):
                    o, s, kt = i // 4, i // 2 % 2, i % 2
                    act.wait_ge(kf_ready, i + 1)
                    na.activation(KF[:, kt, o, s, :], PS[:, 4 + i % 4, :], ACT.Copy).then_inc(kf_out, 1)

            root(1)
            act.wait_ge(two_loaded, 7 * 16)
            for n in range(2):
                act.wait_ge(f_arg, n + 1)
                na.activation(ARG, ARG, ACT.Sin).then_inc(f_sin, 1)
                proj_out(n, n + 1)
            act.wait_ge(f_abs, 1)
            for n in range(4):
                filter_windows(2 * n, 2 * n + 2)
                proj_out(2 + n, 3 + n)
            proj_out(6, 7)
            filter_spectra(0, 4)
            proj_out(7, 8)
            filter_spectra(4, 8)
            act.wait_ge(conv_ready, 1)
            na.activation(QK2, QK2, ACT.Silu).then_inc(conv_act, 1)
            act.wait_ge(gate_rows, 1)
            na.activation(LF[0:H2], LF[0:H2], ACT.Exp, scale=-1.0).then_inc(abs_rows, 1)
            act.wait_ge(abs_rows, 1)
            na.activation(LF[0:H2], LF[0:H2], ACT.Ln, bias=onec[0:H2, :]).then_inc(ln_rows, 1)
            act.wait_ge(m_tr, 1)
            for t in range(TT):
                na.activation(VT2[:, t, :], PS[:, 6 + t, :], ACT.Copy).then_inc(m_out, 1)
            proj_out(8, 9)
            act.wait_ge(m_tr, 2)
            na.activation(small[:, 0:16], PS[:, 5, 0:16], ACT.Copy).then_inc(m_out, 1)
            act.wait_ge(rows_ready, 2)
            na.activation(EMR[0:H2], EMR[0:H2], ACT.Exp, scale=-1.0).then_inc(em_rows, 1)
            for h in range(H2):
                act.wait_ge(m_em, h + 1)
                na.activation(EMS.rearrange("p a b -> p (a b)"), PS[:, 4, :], ACT.Copy).then_inc(m_emo, 1)
                act.wait_ge(m_arg, h + 1)
                na.activation(E2, E2, ACT.Exp).then_inc(m_exp, 1)
                proj_out(9 + 2 * h, min(11 + 2 * h, 16))
            four_roots(1)
            for o in range(2):
                act.wait_ge(z_tr, o + 1)
                for t in range(TT):
                    na.activation(ZTOK[:, t, :], PS[:, 6 + t, :], ACT.Copy).then_inc(z_out, 1)
            four_roots(2)
            root(2)
            for i in range(4):
                t, g = i // 2, i % 2
                act.wait_ge(tok2, i + 1)
                na.activation(HTOK[:, t, 512 * g:512 * (g + 1)], PS[:, 4 + i, :], ACT.Copy).then_inc(tok2_out, 1)
            act.wait_ge(rt_max, 1)
            na.activation(LOG, LOG, ACT.Exp).then_inc(rt_exp, 1)
            act.wait_ge(ix_ready, 1)
            na.activation(IG.rearrange("p a b -> p (a b)"), PS[:, 2, 0:32], ACT.Copy).then_inc(ix_out, 1)
            for k in range(KD):
                act.wait_ge(xs_psum, k + 1)
                na.activation(XS[:, :, k, :], banks(4 + k % 4, 1, EXPERTS, CAP), ACT.Copy).then_inc(xs_out, 1)
            with act.Fori(0, EXPERTS) as e:
                act.wait_ge(expert_slots, EXPERT_SLOTS * e + EXPERT_SLOTS + 4)
                na.activation(HSE, PS[:, 2, :], ACT.Silu).then_inc(hs_ready, 1)
                act.wait_ge(ht_ready, e + 1)
                na.activation(HTE, PS[:, 4, :], ACT.Copy).then_inc(ht_out, 1)
            root(3)

        def second_vector(dve):
            nv = nc.vector
            count = [0]

            def link(ins):
                count[0] += 1
                ins.then_inc(vec2, 1)
                dve.wait_ge(vec2, count[0])

            def square(n):
                nv.tensor_tensor(SQ2, xT[:, :, :], xT[:, :, :], ALU.mult).then_inc(sq2, 1)
                if n == 1:
                    prepare()
                dve.wait_ge(std2, n)
                link(nv.reciprocal(RSTD2, STD2))

            def prepare():
                dve.wait_ge(two_loaded, 7 * 16)
                link(nv.scalar_tensor_tensor(gs1, mod[:, 8:16], 1.0, p2[:, P2_GMIX:P2_GMIX + KD], ALU.add, ALU.mult))
                link(nv.scalar_tensor_tensor(gs2, mod[:, 32:40], 1.0, p2[:, P2_GFFN:P2_GFFN + KD], ALU.add, ALU.mult))
                nv.scalar_tensor_tensor(DELTA, DELTA, -1.0, DELTA, ALU.mult, ALU.max).then_inc(f_abs, 1)
                sine_argument(0)

            def norm(n, gain, shift):
                square(n)
                for k in range(KD):
                    link(nv.scalar_tensor_tensor(hT[:, k, :], xT[:, k, :], gain[:, k:k + 1], RSTD2, ALU.mult, ALU.mult))
                    ins = nv.tensor_scalar(hT[:, k, :], hT[:, k, :], mod[:, shift + k:shift + k + 1], None, ALU.add)
                    if k < KD - 1:
                        link(ins)
                ins.then_inc(h2_ready, 1)

            def sine_argument(n):
                dve.wait_ge(f_hid, n + 1)
                link(nv.tensor_scalar(ARG, PS[0:64, 3, T * n:T * (n + 1)], p2[0:64, P2_HY + n:P2_HY + n + 1], p2[0:64, P2_HY + 2:P2_HY + 3], ALU.add, ALU.mult))
                big = 1.5 * 2.0 ** 23
                two_pi = 2 * math.pi
                c1 = 6.28125
                link(nv.tensor_scalar(TRN, ARG, 1 / two_pi, None, ALU.mult))
                link(nv.tensor_scalar(TRN, TRN, big, None, ALU.add))
                link(nv.tensor_scalar(TRN, TRN, -big, None, ALU.add))
                link(nv.scalar_tensor_tensor(ARG, TRN, -c1, ARG, ALU.mult, ALU.add))
                link(nv.scalar_tensor_tensor(ARG, TRN, -(two_pi - c1), ARG, ALU.mult, ALU.add))
                pi = float(np.nextafter(np.float32(math.pi), np.float32(0)))
                nv.tensor_scalar(ARG, ARG, pi, -pi, ALU.min, ALU.max).then_inc(f_arg, 1)

            def filters():
                sine_argument(1)
                for i in range(8):
                    c, t = i // 2, i % 2
                    dve.wait_ge(f_h, i + 1)
                    dve.wait_ge(f_win, i + 1)
                    nv.scalar_tensor_tensor(FILT[:, t, c, :], WIN[:, i % 2, :], 0.05, PS[:, 4 + i % 2, :], ALU.add, ALU.mult).then_inc(f_filt, 1)
                dve.wait_ge(f_filt, 8)
                for o in range(2):
                    f, b = FILT[:, :, 2 * o, :], FILT[:, :, 2 * o + 1, :]
                    link(nv.tensor_tensor(f, f, b, ALU.add))
                    nv.scalar_tensor_tensor(b, b, -2.0, f, ALU.mult, ALU.add).then_inc(f_sum, 1)

            def conv(dst, src, w, b, lo, hi, blocks):
                for i in range(lo, hi):
                    y, u = dst[:, i, :], proj[:, src + i, :]
                    tap = lambda j: p2[:, w + blocks * j + i:w + blocks * j + i + 1]
                    link(nv.tensor_scalar(y, u, tap(1), p2[:, b + i:b + i + 1], ALU.mult, ALU.add))
                    link(nv.scalar_tensor_tensor(y[:, 1:T], u[:, 0:T - 1], tap(0), y[:, 1:T], ALU.mult, ALU.add))
                    ins = nv.scalar_tensor_tensor(y[:, 0:T - 1], u[:, 1:T], tap(2), y[:, 0:T - 1], ALU.mult, ALU.add)
                    if src == 0 and i == hi - 1:
                        ins.then_inc(conv_ready, 1)
                    else:
                        link(ins)

            def mlstm():
                f = G4[0:H2, 1::2, :]
                i_ = G4[0:H2, 0::2, :]
                lf, bb, aa, nm, emr, zer = (a[0:H2] for a in (LF, BB, AA, NM, EMR, ZER))
                dve.wait_ge(act2, 6)
                conv(QK2, 0, P2_CQW, P2_CQB, 0, 8, 8)
                dve.wait_ge(kf_ready, 8)
                nv.scalar_tensor_tensor(lf, f, -1.0, f, ALU.mult, ALU.max).then_inc(gate_rows, 1)
                dve.wait_ge(conv_ready, 1)
                link(nv.memset(zer, 0.0))
                dve.wait_ge(ln_rows, 1)
                link(nv.scalar_tensor_tensor(lf, f, 0.0, lf, ALU.min, ALU.subtract))
                link(nv.tensor_tensor_scan(bb[:, 0, :], zer[:, 0, :], lf[:, 0, :], 0.0, ALU.add, ALU.add))
                link(nv.tensor_tensor_scan(bb[:, 1, ::-1], zer[:, 0, :], lf[:, 1, ::-1], 0.0, ALU.add, ALU.add))
                link(nv.tensor_tensor(aa, i_, bb, ALU.subtract))
                link(nv.tensor_tensor_scan(nm[:, 0, :], zer[:, 0, :], aa[:, 0, :], NEG, ALU.add, ALU.max))
                nv.tensor_tensor_scan(nm[:, 1, ::-1], zer[:, 0, :], aa[:, 1, ::-1], NEG, ALU.add, ALU.max).then_inc(rows_ready, 1)
                dve.wait_ge(rows_ready, 1)
                link(nv.tensor_tensor(emr, bb, nm, ALU.add))
                nv.tensor_scalar(nm, nm, -1.0, None, ALU.mult).then_inc(rows_ready, 1)
                dve.wait_ge(rows_ready, 2)
                dve.wait_ge(m_out, 3)
                e1 = E2.rearrange("p d j t -> p (d j t)")
                for h in range(H2):
                    dve.wait_ge(m_em, h + 1)
                    for d in range(2):
                        for j in range(TT):
                            ins = nv.tensor_scalar(E2[:, d, j, :], PS[:, 3, T * d:T * (d + 1)], ACOL[:, d, j, h:h + 1], 0.0, ALU.add, ALU.min)
                            if d + j < 2:
                                link(ins)
                    ins.then_inc(m_arg, 1)
                    dve.wait_ge(m_exp, h + 1)
                    link(nv.tensor_tensor(e1, e1, MASK2, ALU.mult))
                    dve.wait_ge(m_s, h + 1)
                    e3 = E2.rearrange("p d j t -> p d (j t)")
                    nv.scalar_tensor_tensor(e3, PS[:, 2, :].unsqueeze(1).broadcast_to([P, 2, 512]), DH2 ** -0.5, e3, ALU.mult, ALU.mult)\
                        .then_inc(m_w, 1)
                    lo, hi = max(4 * h - 2, 0), min(4 * h + 2, 12)
                    dve.wait_ge(act2, 8 + hi // 2)
                    conv(HX2, 16, P2_CHW, P2_CHB, lo, hi, 12)
                    dve.wait_ge(m_num, h + 1)
                    dve.wait_ge(m_emo, h + 1)
                    ems = EMS.rearrange("p a b -> p (a b)")
                    num = NUM.rearrange("p a b -> p (a b)")
                    link(nv.scalar_tensor_tensor(num, PS[:, 6, :], -1.0, ems, ALU.mult, ALU.max))
                    link(nv.tensor_tensor(num, PS[:, 6, :], num, ALU.max))
                    link(nv.reciprocal(num, num))
                    link(nv.tensor_tensor(num, PS[:, 5, :], num, ALU.mult))
                    nv.tensor_tensor(HS2[:, h, :], NUM[:, 0, :], NUM[:, 1, :], ALU.add).then_inc(m_h, 1)
                dve.wait_ge(m_h, H2)
                dve.wait_ge(act2, 16)
                group_norm(1, HS2, P2_MN, 0, proj[:, 12:16, :])

            def group_norm(n, x, gain, at, gate):
                nv.tensor_tensor(E2F, x, x, ALU.mult).then_inc(r_sq, 1)
                dve.wait_ge(r_std, n)
                link(nv.reciprocal(E2F, E2F))
                for b in range(4):
                    ins = nv.scalar_tensor_tensor(hT[:, at + b, :], x[:, b, :], p2[:, gain + b:gain + b + 1], E2F[:, b, :], ALU.mult, ALU.mult)
                    if b < 3 or gate is not None:
                        link(ins)
                if gate is not None:
                    ins = nv.tensor_tensor(hT[:, at:at + 4, :], hT[:, at:at + 4, :], gate, ALU.mult)
                ins.then_inc(cat_ready, 1)

            def hyena():
                z = HX2[:, 8:12, :]
                for o in range(2):
                    dve.wait_ge(u2_ready, o + 1)
                    for kt in range(TT):
                        a, b = PS[:, 2 + 2 * kt, :], PS[:, 3 + 2 * kt, :]
                        c, d = KF[:, kt, o, 0, :], KF[:, kt, o, 1, :]
                        link(nv.tensor_tensor(TMP1, a, c, ALU.mult))
                        link(nv.tensor_tensor(TMP2, b, d, ALU.mult))
                        link(nv.tensor_tensor(YF[:, kt, 0, :], TMP1, TMP2, ALU.subtract))
                        link(nv.tensor_tensor(TMP1, a, d, ALU.mult))
                        link(nv.tensor_tensor(TMP2, b, c, ALU.mult))
                        ins = nv.tensor_tensor(YF[:, kt, 1, :], TMP1, TMP2, ALU.add)
                        if kt == 0:
                            link(ins)
                    ins.then_inc(yf_ready, 1)
                    dve.wait_ge(yt_ready, o + 1)
                    for b in range(4):
                        link(nv.scalar_tensor_tensor(z[:, b, :], z[:, b, :], p2[:, P2_HBIAS + 4 * o + b:P2_HBIAS + 4 * o + b + 1],
                                                     PS[:, 6 + b // 2, T * (b % 2):T * (b % 2 + 1)], ALU.mult, ALU.add))
                    nv.tensor_tensor(z, z, HX2[:, 4 * o:4 * o + 4, :], ALU.mult).then_inc(z_ready2, 1)
                    dve.wait_ge(z_ready2, o + 1)
                group_norm(2, z, P2_HN, 4, None)

            def residual(n, base, signal, gate, bank):
                for b in range(2):
                    k = 2 * n + b
                    ins = nv.scalar_tensor_tensor(xT[:, k, :], PS[:, bank, T * b:T * (b + 1)], mod[:, gate + k:gate + k + 1], xT[:, k, :],
                                                  ALU.mult, ALU.add)
                ins.then_inc(signal, 1)

            def route():
                m, s = ST4[:, 0:TT], ST4[:, TT:2 * TT]
                wide = lambda a: a.unsqueeze(2).broadcast_to([P, TT, EXPERTS])
                dve.wait_ge(rt_logit, 1)
                lg = banks(2, 1, TT, EXPERTS)
                link(nv.tensor_reduce(m, lg, AX, ALU.max))
                nv.tensor_tensor(LOG, lg, wide(m), ALU.subtract).then_inc(rt_max, 1)
                dve.wait_ge(rt_exp, 1)
                link(nv.tensor_reduce(s, LOG, AX, ALU.add))
                link(nv.reciprocal(s, s))
                nv.tensor_tensor(LOG, LOG, wide(s), ALU.mult).then_inc(rt_prob, 1)
                dve.wait_ge(rt_tr, 1)
                link(nv.tensor_copy(AFF, PS[0:EXPERTS, 3, 0:T]))
                for g in range(CAP // 8):
                    v, ix = VAL[:, 8 * g:8 * g + 8], IDXU[:, 8 * g:8 * g + 8].bitcast(U32)
                    link(nv.max(v, AFF))
                    link(nv.max_index(ix, v, AFF))
                    link(nv.match_replace(AFF, v, AFF, -1.0))
                link(nv.tensor_copy(IDXF, IDXU.bitcast(U32)))
                for a, src in enumerate((IDXF, VAL)):
                    ins = nv.tensor_copy(REP[:, a, :, :], src.unsqueeze(1).broadcast_to([EXPERTS, 4, CAP]))
                    if a == 0:
                        link(ins)
                ins.then_inc(topk_done, 1)
                eye = ident[0:EXPERTS, 0:EXPERTS].unsqueeze(2).broadcast_to([EXPERTS, EXPERTS, CAP])
                nv.tensor_tensor(DIAG[0:EXPERTS, :].rearrange("p (e s) -> p e s", s=CAP), eye,
                                 IDXF.unsqueeze(1).broadcast_to([EXPERTS, EXPERTS, CAP]), ALU.mult).then_inc(diag_ready, 1)
                dve.wait_ge(row_ready, 1)
                for t in range(TT):
                    ins = nv.tensor_scalar(PICK[:, t, :], PS[:, 3, :], c2[:, D_TOK + t:D_TOK + t + 1], None, ALU.is_equal)
                    if t == 0:
                        link(ins)
                ins.then_inc(pick_ready, 1)
                nv.memset(ZERO, 0.0).then_inc(zero_e, 1)
                dve.wait_ge(xs_out, KD)
                dve.wait_ge(ix_out, 1)

            def experts():
                iota = c2[:, D_IOTA:D_IOTA + T]
                with dve.Fori(0, EXPERTS) as e:
                    dve.wait_ge(expert_slots, EXPERT_SLOTS * e + 8)
                    nv.tensor_scalar(XSE.rearrange("p k s -> p (k s)"), XS[:, e, :, :].rearrange("p k s -> p (k s)"), 1.0, None, ALU.mult)\
                        .then_inc(xs_staged, 1)
                    dve.wait_ge(scattered, e + 1)
                    nv.tensor_scalar(GE, iota, IG[:, 0, bass.ts(e, 1)], IG[:, 1, bass.ts(e, 1)], ALU.is_equal, ALU.mult).then_inc(ge_ready, 1)
                    dve.wait_ge(expert_slots, EXPERT_SLOTS * e + EXPERT_SLOTS + 8)
                    dve.wait_ge(hs_ready, e + 1)
                    nv.tensor_tensor(HE, HSE, PS[:, 3, :], ALU.mult).then_inc(he_ready, 1)
                    dve.wait_ge(expert_slots, EXPERT_SLOTS * e + EXPERT_SLOTS + 12)
                    nv.tensor_copy(YE, PS[:, 5, :]).then_inc(ye_ready, 1)

            norm(1, gs1, 0)
            filters()
            mlstm()
            hyena()
            for n in range(4):
                dve.wait_ge(block_done, BASE2 + 16 + n + 1)
                residual(n, 0, dve2, 16, (16 + n) % 2)
            dve.wait_ge(dve2, 4)
            norm(2, gs2, 24)
            route()
            experts()
            dve.wait_ge(scattered, EXPERTS + 1)
            for n, b in enumerate((6, 7, 0, 1)):
                residual(n, 0, moe_sum, 40, b)
            dve.wait_ge(moe_sum, 4)
            square(3)
            for k in range(KD):
                ins = nv.scalar_tensor_tensor(hT[:, k, :], xT[:, k, :], p2[:, P2_GFIN + k:P2_GFIN + k + 1], RSTD2, ALU.mult, ALU.mult)
                if k < KD - 1:
                    link(ins)
            ins.then_inc(h2_ready, 1)

        block = ctx.enter_context(nc.Block())

        @block.sync
        def _(sp):
            def load(slot, pieces):
                for dst, src in pieces:
                    sp.dma_start(dst, src).then_inc(ring_full[slot], 16)

            def by_rows(w, slot, cols):
                n = w.shape[0] // P
                c = w.shape[1]
                v = w.rearrange("(k p) n -> p k n", p=P)
                r = ring[:, slot, 0:n * c].rearrange("p (k n) -> p k n", n=c)
                load(slot, [(r[:, 0:n // 2], v[:, 0:n // 2]), (r[:, n // 2:n], v[:, n // 2:n])])

            sp.wait_ge(const_loaded, 4 * 16)
            with sp.Fori(0, LAYERS) as l:
                for n in range(LAYER_SLOTS):
                    if n >= RING:
                        sp.wait_ge(block_done, START + LAYER_BLOCKS * l + SLOT_DONE[n - RING])
                    else:
                        sp.wait_ge(block_done, START + LAYER_BLOCKS * l - (RING - 1 - n))
                    sp.sem_inc(slot_freed, 1)
                    s = n % RING
                    if n in S_ADA:
                        by_rows(io["w_ada_2"][0].rearrange("d (l n) -> l d n", l=LAYERS)[l][:, 512 * S_ADA.index(n):512 * S_ADA.index(n) + 512], s, 512)
                    elif n < N_PROJ // 2:
                        by_rows(io["w_in"][l][:, IN_ORDER[n]:IN_ORDER[n] + 512], s, 512)
                    elif n < S_OUT:
                        by_rows(io[("w_attn_o", "w_rwkv_o", "w_ret_o")[S_MIX.index(n)]][l], s, D)
                    elif n < S_FFN:
                        by_rows(io["w_out"][l][:, 512 * (n - S_OUT):512 * (n - S_OUT + 1)], s, 512)
                    elif n < S_DOWN:
                        c = 256 * (n - S_FFN)
                        load(s, [(ring[:, s, 2048 * g:2048 * (g + 1)].rearrange("p (k n) -> p k n", n=256),
                                  io[("w_ffn_gate", "w_ffn_up")[g]][l][:, c:c + 256].rearrange("(k p) n -> p k n", p=P))
                                 for g in range(2)])
                    else:
                        c = P * (n - S_DOWN)
                        by_rows(io["w_ffn_down"][l][:, c:c + P], s, P)
            second_sync(sp, load, by_rows)

        @block.gpsimd
        def _(pool):
            pool.memset(bias[:, 0:1], EPS).then_inc(bias_set, 1)
            pool.memset(bias[:, 1:2], LNX_EPS).then_inc(bias_set, 1)
            pool.memset(bias[:, 2:3], 1.0).then_inc(bias_set, 1)
            with pool.Fori(0, LAYERS) as l:
                pool.wait_ge(oa_out, 3)
                pool.memset(w_(9216, 4096), 0.0).then_inc(gm_zero, 1)
                pool.wait_ge(layer_fin, 3)
                pool.sem_clear(layer_sems)
                pool.sem_inc(layer_go, 1)
            second_pool(pool)

        @block.tensor
        def _(pe):
            nt = nc.tensor

            def taken(q):
                if q >= 2:
                    pe.wait_ge(act_taken if BY_ACT[q - 2] else dve_taken, TAKEN[q - 2])

            def ada(l, n):
                q, s = Q_ADA[n], S_ADA[n] % RING
                pe.wait_ge(ring_full[s], full(l, S_ADA[n]))
                taken(q)
                for k in range(KD):
                    j = 32 * (k % 4)
                    mm = nt.matmul(PS[j:j + 32, q % 2, :], cond[:, k, 32 - n:64 - n], ring[:, s, 512 * k:512 * (k + 1)],
                                   start=(k < 4), stop=(k >= 4))
                mm.then_inc(block_done, 1)

            def ada_columns():
                taken(Q_COLS)
                pe.wait_ge(dve_taken, TAKEN[Q_ADA[-1]])
                for b in range(4):
                    mm = nt.matmul(PS[:, Q_COLS % 2, N_ADA * b:N_ADA * (b + 1)], mod_rows[:, P * b:P * (b + 1)], con[:, C_SEL:C_SEL + N_ADA],
                                   start=True, stop=True)
                mm.then_inc(block_done, 1)

            def product(q, weight, moving, kn, n_blocks=2):
                taken(q)
                for b in range(n_blocks):
                    for k in range(kn):
                        mm = nt.matmul(PS[:, q % 2, T * b:T * (b + 1)], weight(b, k), moving(k), start=(k == 0), stop=(k == kn - 1))
                mm.then_inc(block_done, 1)

            def norm_sums(n):
                pe.wait_ge(sq_ready, n)
                for k in range(KD):
                    mm = nt.matmul(PS[:, 2, 0:T], ones, SQ[:, k, :], start=(k == 0), stop=(k == KD - 1))
                mm.then_inc(ss_ready, 1)

            def project(l, lo, hi):
                for q in range(lo, hi):
                    s, half = q // 2 % RING, q % 2
                    if half == 0:
                        pe.wait_ge(ring_full[s], full(l, q // 2))
                    product(q, lambda b, k: ring[:, s, 512 * k + P * (2 * half + b):512 * k + P * (2 * half + b + 1)],
                            lambda k: hT[:, k, :], KD)

            def head_sums(bank, src, signal):
                for n in range(2):
                    mm = nt.matmul(PS[:, bank + n, :], bd, src[:, 2 * n:2 * n + 2, :].rearrange("p a b -> p (a b)"), start=True, stop=True)
                mm.then_inc(signal, 1)

            def lora_products():
                pe.wait_ge(lora_in, 2)
                for b in range(HB):
                    mm = nt.matmul(PS[:, 2 + b // 2, T * (b % 2):T * (b % 2 + 1)], lora[0:64, P * b:P * (b + 1)],
                                   proj[0:64, B_LORA, :], start=True, stop=True)
                mm.then_inc(lora_done, 1)
                for b in range(HB):
                    mm = nt.matmul(PS[:, 4 + b // 2, T * (b % 2):T * (b % 2 + 1)], lora[64:128, P * b:P * (b + 1)],
                                   proj[64:128, B_LORA, :], start=True, stop=True)
                mm.then_inc(lora_done, 1)
                for b in range(HB):
                    mm = nt.matmul(PS[:, 6 + b // 2, T * (b % 2):T * (b % 2 + 1)], lora[:, 512 + P * b:512 + P * (b + 1)],
                                   proj[:, B_GD, :], start=True, stop=True)
                mm.then_inc(lora_done, 1)

            def rwkv_prep():
                pe.wait_ge(kk_sq, 1)
                pe.wait_ge(lora_out, 4)
                head_sums(2, X3, kk_ss)
                pe.wait_ge(lora_out, 10)
                for t in range(TT):
                    for b in range(HB):
                        mm = nt.transpose(PS[:, 4 + t, P * b:P * (b + 1)], proj[:, B_V + b, P * t:P * (t + 1)], ident)
                mm.then_inc(tok_ready, 1)

            def rwkv_decayed():
                pe.wait_ge(gram_in, 1)
                for n, src in enumerate((AT, KK)):
                    for b in range(HB):
                        mm = nt.transpose(PS[:, 6 + n, P * b:P * (b + 1)], src[:, b, 0:P], ident)
                mm.then_inc(tok_ready, 1)
                pe.wait_ge(kk_std, 1)
                pe.wait_ge(bonus_in, 1)
                head_sums(2, Y, bonus_ss)

            def rwkv_chunk(l, t):
                cols = slice(P * t, P * (t + 1))
                if t == 0:
                    pe.wait_ge(tok_out, 4)
                    pe.wait_ge(oa_out, 3)
                else:
                    pe.wait_ge(y_out, 1)
                    pe.wait_ge(st_ready, 1)
                for h in range(HEADS):
                    bk = 2 + h % 2 + 2 * (h // 2 % 2)
                    if h >= 4:
                        pe.wait_ge(gram_taken, 8 * t + h - 3)
                    o, b = hrow(h), h // 2
                    nt.matmul(PS[:, bk, 0:P], AR[o, b, t, 0, :], AT[o, b, cols], start=True, stop=True)
                    nt.matmul(PS[:, bk, P:2 * P], AT[o, b, cols], AR[o, b, t, 1, :], start=True, stop=True)
                    nt.matmul(PS[:, bk, 2 * P:4 * P], KK[o, b, cols], AR[o, b, t, :, :].rearrange("p a b -> p (a b)"),
                              start=True, stop=True).then_inc(gram_ready, 1)
                for lev in range(LEVELS):
                    for half in range(2):
                        pe.wait_ge(qt_ready, t * (2 * LEVELS + 1) + (2 * lev + half if lev else 1))
                        if lev == 0:
                            pe.wait_ge(gram_taken, 8 * t + 4 * (half + 1))
                        for u in range(4 * half, 4 * half + 4):
                            mm = nt.matmul(PS[:, 6 + half, P * (u % 4):P * (u % 4 + 1)], GM[:, u, 0:P], QT[:, u, 0, :],
                                           start=True, stop=True)
                        mm.then_inc(w1_ready, 1)
                    if lev in ADA_AT[t]:
                        ada(l, ADA_AT[t][lev])
                    if lev == COLS_AT[t]:
                        ada_columns()
                    for half in range(2):
                        i = (t * LEVELS + lev) * 2 + half
                        pe.wait_ge(w1_masked, i + 1)
                        for u in range(4 * half, 4 * half + 4):
                            bk, c = 2 + 2 * half + u % 4 // 2, 2 * P * (u % 2)
                            nt.matmul(PS[:, bk, c:c + P], QT[:, u, 1, :], W1S[:, u, :], start=True, stop=True)
                            mm = nt.matmul(PS[:, bk, c + P:c + 2 * P], W1S[:, u, :], QT[:, u, 1, :], start=True, stop=True)
                        mm.then_inc(dq_ready, 1)
                pe.wait_ge(qt_ready, (t + 1) * (2 * LEVELS + 1))
                for h in [0, 2, 4, 6, 1, 3, 5, 7]:
                    out = PS[:, 6 + h % 2, HD * (h // 2):HD * (h // 2 + 1)]
                    if t:
                        nt.matmul(out, AR[hrow(h), h // 2, t, 0, :], ST[hrow(h), h // 2, :], start=True, stop=False)
                    mm = nt.matmul(out, GM[:, h, 2 * P:3 * P], VTOK[:, t, HD * h:HD * (h + 1)], start=(t == 0), stop=True)
                mm.then_inc(rhs_ready, 1)
                mix(l, 0, 2 * t, 2 * t + 1)
                pe.wait_ge(rhs_out, 2 * (t + 1))
                for h in range(HEADS):
                    mm = nt.matmul(PS[:, 2, HD * h:HD * (h + 1)], QT[:, h, 0, :], RHS[:, h, :], start=True, stop=True)
                mm.then_inc(u_ready, 1)
                mix(l, 0, 2 * t + 1, 2 * t + 2)
                pe.wait_ge(u_out, t + 1)
                for h in range(HEADS):
                    out = PS[hrow(h), 3, P * (h // 2):P * (h // 2 + 1)]
                    nt.matmul(out, U[:, h, :], GM[:, h, P:2 * P], start=True, stop=False)
                    mm = nt.matmul(out, VTOK[:, t, HD * h:HD * (h + 1)], GM[:, h, 3 * P:4 * P], start=False, stop=(t == 0))
                    if t:
                        mm = nt.matmul(out, ST[hrow(h), h // 2, :], AR[hrow(h), h // 2, t, 1, :], start=False, stop=True)
                mm.then_inc(y_ready, 1)
                if t == 0:
                    for h in range(HEADS):
                        out = PS[hrow(h), 5, HD * (h // 2):HD * (h // 2 + 1)]
                        nt.matmul(out, BKT[:, 0, HD * h:HD * (h + 1)], U[:, h, :], start=True, stop=False)
                        mm = nt.matmul(out, BKT[:, 1, HD * h:HD * (h + 1)], VTOK[:, 0, HD * h:HD * (h + 1)], start=False, stop=True)
                    mm.then_inc(s_ready, 1)

            def attention(l):
                pe.wait_ge(att_sq, 2)
                pe.wait_ge(bonus_out, 1)
                head_sums(2, ATS[:, 0:HB, :], att_ss)
                nt.matmul(PS[:, 4, 0:T], bd, ATS[:, HB, :], start=True, stop=True).then_inc(att_ss, 1)
                pe.wait_ge(tok_out, 4)
                for t in range(TT):
                    mm = nt.transpose(PS[:, 6, P * t:P * (t + 1)], proj[:, B_AV, P * t:P * (t + 1)], ident)
                mm.then_inc(att_tr, 1)
                project(l, 20, 22)
                pe.wait_ge(att_qk, 2)
                for kv in range(2):
                    mm = nt.matmul(PS[:, 5, T * kv:T * (kv + 1)], con[:, C_DUP + P * kv:C_DUP + P * (kv + 1)], proj[:, B_AK, :],
                                   start=True, stop=True)
                mm.then_inc(att_tr, 1)
                pe.wait_ge(att_kv, 2)
                for r, (t, heads) in enumerate(ROUNDS):
                    w = P * (t + 1)
                    if r:
                        pe.wait_ge(oa_out, r)
                    for n, h in enumerate(heads):
                        at = n * w
                        mm = nt.matmul(PS[:, 2 + at // 512, at % 512:at % 512 + w], proj[hrow(h), B_AQ + h // 2, P * t:P * (t + 1)],
                                       KDUP[hrow(h), h // 4, 0:w], start=True, stop=True)
                    mm.then_inc(sc_ready, 1)
                    project(l, *BESIDE_SOFTMAX[r])
                    pe.wait_ge(p_ready, r + 1)
                    for n in range(8):
                        mm = nt.transpose(PS[:, 6 + n // 4, P * (n % 4):P * (n % 4 + 1)], SCO[:, P * n:P * (n + 1)], ident)
                    mm.then_inc(pt_ready, 1)
                    project(l, *BESIDE_COPY[r])
                    pe.wait_ge(pt_out, r + 1)
                    for n, h in enumerate(heads):
                        kv = h // 4
                        for j in range(t + 1):
                            mm = nt.matmul(PS[hrow(h), 4, P * (h // 2):P * (h // 2 + 1)], VATT[:, j, HD * kv:HD * (kv + 1)],
                                           PT[:, n * (t + 1) + j, :], start=(j == 0), stop=(j == t))
                    mm.then_inc(oa_ready, 1)

            def rwkv_norm_and_retention(l):
                def rotate(n, at):
                    for b in range(2):
                        mm = nt.matmul(PS[:, 2 + 2 * n + b, :], perm, proj[:, at + 2 * b:at + 2 * b + 2, :].rearrange("p a b -> p (a b)"),
                                       start=True, stop=True)
                    mm.then_inc(rot_ready, 1)

                pe.wait_ge(y_out, 2)
                head_sums(4, Y, ln_ss)
                rotate(0, B_RQ)
                pe.wait_ge(ln_in, 1)
                head_sums(6, X1, ln_ss)
                rotate(1, B_RK)
                pe.wait_ge(ln_std, 1)
                for t in range(TT):
                    for b in range(HB):
                        mm = nt.transpose(PS[:, 6 + t, P * b:P * (b + 1)], proj[:, B_RV + b, P * t:P * (t + 1)], ident)
                mm.then_inc(vr_ready, 1)
                pe.wait_ge(rot_out, 2)
                for h in range(HEADS):
                    o, b, bk = hrow(h), h // 2, 2 + h % 2 + 2 * (h // 2 % 2)
                    if h >= 4:
                        pe.wait_ge(rs_out, h - 3)
                    nt.matmul(PS[:, bk, 0:T], proj[o, B_RK + b, 0:P], proj[o, B_RQ + b, :], start=True, stop=True)
                    nt.matmul(PS[:, bk, T:T + P], proj[o, B_RK + b, P:T], proj[o, B_RQ + b, P:T], start=True, stop=True)\
                        .then_inc(rs_ready, 1)
                pe.wait_ge(vr_out, 2)
                for h in range(HEADS):
                    pe.wait_ge(rs_out, h + 1)
                    o, b = hrow(h), h // 2
                    bk, c = 6 + b // 2, T * (b % 2)
                    nt.matmul(PS[o, bk, c:c + T], VRET[:, 0, HD * h:HD * (h + 1)], SM[:, h, 0:T], start=True, stop=False)
                    mm = nt.matmul(PS[o, bk, c + P:c + T], VRET[:, 1, HD * h:HD * (h + 1)], SM[:, h, T:T + P], start=False, stop=True)
                mm.then_inc(oc_psum, 1)
                mix(l, 1, 0, 2)
                pe.wait_ge(oc_sq, 1)
                head_sums(2, XR, oc_ss)
                mix(l, 1, 2, 4)

            def mix(l, br, lo, hi):
                src, at, ready = ((proj, B_AQ, oa_out), (Y, 0, ob_ready), (proj, B_RQ, oc_ready))[br]
                s = S_MIX[br] % RING
                if lo == 0:
                    pe.wait_ge(ready, 3 if br == 0 else 1)
                    pe.wait_ge(ring_full[s], full(l, S_MIX[br]))
                for i in range(lo, hi):
                    product(Q_MIX[br][i], lambda b, k: ring[:, s, D * k + P * (2 * i + b):D * k + P * (2 * i + b + 1)],
                            lambda k: src[:, at + k, :], HB)

            def out(l):
                pe.wait_ge(dve_taken, TAKEN[Q_OUT - 1])
                for n in range(2):
                    s = (S_OUT + n) % RING
                    pe.wait_ge(ring_full[s], full(l, S_OUT + n))
                    for i in range(2):
                        product(Q_OUT + 2 * n + i, lambda b, k: ring[:, s, 512 * k + P * (2 * i + b):512 * k + P * (2 * i + b + 1)],
                                lambda k: hT[:, k, :], KD)

            def ffn(l):
                pe.wait_ge(h_ready, 2)
                for n in range(N_FFN // 2):
                    s = (S_FFN + n) % RING
                    pe.wait_ge(ring_full[s], full(l, S_FFN + n))
                    for g in range(2):
                        product(Q_FFN + 2 * n + g, lambda b, k: ring[:, s, 2048 * g + 256 * k + P * b:2048 * g + 256 * k + P * (b + 1)],
                                lambda k: hT[:, k, :], KD)
                pe.wait_ge(dve_taken, TAKEN[Q_DOWN - 1])
                for n in range(N_DOWN):
                    s = (S_DOWN + n) % RING
                    pe.wait_ge(ring_full[s], full(l, S_DOWN + n))
                    product(Q_DOWN + n, lambda b, k: ring[:, s, P * k:P * (k + 1)], lambda k: HID[:, k, :], FB, 1)

            pe.sem_inc(block_done, START)
            pe.wait_ge(const_loaded, 4 * 16)
            with pe.Fori(0, LAYERS) as l:
                pe.wait_ge(par_loaded, 32)
                norm_sums(1)
                pe.wait_ge(h_ready, 1)
                project(l, 0, 10)
                lora_products()
                project(l, 10, 12)
                rwkv_prep()
                project(l, 12, 18)
                rwkv_decayed()
                project(l, 18, 20)
                attention(l)
                project(l, 29, 30)
                rwkv_chunk(l, 0)
                rwkv_chunk(l, 1)
                rwkv_norm_and_retention(l)
                mix(l, 2, 0, 4)
                out(l)
                norm_sums(2)
                ffn(l)
                pe.wait_ge(dve_taken, TAKEN[LAYER_BLOCKS - 1])
                pe.sem_inc(layer_fin, 1)
                pe.wait_ge(layer_go, l + 1)
                pe.sem_inc(layer_joined, 1)
            second_tensor(pe)

        @block.scalar
        def _(act):
            na = nc.scalar
            def proj_out(l, lo, hi):
                for q in range(lo, hi):
                    act.wait_ge(block_done, done(l, q))
                    f = ACT.Copy
                    if 2 * q >= B_GATE:
                        f = ACT.Sigmoid
                    elif 2 * q >= B_RG:
                        f = ACT.Silu
                    na.activation(proj[:, 2 * q:2 * q + 2, :].rearrange("p a b -> p (a b)"), PS[:, q % 2, :], f).then_inc(act_taken, 1)

            def norm_root(n):
                act.wait_ge(ss_ready, n)
                na.activation(STD, PS[:, 2, 0:T], ACT.Sqrt, bias=epsc, scale=1.0 / D).then_inc(std_ready, 1)

            def lora_inputs():
                act.wait_ge(z_ready, 1)
                na.activation(proj[0:64, B_LORA, :], proj[0:64, B_LORA, :], ACT.Tanh).then_inc(lora_in, 1)
                na.activation(proj[:, B_GD, :], proj[:, B_GD, :], ACT.Sigmoid).then_inc(lora_in, 1)

            def lora_outputs():
                for n, (dst, col) in enumerate(((X1, PL_W0), (AT, PL_A0))):
                    act.wait_ge(lora_done, n + 1)
                    for b in range(HB):
                        na.activation(dst[:, b, :], PS[:, 2 + 2 * n + b // 2, T * (b % 2):T * (b % 2 + 1)], ACT.Sigmoid,
                                      bias=par[:, col + b:col + b + 1]).then_inc(lora_out, 1)
                act.wait_ge(lora_done, 3)
                for n in range(2):
                    na.activation(GT[:, 2 * n:2 * n + 2, :].rearrange("p a b -> p (a b)"), PS[:, 6 + n, :], ACT.Copy).then_inc(lora_out, 1)

            def rwkv_prep():
                act.wait_ge(kk_ss, 1)
                na.activation(Y[:, :, :].rearrange("p a b -> p (a b)"), banks(2, 2), ACT.Sqrt).then_inc(kk_std, 1)
                act.wait_ge(tok_ready, 1)
                for t in range(TT):
                    na.activation(VTOK[:, t, :], PS[:, 4 + t, :], ACT.Copy).then_inc(tok_out, 1)

            def rwkv_exponentials():
                act.wait_ge(cum_ready, 2)
                na.activation(X1[:, :, :], X1[:, :, :], ACT.Exp, scale=-KAPPA).then_inc(exps_ready, 1)
                na.activation(X3[:, :, :], X2[:, :, :], ACT.Exp, scale=-KAPPA).then_inc(exps_ready, 1)
                act.wait_ge(exps_ready, 2)
                na.activation(X2[:, :, :], X2[:, :, :], ACT.Exp, scale=KAPPA).then_inc(exps_ready, 1)
                na.activation(MIDE, MID[:, :, 1], ACT.Exp, scale=-KAPPA).then_inc(exps_ready, 1)

            def rwkv_decayed():
                act.wait_ge(tok_ready, 2)
                for n in range(2):
                    na.activation(BKT[:, n, :], PS[:, 6 + n, :], ACT.Copy).then_inc(tok_out, 1)

            def rwkv_chunk(t):
                act.wait_ge(rhs_ready, t + 1)
                for odd in range(2):
                    na.activation(RHS[:, odd::2, :], banks(6 + odd, 1, HB, HD), ACT.Copy).then_inc(rhs_out, 1)
                act.wait_ge(u_ready, t + 1)
                na.activation(U[:, :, :].rearrange("p a b -> p (a b)"), PS[:, 2, :], ACT.Copy).then_inc(u_out, 1)
                act.wait_ge(y_ready, t + 1)
                na.activation(Y[:, :, P * t:P * (t + 1)], banks(3, 1, HB, P), ACT.Copy).then_inc(y_out, 1)

            def rwkv_norm():
                act.wait_ge(y_ready, 2)
                act.dma_start(w_(9216, HEADS * 3 * P), io["decay"]).then_inc(dec_loaded, 16)
                act.wait_ge(ln_ss, 2)
                na.activation(X2[:, :, :].rearrange("p a b -> p (a b)"), banks(6, 2), ACT.Sqrt, bias=lnxc, scale=1.0 / HD).then_inc(ln_std, 1)

            def attention(l):
                act.wait_ge(att_ss, 2)
                na.activation(ATS[:, 0:HB, :].rearrange("p a b -> p (a b)"), banks(2, 2), ACT.Sqrt, bias=epsc, scale=1.0 / HD).then_inc(att_std, 1)
                na.activation(ATS[:, HB, :], PS[:, 4, 0:T], ACT.Sqrt, bias=epsc, scale=1.0 / HD).then_inc(att_std, 1)
                act.wait_ge(att_tr, 1)
                na.activation(VATT[:, :, :].rearrange("p a b -> p (a b)"), PS[:, 6, 0:T], ACT.Copy).then_inc(att_kv, 1)
                proj_out(l, 20, 22)
                act.wait_ge(att_tr, 2)
                na.activation(KDUP[:, :, :].rearrange("p a b -> p (a b)"), PS[:, 5, :], ACT.Copy).then_inc(att_kv, 1)
                for r, (t, heads) in enumerate(ROUNDS):
                    act.wait_ge(sc_max, r + 1)
                    na.activation(SCO, SCO, ACT.Exp).then_inc(sc_exp, 1)
                    na.activation(SK[:, 0:len(heads)], SK[:, 0:len(heads)], ACT.Exp).then_inc(sc_exp, 1)
                    proj_out(l, *BESIDE_SOFTMAX[r])
                    act.wait_ge(pt_ready, r + 1)
                    na.activation(PT[:, :, :].rearrange("p a b -> p (a b)"), banks(6, 2), ACT.Copy).then_inc(pt_out, 1)
                    proj_out(l, *BESIDE_COPY[r])
                    act.wait_ge(oa_ready, r + 1)
                    b0, b1 = (0, 4) if t == 0 else (2 * (r - 1), 2 * r)
                    na.activation(proj[:, B_AQ + b0:B_AQ + b1, P * t:P * (t + 1)],
                                  PS[:, 4, P * b0:P * b1].rearrange("p (a b) -> p a b", b=P), ACT.Copy).then_inc(oa_out, 1)

            def retention():
                act.wait_ge(vr_ready, 1)
                for t in range(TT):
                    na.activation(VRET[:, t, :], PS[:, 6 + t, :], ACT.Copy).then_inc(vr_out, 1)
                act.wait_ge(oc_psum, 1)
                na.activation(proj[:, B_RQ:B_RQ + HB, :].rearrange("p a b -> p (a b)"), banks(6, 2), ACT.Copy).then_inc(oc_out, 1)
                act.wait_ge(oc_ss, 1)
                na.activation(XR[:, :, :].rearrange("p a b -> p (a b)"), banks(2, 2), ACT.Sqrt, bias=epsc, scale=1.0 / HD).then_inc(oc_std, 1)

            def ffn(l):
                for n in range(N_FFN // 2):
                    act.wait_ge(block_done, done(l, Q_FFN + 2 * n))
                    if n >= 2:
                        act.wait_ge(dve_taken, TAKEN[Q_FFN + 2 * n - 3])
                    na.activation(SILU[:, n % 2, :], PS[:, Q_FFN % 2, :], ACT.Silu).then_inc(act_taken, 1)

            act.dma_start(con[:, :], io["constants"]).then_inc(const_loaded, 16)
            act.dma_start(xT[:, :, :], io["xT"]).then_inc(const_loaded, 16)
            act.dma_start(cond[:, :, :], io["cond"]).then_inc(const_loaded, 16)
            act.dma_start(mod[:, :], io["ada_bias"]).then_inc(const_loaded, 16)
            act.wait_ge(bias_set, 3)
            with act.Fori(0, LAYERS) as l:
                act.dma_start(par[:, :], io["layer_params"][l]).then_inc(par_loaded, 16)
                act.dma_start(lora[:, :], io["layer_lora"][l]).then_inc(par_loaded, 16)
                norm_root(1)
                proj_out(l, 0, 8)
                lora_inputs()
                proj_out(l, 8, 10)
                lora_outputs()
                proj_out(l, 10, 12)
                rwkv_prep()
                proj_out(l, 12, 14)
                rwkv_exponentials()
                proj_out(l, 14, 18)
                rwkv_decayed()
                proj_out(l, 18, 20)
                attention(l)
                proj_out(l, 29, 30)
                rwkv_chunk(0)
                rwkv_chunk(1)
                rwkv_norm()
                retention()
                norm_root(2)
                ffn(l)
                act.wait_ge(act_taken, TAKEN[Q_DOWN - 2])
                act.sem_inc(layer_fin, 1)
                act.wait_ge(layer_go, l + 1)
                act.sem_inc(layer_joined, 1)
            second_scalar(act)

        @block.vector
        def _(dve):
            nv = nc.vector
            count = [0]

            def link(ins):
                count[0] += 1
                ins.then_inc(vec_order, 1)
                dve.wait_ge(vec_order, count[0])

            def norm(n, gain):
                nv.tensor_tensor(SQ, xT[:, :, :], xT[:, :, :], ALU.mult).then_inc(sq_ready, 1)
                dve.wait_ge(std_ready, n)
                link(nv.reciprocal(RSTD, STD))
                for k in range(KD):
                    ins = nv.scalar_tensor_tensor(hT[:, k, :], xT[:, k, :], par[:, gain + k:gain + k + 1], RSTD, ALU.mult, ALU.mult)
                    if k < KD - 1:
                        link(ins)
                ins.then_inc(h_ready, 1)

            def rwkv_mix():
                dve.wait_ge(act_taken, 8)
                raw = proj[:, B_R:B_R + RW_BLOCKS, :]
                link(nv.tensor_tensor(SHIFT[:, :, 1:T], raw[:, :, 0:T - 1], raw[:, :, 1:T], ALU.subtract))
                link(nv.tensor_scalar(SHIFT[:, :, 0:1], raw[:, :, 0:1], -1.0, None, ALU.mult))
                for b in range(RW_BLOCKS):
                    ins = nv.scalar_tensor_tensor(raw[:, b, :], SHIFT[:, b, :], par[:, PL_MU + b:PL_MU + b + 1], raw[:, b, :],
                                                  ALU.mult, ALU.add)
                    if b < RW_BLOCKS - 1:
                        link(ins)
                ins.then_inc(z_ready, 1)

            r, k, v = (proj[:, b:b + HB, :] for b in (B_R, B_K, B_V))

            def rwkv_prep():
                dve.wait_ge(z_ready, 1)
                for b in range(HB):
                    link(nv.tensor_scalar(KK[:, b, :], k[:, b, :], par[:, PL_KK + b:PL_KK + b + 1], None, ALU.mult))
                nv.tensor_tensor(X3, KK, KK, ALU.mult).then_inc(kk_sq, 1)
                dve.wait_ge(lora_out, 8)
                for b in range(HB):
                    for t in range(TT):
                        c = slice(P * t, P * (t + 1))
                        link(nv.tensor_tensor_scan(X2[:, b, c], ones, X1[:, b, c], 0.0, ALU.mult, ALU.add))
                by_chunk = lambda a: a.rearrange("p b (t n) -> p (b t) n", n=P)
                x2c = by_chunk(X2)
                mid = small[:, 0:8]
                link(nv.tensor_copy(mid, x2c[:, :, P // 2 - 1]))
                nv.tensor_tensor(x2c, x2c, mid.unsqueeze(2).broadcast_to([P, 8, P]), ALU.subtract).then_inc(cum_ready, 1)
                dve.wait_ge(cum_ready, 1)
                nv.tensor_tensor(X1, X2, X1, ALU.subtract).then_inc(cum_ready, 1)
                dve.wait_ge(kk_std, 1)
                link(nv.tensor_scalar(Y, Y, 1e-12, None, ALU.max))
                link(nv.reciprocal(Y, Y))
                link(nv.tensor_tensor(KK, KK, Y, ALU.mult))
                for b in range(HB):
                    link(nv.tensor_scalar(Y[:, b, :], AT[:, b, :], -1.0, par[:, PL_KA + b:PL_KA + b + 1], ALU.add, ALU.mult))
                link(nv.scalar_tensor_tensor(k, Y, 1.0, k, ALU.add, ALU.mult))
                link(nv.tensor_tensor(AT, KK, AT, ALU.mult))
                dve.wait_ge(exps_ready, 4)
                arv = AR.rearrange("p b t s n -> p (b t) s n")
                link(nv.tensor_tensor(arv[:, :, 1, :], by_chunk(r), by_chunk(X3), ALU.mult))
                link(nv.scalar_tensor_tensor(arv[:, :, 0, :], by_chunk(KK), -1.0, by_chunk(X1), ALU.mult, ALU.mult))
                link(nv.tensor_tensor(AT, AT, X2, ALU.mult))
                link(nv.tensor_tensor(SC, X3[:, :, P - 1], MIDE, ALU.mult))
                nv.tensor_tensor(KK, k, X2, ALU.mult).then_inc(gram_in, 1)
                for b in range(HB):
                    ins = nv.scalar_tensor_tensor(Y[:, b, :], r[:, b, :], par[:, PL_RK + b:PL_RK + b + 1], k[:, b, :], ALU.mult, ALU.mult)
                    if b < HB - 1:
                        link(ins)
                ins.then_inc(bonus_in, 1)

            def rwkv_chunk(l, t):
                dve.wait_ge(gm_zero, 1)
                dve.wait_ge(gram_in, 1)
                if t:
                    dve.wait_ge(y_ready, 1)
                    dve.wait_ge(s_ready, 1)
                else:
                    dve.wait_ge(bonus_in, 1)
                nv.tensor_copy(QT.rearrange("p h s n -> p (h s) n"), ident.unsqueeze(1).broadcast_to([P, 2 * HEADS, P])).then_inc(qt_ready, 1)
                mask = con[:, C_GRAM:C_GRAM + 512].bitcast(U32)
                for h in range(HEADS):
                    dve.wait_ge(gram_ready, 8 * t + h + 1)
                    nv.copy_predicated(GM[:, h, :], mask, PS[:, 2 + h % 2 + 2 * (h // 2 % 2), :]).then_inc(gram_taken, 1)
                dve.wait_ge(qt_ready, t * (2 * LEVELS + 1) + 1)
                for lev in range(LEVELS):
                    lm = con[:, C_LVL + P * lev:C_LVL + P * (lev + 1)]
                    for half in range(2):
                        i = (t * LEVELS + lev) * 2 + half
                        u = slice(4 * half, 4 * half + 4)
                        dve.wait_ge(w1_ready, i + 1)
                        nv.tensor_tensor(W1S[:, u, :], banks(6 + half, 1, 4, P), lm.unsqueeze(1).broadcast_to([P, 4, P]), ALU.mult)\
                            .then_inc(w1_masked, 1)
                    if lev in ADA_AT[t]:
                        n = ADA_AT[t][lev]
                        dve.wait_ge(block_done, done(l, Q_ADA[n]))
                        rows = PS[:, Q_ADA[n] % 2, :]
                        if n == 0:
                            nv.tensor_copy(mod_rows[:, :], rows).then_inc(dve_taken, 1)
                        else:
                            dve.wait_ge(dve_taken, TAKEN[Q_ADA[n] - 1])
                            nv.tensor_tensor(mod_rows[:, :], rows, mod_rows[:, :], ALU.add).then_inc(dve_taken, 1)
                    if lev == COLS_AT[t]:
                        dve.wait_ge(block_done, done(l, Q_COLS))
                        m = MOD2[:, l, :, :]
                        nv.tensor_tensor(m, PS[:, Q_COLS % 2, 0:4 * N_ADA].rearrange("p (n b) -> p n b", b=N_ADA), m, ALU.add).then_inc(dve_taken, 1)
                    for half in range(2):
                        i = (t * LEVELS + lev) * 2 + half
                        u = slice(4 * half, 4 * half + 4)
                        dve.wait_ge(dq_ready, i + 1)
                        q = QT[:, u, :, :].rearrange("p a b c -> p (a b c)")
                        nv.tensor_tensor(q, q, banks(2 + 2 * half, 2), ALU.add).then_inc(qt_ready, 1)
                mix(l, 0, 2 * t, 2 * t + 2)
                if t == 0:
                    dve.wait_ge(s_ready, 1)
                    nv.tensor_tensor(ST, banks(5, 1, HB, HD), SC.unsqueeze(2).broadcast_to([P, HB, HD]), ALU.mult).then_inc(st_ready, 1)

            def attention():
                q, kk = proj[:, B_AQ:B_AQ + HB, :], proj[:, B_AK, :]
                dve.wait_ge(act_taken, 10)
                nv.tensor_tensor(ATS[:, 0:HB, :], q, q, ALU.mult).then_inc(att_sq, 1)
                nv.tensor_tensor(ATS[:, HB, :], kk, kk, ALU.mult).then_inc(att_sq, 1)
                dve.wait_ge(bonus_ss, 1)
                nv.tensor_tensor(r, banks(2, 2, HB, T), v, ALU.mult).then_inc(bonus_out, 1)
                dve.wait_ge(att_std, 2)
                link(nv.reciprocal(ATS, ATS))
                nv.scalar_tensor_tensor(q, q, par[:, PL_QN:PL_QN + 1], ATS[:, 0:HB, :], ALU.mult, ALU.mult).then_inc(att_qk, 1)
                nv.scalar_tensor_tensor(kk, kk, par[:, PL_KN:PL_KN + 1], ATS[:, HB, :], ALU.mult, ALU.mult).then_inc(att_qk, 1)
                at = 0
                for rnd, (t, heads) in enumerate(ROUNDS):
                    n, w = len(heads), P * (t + 1)
                    s = SCO.rearrange("p (a b) -> p a b", b=w)
                    wide = lambda a: a[:, 0:n].unsqueeze(2).broadcast_to([P, n, w])
                    mask = con[:, C_BAND:C_BAND + w] if t else con[:, C_CAUSAL:C_CAUSAL + P]
                    sink = par[:, PL_SINK + at:PL_SINK + at + n]
                    at += n
                    dve.wait_ge(sc_ready, rnd + 1)
                    if rnd:
                        dve.wait_ge(pt_ready, rnd)
                    link(nv.scalar_tensor_tensor(s, banks(2, 2, n, w), HD ** -0.5, mask.unsqueeze(1).broadcast_to([P, n, w]), ALU.mult, ALU.add))
                    link(nv.tensor_reduce(MX[:, 0:n], s, AX, ALU.max))
                    link(nv.tensor_tensor(MM[:, 0:n], MX[:, 0:n], sink, ALU.max))
                    link(nv.tensor_tensor(s, s, wide(MM), ALU.subtract))
                    nv.tensor_tensor(SK[:, 0:n], sink, MM[:, 0:n], ALU.subtract).then_inc(sc_max, 1)
                    dve.wait_ge(sc_exp, 2 * (rnd + 1))
                    link(nv.tensor_reduce(SUM[:, 0:n], s, AX, ALU.add))
                    link(nv.tensor_tensor(SUM[:, 0:n], SUM[:, 0:n], SK[:, 0:n], ALU.add))
                    link(nv.reciprocal(SUM[:, 0:n], SUM[:, 0:n]))
                    nv.tensor_tensor(s, s, wide(SUM), ALU.mult).then_inc(p_ready, 1)

            def rwkv_norm_and_retention(l):
                dve.wait_ge(ln_ss, 1)
                dve.wait_ge(y_out, 2)
                link(nv.scalar_tensor_tensor(Y, banks(4, 2, HB, T), -1.0 / HD, Y, ALU.mult, ALU.add))
                nv.tensor_tensor(X1, Y, Y, ALU.mult).then_inc(ln_in, 1)
                cos, sin = (con[:, c:c + T].unsqueeze(1).broadcast_to([P, HB, T]) for c in (C_COS, C_SIN))
                dve.wait_ge(act_taken, 18)
                for n, at in enumerate((B_RQ, B_RK)):
                    x = proj[:, at:at + HB, :]
                    dve.wait_ge(rot_ready, n + 1)
                    link(nv.tensor_tensor(XR, banks(2 + 2 * n, 2, HB, T), sin, ALU.mult))
                    link(nv.tensor_tensor(x, x, cos, ALU.mult))
                    nv.tensor_tensor(x, x, XR, ALU.add).then_inc(rot_out, 1)
                    dve.wait_ge(rot_out, n + 1)
                dve.wait_ge(ln_std, 1)
                link(nv.reciprocal(X2, X2))
                link(nv.tensor_tensor(Y, Y, X2, ALU.mult))
                for b in range(HB):
                    link(nv.tensor_scalar(Y[:, b, :], Y[:, b, :], par[:, PL_LG + b:PL_LG + b + 1], par[:, PL_LB + b:PL_LB + b + 1],
                                          ALU.mult, ALU.add))
                link(nv.tensor_tensor(Y, Y, r, ALU.add))
                nv.tensor_tensor(Y, Y, GT, ALU.mult).then_inc(ob_ready, 1)
                dve.wait_ge(dec_loaded, 16)
                for h in range(HEADS):
                    dve.wait_ge(rs_ready, h + 1)
                    nv.tensor_tensor(SM[:, h, :], PS[:, 2 + h % 2 + 2 * (h // 2 % 2), 0:3 * P], DEC[:, h, :], ALU.mult).then_inc(rs_out, 1)
                o, g = proj[:, B_RQ:B_RQ + HB, :], proj[:, B_RG:B_RG + HB, :]
                mix(l, 1, 0, 1)
                dve.wait_ge(oc_out, 1)
                nv.tensor_tensor(XR, o, o, ALU.mult).then_inc(oc_sq, 1)
                mix(l, 1, 1, 2)
                dve.wait_ge(oc_std, 1)
                link(nv.reciprocal(XR, XR))
                link(nv.tensor_tensor(o, o, XR, ALU.mult))
                nv.tensor_tensor(o, o, g, ALU.mult).then_inc(oc_ready, 1)
                mix(l, 1, 2, 4)

            def mix(l, br, lo, hi):
                for i in range(lo, hi):
                    q = Q_MIX[br][i]
                    gate = proj[:, B_GATE + KD * br + 2 * i:B_GATE + KD * br + 2 * i + 2, :]
                    out = hT[:, 2 * i:2 * i + 2, :]
                    dve.wait_ge(block_done, done(l, q))
                    ps = banks(q % 2, 1, 2, T)
                    if br == 0:
                        nv.tensor_tensor(out, ps, gate, ALU.mult).then_inc(dve_taken, 1)
                    else:
                        link(nv.tensor_tensor(gate, ps, gate, ALU.mult))
                        if i == 0:
                            dve.wait_ge(dve_taken, TAKEN[q - 1])
                        nv.tensor_tensor(out, out, gate, ALU.add).then_inc(dve_taken, 1)

            def residual(l, q0, n, blocks):
                for i in range(n):
                    dve.wait_ge(block_done, done(l, q0 + i))
                    x = xT[:, blocks * i:blocks * (i + 1), :]
                    nv.tensor_tensor(x, x, banks((q0 + i) % 2, 1, blocks, T), ALU.add).then_inc(dve_taken, 1)
                dve.wait_ge(dve_taken, TAKEN[q0 + n - 1])

            def ffn(l):
                for n in range(N_FFN // 2):
                    dve.wait_ge(block_done, done(l, Q_FFN + 2 * n + 1))
                    dve.wait_ge(act_taken, TAKEN[Q_FFN + 2 * n])
                    nv.tensor_tensor(HID[:, 2 * n:2 * n + 2, :], banks((Q_FFN + 1) % 2, 1, 2, T), SILU[:, n % 2, :].rearrange("p (a b) -> p a b", b=T),
                                     ALU.mult).then_inc(dve_taken, 1)

            dve.wait_ge(const_loaded, 4 * 16)
            with dve.Fori(0, LAYERS) as l:
                dve.wait_ge(par_loaded, 32)
                norm(1, PL_G1)
                rwkv_mix()
                rwkv_prep()
                attention()
                rwkv_chunk(l, 0)
                rwkv_chunk(l, 1)
                rwkv_norm_and_retention(l)
                mix(l, 2, 0, 4)
                residual(l, Q_OUT, N_OUT, 2)
                norm(2, PL_G2)
                ffn(l)
                residual(l, Q_DOWN, N_DOWN, 1)
                dve.sem_inc(layer_fin, 1)
                dve.wait_ge(layer_go, l + 1)
                dve.sem_inc(layer_joined, 1)
            second_vector(dve)


_NATURAL = ["w_ada_2", "w_in", "w_attn_o", "w_rwkv_o", "w_ret_o", "w_out", "w_ffn_gate", "w_ffn_up", "w_ffn_down",
            "w_in_2", "w_out_2", "hy_w1_2", "hy_w2_2", "hy_w3_2", "hy_deltas_2", "w_gate_2", "w_up_2", "w_down_2"]


def kernel(**inputs):
    import concourse.bacc as bacc
    from concourse.bass_utils import run_bass_kernel_spmd

    a = {n: np.asarray(v) for n, v in inputs.items()}
    arrays = {n: np.ascontiguousarray(a[n]) for n in _NATURAL}
    blocks = lambda m: np.ascontiguousarray(m.reshape(KD, P, -1).transpose(1, 0, 2))
    arrays["xT"] = blocks(a["x"][0].T)
    cond = np.zeros((P, KD, 64), a["c_2"].dtype)
    cond[:, :, 32] = a["c_2"].reshape(KD, P).T
    arrays["cond"] = cond
    arrays["ada_bias"] = columns(a["b_ada_2"][0])
    arrays["router"] = blocks(a["w_router_2"][0])
    arrays["layer_params"] = np.stack([pack_layer(a, l) for l in range(LAYERS)])
    arrays["layer_lora"] = np.stack([pack_lora(a, l) for l in range(LAYERS)])
    arrays["params_2"] = pack_second(a)
    arrays["constants"], arrays["decay"] = layer_constants()
    arrays["constants_2"] = second_constants()

    nc = bacc.Bacc("TRN2", target_bir_lowering=False, num_devices=1)
    io = {}
    for n, v in arrays.items():
        v = arrays[n] = np.ascontiguousarray(v)
        io[n] = nc.dram_tensor(f"in_{n}", v.shape, mybir.dt.from_np(v.dtype), kind="ExternalInput").ap()
    io["yT"] = nc.dram_tensor("out_yT", (D, T), F32, kind="ExternalOutput").ap()
    build(nc, io)
    r = run_bass_kernel_spmd(nc, [{f"in_{n}": v for n, v in arrays.items()}], core_ids=[0])
    return np.ascontiguousarray(r.results[0]["out_yT"].T)[None]
```

```python
import math
from contextlib import ExitStack

import numpy as np

import concourse.bass as bass
import concourse.mybir as mybir
from concourse.alu_op_type import AluOpType as ALU

F32 = mybir.dt.float32
U32 = mybir.dt.uint32
F32R = mybir.dt.float32r
ACT = mybir.ActivationFunctionType
AX = mybir.AxisListType.X

P = 128
T = 256
TT = T // P
D = 1024
KD = D // P
LAYERS = 2
HD = 64
HEADS = 8
HB = HEADS * HD // P
F_FF = 2816
FB = F_FF // P
W_IN = 7680
EPS = 1e-6
LNX_EPS = 64e-5
KAPPA = math.exp(-0.5)
NEG = -1e30

QKV, RW, RET0, GATE0 = 0, 768, 2560, 4608
IN_ORDER = [512, 1024, 1536, 2048, 0] + list(range(2560, W_IN, 512))
B_AK, B_AV, B_R, B_K, B_V, B_LORA, B_GD, B_AQ, B_RQ, B_RK, B_RV, B_RG, B_GATE = (
    0, 1, 2, 6, 10, 14, 15, 16, 20, 24, 28, 32, 36)
RW_BLOCKS = 14

H2, DH2 = 4, 128
EXPERTS, CAP, F_E = 16, 32, 2048
IN2 = 3600

RING, SLOT = 3, 4096
RING_E = 6
LAYER_SLOTS, TWO_SLOTS, EXPERT_SLOTS = 45, 12, 12
START, TWO_BLOCKS = RING, 20
N_PROJ, N_ADA, N_MIX, N_OUT, N_FFN, N_DOWN = 30, 6, 12, 4, 22, 8
Q_ADA = [30, 31, 32, 33, 36, 37]
Q_COLS = 38
Q_MIX = [[34, 35, 39, 40], [41, 42, 43, 44], [45, 46, 47, 48]]
Q_OUT = N_PROJ + N_ADA + 1 + N_MIX
Q_FFN = Q_OUT + N_OUT
Q_DOWN = Q_FFN + N_FFN
LAYER_BLOCKS = Q_DOWN + N_DOWN
S_ADA, S_MIX, S_OUT, S_FFN, S_DOWN = [15, 16, 17, 18, 20, 21], [19, 22, 23], 24, 26, 37
SLOT_DONE = [0] * LAYER_SLOTS
for _n in range(15):
    SLOT_DONE[_n] = 2 * _n + 2
for _s, _q in list(zip(S_ADA, Q_ADA)) + [(_s, _q[-1]) for _s, _q in zip(S_MIX, Q_MIX)]:
    SLOT_DONE[_s] = _q + 1
for _n in range(N_OUT // 2):
    SLOT_DONE[S_OUT + _n] = Q_OUT + 2 * _n + 2
for _n in range(N_FFN // 2):
    SLOT_DONE[S_FFN + _n] = Q_FFN + 2 * _n + 2
for _n in range(N_DOWN):
    SLOT_DONE[S_DOWN + _n] = Q_DOWN + _n + 1
BY_ACT = [q < N_PROJ or (Q_FFN <= q < Q_DOWN and (q - Q_FFN) % 2 == 0) for q in range(LAYER_BLOCKS)]
TAKEN = [sum(b == BY_ACT[q] for b in BY_ACT[:q + 1]) for q in range(LAYER_BLOCKS)]
ADA_AT = [{2: 0, 3: 1, 4: 2, 6: 3}, {1: 4, 4: 5}]
COLS_AT = [None, 6]

SPLIT_A = 8
SPLIT = list(range(SPLIT_A)) + list(range(S_OUT, LAYER_SLOTS))

C_ID, C_ONES, C_BD, C_PERM, C_DUP, C_COS, C_SIN = 0, 128, 256, 384, 512, 768, 1024
C_LVL = 1280
LEVELS = 7
C_GRAM = C_LVL + LEVELS * P
C_CAUSAL = C_GRAM + 512
C_BAND = C_CAUSAL + P
C_SEL = C_BAND + 2 * P
C_N = C_SEL + N_ADA
PL_G1, PL_G2, PL_QN, PL_KN, PL_MU, PL_W0, PL_A0, PL_KK, PL_KA, PL_RK, PL_LG, PL_LB, PL_SINK = (
    0, 8, 16, 17, 18, 32, 36, 40, 44, 48, 52, 56, 60)
PL_N = PL_SINK + 16
D_CS, D_CI, D_MASK, D_IOTA, D_Z, D_SEL, D_TOK, D_NT = 0, 1024, 2048, 3072, 3328, 3584, 4096, 4098
D_N = 4100
P2_GMIX, P2_GFFN, P2_GFIN, P2_BIN, P2_BG, P2_CQW, P2_CQB, P2_CHW, P2_CHB, P2_MN, P2_HBIAS, P2_HN, P2_HY = (
    0, 8, 16, 24, 52, 56, 80, 88, 124, 136, 140, 148, 152)
P2_N = 155

BESIDE_SOFTMAX = [(22, 24), (25, 26), (27, 28)]
BESIDE_COPY = [(24, 25), (26, 27), (28, 29)]

ROUNDS = [(0, [0, 2, 4, 6, 1, 3, 5, 7]), (1, [0, 2, 1, 3]), (1, [4, 6, 5, 7])]


def layer_constants():
    c = np.zeros((P, C_N), np.float32)
    p, f = np.arange(P)[:, None], np.arange(P)[None, :]
    c[:, C_ID:C_ID + P] = p == f
    c[:, C_ONES:C_ONES + P] = 1
    c[:, C_BD:C_BD + P] = p // HD == f // HD
    half = HD // 2
    same = p // HD == f // HD
    c[:, C_PERM:C_PERM + P] = np.where(same & (p == f + half), -1.0, 0) + np.where(same & (p == f - half), 1.0, 0)
    for kv in range(2):
        c[:, C_DUP + kv * P:C_DUP + (kv + 1) * P] = p == kv * HD + f % HD
    inv = (1.0 / (np.float32(10000.0) ** (np.arange(half, dtype=np.float32) * np.float32(2.0) / HD))).astype(np.float32)
    ang = np.arange(T, dtype=np.float32)[None, :] * inv[:, None]
    c[:, C_COS:C_COS + T] = np.tile(np.cos(ang), (P // half, 1))
    c[:, C_SIN:C_SIN + T] = np.tile(np.sin(ang), (P // half, 1))
    for n in range(LEVELS):
        m = 1 << n
        c[:, C_LVL + n * P:C_LVL + (n + 1) * P] = (p // (2 * m) == f // (2 * m)) & (p // m % 2 == 0) & (f // m % 2 == 1)
    for n, keep in enumerate([p > f, p <= f, p < f, p <= f]):
        c[:, C_GRAM + n * P:C_GRAM + (n + 1) * P] = keep
    c[:, C_CAUSAL:C_CAUSAL + P] = np.where(f <= p, 0, NEG)
    c[:, C_BAND:C_BAND + P] = np.where(f > p, 0, NEG)
    c[:, C_BAND + P:C_BAND + 2 * P] = np.where(f <= p, 0, NEG)
    c[:, C_SEL:C_SEL + N_ADA] = p % 32 == np.arange(N_ADA)[None, :]
    gamma = np.log1p(-np.power(2.0, -5.0 - np.arange(HEADS, dtype=np.float64)))[None, :, None]
    diff = np.arange(T)[None, None, :] - np.arange(P)[:, None, None]
    dec = np.where(diff >= 0, np.exp(gamma * np.maximum(diff, 0)), 0) * HD ** -0.5
    decay = np.concatenate([dec, dec[:, :, :P]], axis=2).astype(np.float32)
    return c, decay.reshape(P, HEADS * 3 * P)


def second_constants():
    c = np.zeros((P, D_N), np.float32)
    t, k = np.arange(T, dtype=np.float64), np.arange(T, dtype=np.float64) + 0.5
    ang = 2 * np.pi * t[:, None] * k[None, :] / (2 * T)
    fwd = np.stack([np.cos(ang), np.sin(ang)], axis=1)
    c[:, D_CS:D_CS + 1024] = fwd.reshape(TT, P, 512).transpose(1, 0, 2).reshape(P, 1024)
    inv = np.stack([np.cos(ang.T), np.sin(ang.T)], axis=1) / T
    c[:, D_CI:D_CI + 1024] = inv.reshape(TT, P, 512).transpose(1, 0, 2).reshape(P, 1024)
    s, q = np.arange(T)[:, None], np.arange(T)[None, :]
    masks = np.stack([s <= q, s >= q], axis=1).astype(np.float32)
    c[:, D_MASK:D_MASK + 1024] = masks.reshape(TT, P, 2, T).transpose(1, 2, 0, 3).reshape(P, 1024)
    c[:, D_IOTA:D_IOTA + T] = np.arange(T)
    f32 = np.float32
    tl = np.linspace(0.0, 1.0, T, dtype=f32)[:, None]
    w = (f32(2.0 * math.pi) * np.arange(T, dtype=f32)[:, None] / f32(T)).astype(f32)
    bands = np.linspace(1e-4, 15, 16, dtype=f32)[None, :]
    z = np.concatenate([tl, np.cos(bands * w), -np.sin(bands * w)], axis=-1)
    c[:33, D_Z:D_Z + T] = z.T
    for h in range(H2):
        c[h, D_SEL + h * P:D_SEL + (h + 1) * P] = 1
    c[:, D_TOK:D_TOK + TT] = np.arange(T).reshape(TT, P).T
    c[:, D_NT:D_NT + TT] = -tl[:, 0].reshape(TT, P).T
    return c


def columns(v):
    return np.ascontiguousarray(v).reshape(-1, P).T


def pack_layer(a, l):
    dup = lambda g: np.concatenate([g, g])[:, None]
    order = [h for _, heads in ROUNDS for h in heads]
    parts = [columns(a["norm1_g"][l]), columns(a["norm2_g"][l]), dup(a["attn_q_norm_g"][l]), dup(a["attn_k_norm_g"][l]),
             columns(a["rwkv_shift_mu"][l]), columns(a["rwkv_w0"][l]), columns(a["rwkv_a0"][l]), columns(a["rwkv_k_k"][l]),
             columns(a["rwkv_k_a"][l]), columns(a["rwkv_r_k"][l]), columns(a["rwkv_lnx_g"][l]), columns(a["rwkv_lnx_b"][l]),
             np.broadcast_to(a["attn_sinks"][l][order][None, :], (P, 16))]
    return np.concatenate(parts, axis=1)


def pack_lora(a, l):
    return np.concatenate([np.concatenate([a["rwkv_w2"][l], a["rwkv_a2"][l]], axis=0), a["rwkv_g2"][l]], axis=1)


def pack_second(a):
    rows = lambda v: np.concatenate([v, np.zeros((P - v.shape[0],) + v.shape[1:], v.dtype)], axis=0)
    b = a["b_in_2"][0]
    bias = np.concatenate([b[:2048], b[2064:]])
    parts = [columns(a["g_mix_2"][0]), columns(a["g_ffn_2"][0]), columns(a["g_final_2"]), columns(bias),
             rows(b[2048:2064].reshape(4, H2).T),
             columns(a["conv_qk_w_2"][0]), columns(a["conv_qk_b_2"][0]), columns(a["conv_hy_w_2"][0]), columns(a["conv_hy_b_2"][0]),
             columns(a["mlstm_norm_g_2"][0]), columns(a["hy_bias_2"][0]), columns(a["hyena_norm_g_2"][0]),
             rows(a["hy_b1_2"][0][:, None]), rows(a["hy_b2_2"][0][:, None]), rows(a["hy_freq_2"][0][:, None])]
    return np.concatenate(parts, axis=1)


def build(nc, io):
    ctx = ExitStack()
    with ctx:
        place = {}

        def sb(name, shape):
            t = ctx.enter_context(nc.sbuf_tensor(name, shape, F32))
            place[name] = nc.sbuf_base - 4 * math.prod(shape[1:])
            return t

        def rounded(name, within, column, shape):
            return nc.alloc_sbuf_tensor_at(name, [P] + shape, F32R, offset=place[within] + 4 * column)

        def sem(name):
            return ctx.enter_context(nc.semaphore(name))

        ring = sb("ring", [P, RING, SLOT])
        xT = sb("xT", [P, KD, T])
        hT = sb("hT", [P, KD, T])
        con = sb("con", [P, C_N])
        par = sb("par", [P, PL_N])
        lora = sb("lora", [P, 1024])
        proj = sb("proj", [P, 60, T])
        work = sb("work", [P, 16640])
        small = sb("small", [P, 64])
        cond = sb("cond", [P, KD, 64])
        mod = sb("mod", [P, 48])
        bias = sb("bias", [P, 4])
        PS = ctx.enter_context(nc.psum_tensor("PS", [P, 8, 512], F32))

        def w_(at, *dims):
            n = 1
            for d in dims:
                n *= d
            v = work[:, at:at + n]
            if len(dims) == 2:
                v = v.rearrange("p (a b) -> p a b", b=dims[1])
            if len(dims) == 3:
                v = v.rearrange("p (a b c) -> p a b c", b=dims[1], c=dims[2])
            if len(dims) == 4:
                v = v.rearrange("p (a b c d) -> p a b c d", b=dims[1], c=dims[2], d=dims[3])
            return v

        def banks(at, n, *dims):
            v = PS[:, at:at + n, :].rearrange("p a b -> p (a b)")
            if dims:
                m = 1
                for d in dims:
                    m *= d
                v = v[:, 0:m]
            if len(dims) == 2:
                v = v.rearrange("p (a b) -> p a b", b=dims[1])
            if len(dims) == 3:
                v = v.rearrange("p (a b c) -> p a b c", b=dims[1], c=dims[2])
            return v

        ident, ones, bd = con[:, C_ID:C_ID + P], con[:, C_ONES:C_ONES + P], con[:, C_BD:C_BD + P]
        perm = con[:, C_PERM:C_PERM + P]
        epsc, lnxc, onec = bias[:, 0:1], bias[:, 1:2], bias[:, 2:3]

        X1, X2, X3 = (w_(n * 1024, HB, T) for n in range(3))
        QT, W1S = w_(0, HEADS, 2, P), w_(2048, HEADS, P)
        KK, AT = w_(3072, HB, T), w_(4096, HB, T)
        AR = w_(5120, HB, TT, 2, P)
        GT, Y = w_(7168, HB, T), w_(8192, HB, T)
        GM = w_(9216, HEADS, 4 * P)
        SHIFT = w_(0, RW_BLOCKS, T)
        VTOK, BKT = w_(13312, TT, 512), w_(14336, 2, 512)
        RHS, U, ST = w_(2048, HEADS, HD), w_(2560, HEADS, HD), w_(15872, HB, HD)
        MID, SC, MIDE = small[:, 0:8].rearrange("p (a b) -> p a b", b=TT), small[:, 8:12], small[:, 12:16]
        MX, MM, SK, SUM = small[:, 16:24], small[:, 24:32], small[:, 32:40], small[:, 40:48]
        ATS, SCO, PT = w_(9216, 5, T), w_(9216 + 1280, 1024), w_(9216 + 2304, HEADS, P)
        KDUP, VATT = w_(9216 + 3328, 2, T), w_(9216 + 3840, TT, P)
        DEC, SM = w_(9216, HEADS, 3 * P), w_(3072, HEADS, 3 * P)
        GATED = w_(6144, HB, T)
        VRET, XR = w_(13312, TT, 512), w_(14336, HB, T)
        SQ, STD, RSTD = w_(5120, KD, T), w_(0, T), w_(256, T)
        HID = proj[:, 0:FB, :]
        SILU = proj[:, 24:28, :].rearrange("p a b -> p (a b)").rearrange("p (a b) -> p a b", b=512)
        high_a, high_f = rounded("high_a", "proj", 28 * T, [2, SLOT]), rounded("high_f", "work", 8192, [2, SLOT])
        ring_low = rounded("ring_low", "ring", 0, [RING, SLOT])
        XH_A, XL_A = rounded("xh_a", "work", 9216, [KD, T]), rounded("xl_a", "work", 11264, [KD, T])
        XH_F, hT_low = rounded("xh_f", "work", 3072, [KD, T]), rounded("hT_low", "hT", 0, [KD, T])
        HID_H, HID_low = rounded("hid_h", "proj", 28 * T, [FB, T]), rounded("hid_low", "proj", 0, [FB, T])

        def width(n):
            return FB * P if n >= S_DOWN else SLOT

        def high(n):
            tile, first = (high_a, 0) if n < S_OUT else (high_f, S_OUT)
            return tile[:, (n - first) % 2, :]

        mod_rows = w_(15360, 512)
        MOD2 = mod[:, :].rearrange("p (l b n) -> p l n b", l=LAYERS, n=4)

        ring_full = [sem(f"ring_full{n}") for n in range(RING_E)]
        block_done = sem("block_done")
        const_loaded, par_loaded = sem("const_loaded"), sem("par_loaded")
        bias_set, slot_freed = sem("bias_set"), sem("slot_freed")
        layer_go, layer_joined = sem("layer_go"), sem("layer_joined")

        names = """sq_ready ss_ready std_ready h_ready act_taken dve_taken
            z_ready lora_in lora_done lora_out kk_sq kk_ss kk_std cum_ready exps_ready gram_in bonus_in bonus_ss
            bonus_out tok_ready tok_out gm_zero pool_made gram_ready gram_taken qt_ready w1_ready w1_masked dq_ready
            rhs_ready rhs_out u_ready u_out y_ready y_out s_ready st_ready ln_in ln_ss ln_std ob_ready
            att_sq att_ss att_std att_qk att_tr att_kv sc_ready sc_max sc_exp p_ready pt_ready pt_out oa_ready oa_out
            rot_ready rot_out vr_ready vr_out dec_loaded rs_ready rs_out oc_psum oc_out oc_sq oc_ss oc_std oc_ready
            high_ready low_dve low_pool vec_order layer_fin""".split()
        L = {n: sem(n) for n in names}
        (sq_ready, ss_ready, std_ready, h_ready, act_taken, dve_taken,
         z_ready, lora_in, lora_done, lora_out, kk_sq, kk_ss, kk_std, cum_ready, exps_ready, gram_in, bonus_in, bonus_ss,
         bonus_out, tok_ready, tok_out, gm_zero, pool_made, gram_ready, gram_taken, qt_ready, w1_ready, w1_masked, dq_ready,
         rhs_ready, rhs_out, u_ready, u_out, y_ready, y_out, s_ready, st_ready, ln_in, ln_ss, ln_std, ob_ready,
         att_sq, att_ss, att_std, att_qk, att_tr, att_kv, sc_ready, sc_max, sc_exp, p_ready, pt_ready, pt_out, oa_ready, oa_out,
         rot_ready, rot_out, vr_ready, vr_out, dec_loaded, rs_ready, rs_out, oc_psum, oc_out, oc_sq, oc_ss, oc_std, oc_ready,
         high_ready, low_dve, low_pool, vec_order, layer_fin) = (L[n] for n in names)
        layer_sems = range(sq_ready.num, layer_fin.num + 1)
        assert sorted(s.num for s in L.values()) == list(layer_sems)

        def done(l, q):
            return START + LAYER_BLOCKS * l + q + 1

        def full(l, n):
            return 32 * (LAYER_SLOTS // RING * l + n // RING + 1)

        def every_other(x, lev, odd):
            m = 1 << lev
            if len(x.shape) == 2:
                return x.rearrange("p (a s m) -> p a s m", s=2, m=m)[:, :, odd, :]
            return x.rearrange("p u (a s m) -> p u a s m", s=2, m=m)[:, :, :, odd, :]

        def hrow(h):
            return slice(HD * (h % 2), HD * (h % 2) + HD)

        c2 = w_(12288, D_N)
        p2 = w_(12288 + D_N, P2_N)
        wrt = lora[:, 256:384].rearrange("p (k e) -> p k e", e=EXPERTS)
        hyw1, hyw2 = lora[0:33, 384:448], lora[0:64, 448:512]
        ARG, TRN = lora[0:64, 512:768], lora[0:64, 768:1024]
        CS, CI = (c2[:, c:c + 1024].rearrange("p (a s n) -> p a s n", s=2, n=T) for c in (D_CS, D_CI))
        MASK2 = c2[:, D_MASK:D_MASK + 1024]
        FILT, KF = w_(0, TT, 4, 512), w_(4096, TT, 2, 2, 512)
        HYW3, DELTA = w_(8192, 2048), w_(10240, 2048)
        YF = w_(10240, TT, 2, 512)
        TMP = w_(8192, 4, 512)
        WIN = proj[:, 56:60, :].rearrange("p a b -> p (a b)").rearrange("p (a b) -> p a b", b=512)
        ZTOK = WIN
        E2, EMS, NUM = w_(0, 2, TT, T), w_(1024, 2, T), w_(1536, 2, T)
        HS2, LF, BB = w_(2048, H2, T), w_(3072, 2, T), w_(3584, 2, T)
        VT2 = proj[:, 48:52, :].rearrange("p a b -> p (a b)").rearrange("p (a b) -> p a b", b=512)
        G4 = proj[:, 52:56, :]
        AA, NM, EMR, ZER = (proj[:, b:b + 2, :] for b in (0, 2, 4, 6))
        ACOL = small[:, 0:16].rearrange("p (d t h) -> p d t h", t=TT, h=H2)
        gs1, gs2 = small[:, 16:24], small[:, 24:32]
        QK2, HX2 = proj[:, 28:36, :], proj[:, 36:48, :]
        tok_high, tok_low = rounded("tok_high", "proj", 0, [TT, D]), rounded("tok_low", "proj", 49 * T, [TT, D])
        XS = proj[:, 8:24, :].rearrange("p e (k s) -> p e k s", s=CAP)
        XSE = proj[:, 24, :].rearrange("p (k s) -> p k s", s=CAP)
        PICK = rounded("pick", "proj", 25 * T, [TT, 512])
        GE = proj[:, 29, :]
        flat = lambda a: proj[:, a:a + 2, :].rearrange("p a b -> p (a b)")
        HSE, HE, HTE, YE = flat(32), flat(34), flat(36), flat(38)
        AFF = proj[0:EXPERTS, 40, :]
        DIAG = flat(42)
        LOG = proj[:, 44, 0:32].rearrange("p (t e) -> p t e", e=EXPERTS)
        VAL, IDXU, IDXF = proj[0:EXPERTS, 45, 0:32], proj[0:EXPERTS, 45, 32:64], proj[0:EXPERTS, 45, 64:96]
        REP = proj[0:EXPERTS, 46, :].rearrange("p (a r s) -> p a r s", r=4, s=CAP)
        IG = proj[:, 47, 0:32].rearrange("p (a e) -> p a e", e=EXPERTS)
        ST4 = proj[:, 47, 32:64]
        ZERO = proj[:, 48, 0:P]

        SQ2, STD2, RSTD2 = proj[:, 48:56, :], proj[:, 40, :], proj[:, 41, :]
        E2F = w_(0, 4, T)
        more_slots = w_(0, RING_E - RING, SLOT)

        def expert_slot(n):
            n %= RING_E
            return ring[:, n, :] if n < RING else more_slots[:, n - RING, :]

        def expert_full(e, n):
            base = FULLE if n % RING_E < RING else 0
            return base + 32 * (EXPERT_SLOTS // RING_E) * e + 32 * (n // RING_E + 1)


        names2 = """two_loaded f_hid f_arg f_sin f_abs f_win f_h f_filt f_sum kf_ready kf_out
            sq2 ss2 std2 h2_ready act2 dve2 conv_ready conv_act gate_rows ln_rows rows_ready em_rows
            m_tr m_out m_s m_em m_emo m_arg m_exp m_w m_num m_h
            z_tr z_out u2_ready yf_ready yt_ready z_ready2 r_sq r_ss r_std cat_ready
            tok2 tok2_out tok2_low rt_logit rt_max rt_exp rt_prob rt_tr topk_done ix_ready ix_out diag_ready row_ready pick_ready xs_psum xs_out
            expert_slots xs_staged ge_ready hs_ready he_ready ht_ready ht_out ye_ready scattered
            moe_sum vec2 out_done""".split()
        S = {n: sem(n) for n in names2}
        (two_loaded, f_hid, f_arg, f_sin, f_abs, f_win, f_h, f_filt, f_sum, kf_ready, kf_out,
         sq2, ss2, std2, h2_ready, act2, dve2, conv_ready, conv_act, gate_rows, ln_rows, rows_ready, em_rows,
         m_tr, m_out, m_s, m_em, m_emo, m_arg, m_exp, m_w, m_num, m_h,
         z_tr, z_out, u2_ready, yf_ready, yt_ready, z_ready2, r_sq, r_ss, r_std, cat_ready,
         tok2, tok2_out, tok2_low, rt_logit, rt_max, rt_exp, rt_prob, rt_tr, topk_done, ix_ready, ix_out, diag_ready, row_ready, pick_ready, xs_psum, xs_out,
         expert_slots, xs_staged, ge_ready, hs_ready, he_ready, ht_ready, ht_out, ye_ready, scattered,
         moe_sum, vec2, out_done) = (S[n] for n in names2)
        BASE2 = START + LAYERS * LAYER_BLOCKS
        FULL2 = 32 * LAYERS * LAYER_SLOTS // RING
        FULLE = FULL2 + 32 * TWO_SLOTS // RING
        IN2_ORDER = [(0, 512), (512, 512), (2048, 16), (1024, 512), (2064, 512), (2576, 512), (3088, 512), (1536, 512)]
        IN2_BLOCKS = [0, 4, None, 8, 16, 20, 24, 12]

        def second_sync(sp, load, by_rows):
            for n in range(TWO_SLOTS):
                if n < RING:
                    sp.wait_ge(block_done, BASE2 - (RING - 1 - n))
                else:
                    m = n - RING + 1
                    sp.wait_ge(block_done, BASE2 + (2 * m if m <= 8 else 16 + m - 8))
                s = n % RING
                if n < 8:
                    at, cols = IN2_ORDER[n]
                    by_rows(io["w_in_2"][0][:, at:at + cols], s, cols)
                else:
                    by_rows(io["w_out_2"][0][:, 256 * (n - 8):256 * (n - 7)], s, 256)
            sp.wait_ge(block_done, BASE2 + TWO_BLOCKS)
            with sp.Fori(0, EXPERTS) as e:
                for n in range(EXPERT_SLOTS):
                    sp.wait_ge(expert_slots, EXPERT_SLOTS * e + EXPERT_SLOTS + n - RING_E + 1)
                    sp.sem_inc(slot_freed, 1)
                    if n < 8:
                        w = io[("w_gate_2", "w_up_2")[n // 4]][0][e]
                        rows, cols = 2 * P, F_E
                        w = w[rows * (n % 4):rows * (n % 4 + 1), :]
                    else:
                        cols = D
                        w = io["w_down_2"][0][e][4 * P * (n - 8):4 * P * (n - 7), :]
                    by_rows(w, n % RING_E, cols, expert_slot(n))
            sp.wait_ge(h2_ready, 3)
            sp.dma_start(io["yT"].rearrange("(k p) t -> p k t", p=P), hT[:, :, :]).then_inc(out_done, 16)
            sp.wait_ge(out_done, 16)

        def second_pool(pool):
            pool.wait_ge(layer_go, LAYERS)

        def second_tensor(pe):
            nt = nc.tensor

            def norm_sums(n):
                for k in range(KD):
                    if k % 2 == 0:
                        pe.wait_ge(sq2, 4 * (n - 1) + k // 2 + 1)
                    mm = nt.matmul(PS[:, 2, 0:T], ones, SQ2[:, k, :], start=(k == 0), stop=(k == KD - 1))
                mm.then_inc(ss2, 1)

            def four_sums(bank, src, signal):
                for n in range(2):
                    mm = nt.matmul(PS[:, bank + n, :], ones, src[:, 2 * n:2 * n + 2, :].rearrange("p a b -> p (a b)"), start=True, stop=True)
                mm.then_inc(signal, 1)

            def product(q, weight, moving, kn, n_blocks=2, m=P, hyena_at=None):
                if q >= 2:
                    if q - 2 < 16:
                        pe.wait_ge(act2, q - 1)
                    else:
                        pe.wait_ge(dve2, q - 17)
                for b in range(n_blocks):
                    for k in range(kn):
                        if b == 0 and k == hyena_at:
                            pe.wait_ge(cat_ready, 2)
                        mm = nt.matmul(PS[0:m, q % 2, T * b:T * (b + 1)], weight(b, k), moving(k), start=(k == 0), stop=(k == kn - 1))
                mm.then_inc(block_done, 1)

            def project(lo, hi):
                for q in range(lo, hi):
                    n, half = q // 2, q % 2
                    s, cols = n % RING, IN2_ORDER[n][1]
                    if half == 0:
                        pe.wait_ge(ring_full[s], FULL2 + 32 * (n // RING + 1))
                    m = cols // 4
                    product(q, lambda b, k: ring[:, s, cols * k + m * (2 * half + b):cols * k + m * (2 * half + b + 1)],
                            lambda k: hT[:, k, :], KD, 2, m)

            def filter_tiles(lo, hi):
                for i in range(lo, hi):
                    c, t = i // 2, i % 2
                    if i >= 2:
                        pe.wait_ge(f_filt, i - 1)
                    nt.matmul(PS[:, 4 + i % 2, :], ARG[:, P * t:P * (t + 1)], HYW3[0:64, 512 * c:512 * (c + 1)], start=True, stop=True)\
                        .then_inc(f_h, 1)

            def filter_spectra(lo, hi):
                for i in range(lo, hi):
                    o, s, kt = i // 4, i // 2 % 2, i % 2
                    if i >= 4:
                        pe.wait_ge(kf_out, i - 3)
                    for t in range(TT):
                        mm = nt.matmul(PS[:, 4 + i % 4, :], CS[:, t, s, P * kt:P * (kt + 1)], FILT[:, t, 2 * o + s, :], start=(t == 0), stop=(t == 1))
                    mm.then_inc(kf_ready, 1)

            def project_beside_filters():
                pe.wait_ge(h2_ready, 1)
                project(0, 1)
                pe.wait_ge(two_loaded, 7 * 16)
                nt.matmul(PS[0:64, 3, 0:T], hyw1, c2[0:33, D_Z:D_Z + T], start=True, stop=True).then_inc(f_hid, 1)
                project(1, 2)
                pe.wait_ge(f_sin, 1)
                nt.matmul(PS[0:64, 3, T:2 * T], hyw2, ARG, start=True, stop=True).then_inc(f_hid, 1)
                project(2, 3)
                pe.wait_ge(f_sin, 2)
                for n in range(4):
                    filter_tiles(2 * n, 2 * n + 2)
                    project(3 + n, 4 + n)
                pe.wait_ge(f_sum, 2)
                filter_spectra(0, 4)
                project(7, 8)
                filter_spectra(4, 8)

            def mlstm():
                pe.wait_ge(act2, 8)
                pe.wait_ge(kf_out, 8)
                for t in range(TT):
                    for b in range(H2):
                        mm = nt.transpose(PS[:, 6 + t, P * b:P * (b + 1)], proj[:, 8 + b, P * t:P * (t + 1)], ident)
                mm.then_inc(m_tr, 1)
                project(8, 9)
                pe.wait_ge(rows_ready, 2)
                for d in range(2):
                    for t in range(TT):
                        at = 4 * (2 * d + t)
                        mm = nt.transpose(PS[:, 5, at:at + 4], AA[0:H2, d, P * t:P * (t + 1)], ident[0:H2, 0:H2])
                mm.then_inc(m_tr, 1)
                pe.wait_ge(em_rows, 1)
                pe.wait_ge(conv_act, 1)
                pe.wait_ge(m_out, 3)
                for h in range(H2):
                    if h:
                        pe.wait_ge(m_h, h)
                    sel = c2[0:H2, D_SEL + P * h:D_SEL + P * (h + 1)]
                    nt.matmul(PS[:, 3, :], sel, NM[0:H2, :, :].rearrange("p a b -> p (a b)"), start=True, stop=True)
                    nt.matmul(PS[:, 4, :], sel, EMR[0:H2, :, :].rearrange("p a b -> p (a b)"), start=True, stop=True).then_inc(m_em, 1)
                    for j in range(TT):
                        mm = nt.matmul(PS[:, 2, T * j:T * (j + 1)], QK2[:, 4 + h, P * j:P * (j + 1)], QK2[:, h, :], start=True, stop=True)
                    mm.then_inc(m_s, 1)
                    project(9 + 2 * h, 10 + 2 * h)
                    pe.wait_ge(m_w, h + 1)
                    for d in range(2):
                        for j in range(TT):
                            nt.matmul(PS[:, 5, T * d:T * (d + 1)], VT2[:, j, P * h:P * (h + 1)], E2[:, d, j, :], start=(j == 0), stop=(j == 1))
                    for d in range(2):
                        for j in range(TT):
                            mm = nt.matmul(PS[:, 6, T * d:T * (d + 1)], ones, E2[:, d, j, :], start=(j == 0), stop=(j == 1))
                    mm.then_inc(m_num, 1)
                    if h < H2 - 1:
                        project(10 + 2 * h, 11 + 2 * h)

            def hyena():
                for o in range(2):
                    if o:
                        pe.wait_ge(z_ready2, 1)
                    else:
                        pe.wait_ge(m_h, H2)
                    for t in range(TT):
                        for b in range(4):
                            mm = nt.transpose(PS[:, 6 + t, P * b:P * (b + 1)], HX2[:, 8 + b, P * t:P * (t + 1)], ident)
                    mm.then_inc(z_tr, 1)
                    if o == 0:
                        pe.wait_ge(r_sq, 1)
                        four_sums(2, E2F, r_ss)
                        pe.wait_ge(r_std, 1)
                    pe.wait_ge(z_out, 2 * (o + 1))
                    for kt in range(TT):
                        for s in range(2):
                            for t in range(TT):
                                mm = nt.matmul(PS[:, 2 + 2 * kt + s, :], CS[:, t, s, P * kt:P * (kt + 1)], ZTOK[:, t, :], start=(t == 0), stop=(t == 1))
                        mm.then_inc(u2_ready, 1)
                    for b, n in ([(b, n) for n in range(4) for b in (0, 2)] + [(b, n) for b in (1, 3) for n in range(4)]):
                        if b == 0 and n % 2 == 0:
                            pe.wait_ge(yf_ready, TT * o + n // 2 + 1)
                        mm = nt.matmul(PS[:, 6 + b // 2, T * (b % 2):T * (b % 2 + 1)], YF[:, n // 2, n % 2, P * b:P * (b + 1)],
                                       CI[:, n // 2, n % 2, :], start=(n == 0), stop=(n == 3))
                    mm.then_inc(yt_ready, 1)
                pe.wait_ge(r_sq, 2)
                four_sums(2, E2F, r_ss)

            def out():
                pe.wait_ge(cat_ready, 1)
                for n in range(4):
                    s = (8 + n) % RING
                    pe.wait_ge(ring_full[s], FULL2 + 32 * ((8 + n) // RING + 1))
                    product(16 + n, lambda b, k: ring[:, s, 256 * k + P * b:256 * k + P * (b + 1)], lambda k: hT[:, k, :], KD,
                            hyena_at=4 if n == 0 else None)

            def route():
                pe.wait_ge(h2_ready, 2)
                for t in range(TT):
                    for k in range(KD):
                        mm = nt.matmul(PS[:, 2, EXPERTS * t:EXPERTS * (t + 1)], hT[:, k, P * t:P * (t + 1)], wrt[:, k, :],
                                       start=(k == 0), stop=(k == KD - 1))
                mm.then_inc(rt_logit, 1)
                for i in range(4):
                    t, g = i // 2, i % 2
                    for b in range(4):
                        mm = nt.transpose(PS[:, 4 + i, P * b:P * (b + 1)], hT[:, 4 * g + b, P * t:P * (t + 1)], ident)
                    mm.then_inc(tok2, 1)
                pe.wait_ge(rt_prob, 1)
                for t in range(TT):
                    mm = nt.transpose(PS[0:EXPERTS, 3, P * t:P * (t + 1)], LOG[:, t, :], ident)
                mm.then_inc(rt_tr, 1)
                pe.wait_ge(topk_done, 1)
                for a in range(2):
                    mm = nt.matmul(PS[:, 2, EXPERTS * a:EXPERTS * (a + 1)], REP[:, a, :, :].rearrange("p a b -> p (a b)"),
                                   ident[0:EXPERTS, 0:EXPERTS], start=True, stop=True)
                mm.then_inc(ix_ready, 1)
                pe.wait_ge(diag_ready, 1)
                nt.matmul(PS[:, 3, :], ones[0:EXPERTS, :], DIAG[0:EXPERTS, :], start=True, stop=True).then_inc(row_ready, 1)
                pe.wait_ge(pick_ready, 1)
                pe.wait_ge(tok2_low, 4)
                for k in range(KD):
                    if k >= 4:
                        pe.wait_ge(xs_out, k - 3)
                    for n in range(2 * TT):
                        part, t = (tok_high, tok_low)[n % 2], n // 2
                        mm = nt.matmul(PS[:, 4 + k % 4, :], part[:, t, P * k:P * (k + 1)], PICK[:, t, :], start=(n == 0), stop=(n == 2 * TT - 1))
                    mm.then_inc(xs_psum, 1)

            def experts():
                pe.wait_ge(xs_out, KD)
                pe.wait_ge(pick_ready, 1)
                pe.wait_ge(dve2, 4)
                YB = [6, 7, 0, 1]
                for b in YB:
                    nt.matmul(PS[:, b, :], ZERO, con[:, 0:512], start=True, stop=False, skip_group_check=True)
                pe.sem_inc(scattered, 1)
                with pe.Fori(0, EXPERTS) as e:
                    pe.wait_ge(xs_staged, e + 1)
                    for n in range(8):
                        w = expert_slot(n)
                        pe.wait_ge(ring_full[n % RING_E], expert_full(e, n))
                        for kk in range(2):
                            k = 2 * (n % 4) + kk
                            for j in range(4):
                                mm = nt.matmul(PS[32 * j:32 * j + 32, 2 + n // 4, :], XSE[:, k, :],
                                               w[:, F_E * kk + 512 * j:F_E * kk + 512 * (j + 1)], start=(k == 0), stop=(k == KD - 1))
                        mm.then_inc(expert_slots, 1)
                    pe.wait_ge(he_ready, e + 1)
                    for c in range(4):
                        mm = nt.transpose(PS[:, 4, P * c:P * (c + 1)], HE[:, P * c:P * (c + 1)], ident)
                    mm.then_inc(ht_ready, 1)
                    pe.wait_ge(ht_out, e + 1)
                    for n in range(8, 12):
                        w, d = expert_slot(n), n - 8
                        pe.wait_ge(ring_full[n % RING_E], expert_full(e, n))
                        for c in range(4):
                            for dh in range(2):
                                g = 2 * dh + c % 2
                                mm = nt.matmul(PS[32 * g:32 * g + 32, 5, :], HTE[:, P * c + 32 * d:P * c + 32 * (d + 1)],
                                               w[:, D * c + 512 * dh:D * c + 512 * (dh + 1)],
                                               start=(d == 0 and c < 2), stop=(d == 3 and c >= 2))
                        mm.then_inc(expert_slots, 1)
                    pe.wait_ge(ye_ready, e + 1)
                    for b in range(KD):
                        o = slice(64 * (b // 4), 64 * (b // 4) + 64)
                        mm = nt.matmul(PS[:, YB[b // 2], T * (b % 2):T * (b % 2 + 1)], YE[o, P * (b % 4):P * (b % 4 + 1)], GE[o, :],
                                       start=False, stop=False, skip_group_check=True)
                    mm.then_inc(scattered, 1)

            norm_sums(1)
            project_beside_filters()
            mlstm()
            hyena()
            out()
            pe.sem_inc(expert_slots, EXPERT_SLOTS)
            norm_sums(2)
            route()
            experts()
            norm_sums(3)

        def second_scalar(act):
            na = nc.scalar

            def root(n):
                act.wait_ge(ss2, n)
                na.activation(STD2, PS[:, 2, 0:T], ACT.Sqrt, bias=epsc, scale=1.0 / D).then_inc(std2, 1)

            def four_roots(n):
                act.wait_ge(r_ss, n)
                na.activation(E2F.rearrange("p a b -> p (a b)"), banks(2, 2), ACT.Sqrt, bias=epsc, scale=1.0 / P).then_inc(r_std, 1)

            act.wait_ge(par_loaded, 32 * (LAYERS + 1))
            act.dma_start(c2, io["constants_2"]).then_inc(two_loaded, 16)
            act.dma_start(wrt, io["router"]).then_inc(two_loaded, 16)
            act.dma_start(hyw1, io["hy_w1_2"][0]).then_inc(two_loaded, 16)
            act.dma_start(hyw2, io["hy_w2_2"][0]).then_inc(two_loaded, 16)
            act.dma_start(HYW3[0:64, :], io["hy_w3_2"][0]).then_inc(two_loaded, 16)
            act.dma_start(DELTA, io["hy_deltas_2"].partition_broadcast(P).rearrange("p o n -> p (o n)")).then_inc(two_loaded, 16)

            def proj_out(lo, hi):
                for q in range(lo, hi):
                    act.wait_ge(block_done, BASE2 + q + 1)
                    at = IN2_BLOCKS[q // 2]
                    for b in range(2):
                        if at is None:
                            n = 2 * (q % 2) + b
                            ins = na.activation(G4[0:H2, n, :], PS[0:H2, q % 2, T * b:T * (b + 1)], ACT.Identity,
                                                bias=p2[0:H2, P2_BG + n:P2_BG + n + 1])
                        else:
                            n = at + 2 * (q % 2) + b
                            ins = na.activation(proj[:, n, :], PS[:, q % 2, T * b:T * (b + 1)], ACT.Sigmoid if at == 12 else ACT.Identity,
                                                bias=p2[:, P2_BIN + n:P2_BIN + n + 1])
                    ins.then_inc(act2, 1)

            def filter_windows(lo, hi):
                for i in range(lo, hi):
                    c, t = i // 2, i % 2
                    if i >= 2:
                        act.wait_ge(f_filt, i - 1)
                    na.activation(WIN[:, i % 2, :], DELTA[:, 512 * c:512 * (c + 1)], ACT.Exp, scale=c2[:, D_NT + t:D_NT + t + 1]).then_inc(f_win, 1)

            def filter_spectra(lo, hi):
                for i in range(lo, hi):
                    o, s, kt = i // 4, i // 2 % 2, i % 2
                    act.wait_ge(kf_ready, i + 1)
                    na.activation(KF[:, kt, o, s, :], PS[:, 4 + i % 4, :], ACT.Copy).then_inc(kf_out, 1)

            root(1)
            for n in range(2):
                proj_out(n, n + 1)
                act.wait_ge(f_arg, n + 1)
                na.activation(ARG, ARG, ACT.Sin).then_inc(f_sin, 1)
            proj_out(2, 3)
            act.wait_ge(f_abs, 1)
            for n in range(4):
                filter_windows(2 * n, 2 * n + 2)
                proj_out(3 + n, 4 + n)
            filter_spectra(0, 4)
            proj_out(7, 8)
            filter_spectra(4, 8)
            act.wait_ge(conv_ready, 1)
            na.activation(QK2, QK2, ACT.Silu).then_inc(conv_act, 1)
            act.wait_ge(gate_rows, 1)
            na.activation(LF[0:H2], LF[0:H2], ACT.Exp, scale=-1.0).then_inc(ln_rows, 1)
            act.wait_ge(ln_rows, 1)
            na.activation(LF[0:H2], LF[0:H2], ACT.Ln, bias=onec[0:H2, :]).then_inc(ln_rows, 1)
            act.wait_ge(m_tr, 1)
            for t in range(TT):
                na.activation(VT2[:, t, :], PS[:, 6 + t, :], ACT.Copy).then_inc(m_out, 1)
            proj_out(8, 9)
            act.wait_ge(m_tr, 2)
            na.activation(small[:, 0:16], PS[:, 5, 0:16], ACT.Copy).then_inc(m_out, 1)
            act.wait_ge(rows_ready, 2)
            na.activation(EMR[0:H2], EMR[0:H2], ACT.Exp, scale=-1.0).then_inc(em_rows, 1)
            for h in range(H2):
                act.wait_ge(m_em, h + 1)
                na.activation(EMS.rearrange("p a b -> p (a b)"), PS[:, 4, :], ACT.Copy).then_inc(m_emo, 1)
                act.wait_ge(m_arg, h + 1)
                na.activation(E2, E2, ACT.Exp).then_inc(m_exp, 1)
                proj_out(9 + 2 * h, min(11 + 2 * h, 16))
            for o in range(2):
                act.wait_ge(z_tr, o + 1)
                for t in range(TT):
                    na.activation(ZTOK[:, t, :], PS[:, 6 + t, :], ACT.Copy).then_inc(z_out, 1)
                if o == 0:
                    four_roots(1)
            four_roots(2)
            root(2)
            for i in range(4):
                t, g = i // 2, i % 2
                act.wait_ge(tok2, i + 1)
                na.activation(tok_high[:, t, 512 * g:512 * (g + 1)], PS[:, 4 + i, :], ACT.Copy).then_inc(tok2_out, 1)
            act.wait_ge(rt_max, 1)
            na.activation(LOG, LOG, ACT.Exp).then_inc(rt_exp, 1)
            act.wait_ge(ix_ready, 1)
            na.activation(IG.rearrange("p a b -> p (a b)"), PS[:, 2, 0:32], ACT.Copy).then_inc(ix_out, 1)
            for k in range(KD):
                act.wait_ge(xs_psum, k + 1)
                na.activation(XS[:, :, k, :], banks(4 + k % 4, 1, EXPERTS, CAP), ACT.Copy).then_inc(xs_out, 1)
            with act.Fori(0, EXPERTS) as e:
                act.wait_ge(expert_slots, EXPERT_SLOTS * e + EXPERT_SLOTS + 4)
                na.activation(HSE, PS[:, 2, :], ACT.Silu).then_inc(hs_ready, 1)
                act.wait_ge(ht_ready, e + 1)
                na.activation(HTE, PS[:, 4, :], ACT.Copy).then_inc(ht_out, 1)
            root(3)

        def second_vector(dve):
            nv = nc.vector
            count = [0]

            def link(ins):
                count[0] += 1
                ins.then_inc(vec2, 1)
                dve.wait_ge(vec2, count[0])

            def square(n):
                x = slice(2 * n, 2 * n + 2)
                nv.tensor_tensor(SQ2[:, x, :], xT[:, x, :], xT[:, x, :], ALU.mult).then_inc(sq2, 1)

            def root(n):
                dve.wait_ge(std2, n)
                link(nv.reciprocal(RSTD2, STD2))

            def norm(n, gain, shift):
                root(n)
                for k in range(KD):
                    ins = nv.scalar_tensor_tensor(hT[:, k, :], xT[:, k, :], gain[:, k:k + 1], RSTD2, ALU.mult, ALU.mult)
                link(ins)
                for k in range(KD):
                    ins = nv.tensor_scalar(hT[:, k, :], hT[:, k, :], mod[:, shift + k:shift + k + 1], None, ALU.add)
                ins.then_inc(h2_ready, 1)

            def sine_argument(n):
                dve.wait_ge(f_hid, n + 1)
                link(nv.tensor_scalar(ARG, PS[0:64, 3, T * n:T * (n + 1)], p2[0:64, P2_HY + n:P2_HY + n + 1], p2[0:64, P2_HY + 2:P2_HY + 3], ALU.add, ALU.mult))
                big = 1.5 * 2.0 ** 23
                two_pi = 2 * math.pi
                c1 = 6.28125
                link(nv.tensor_scalar(TRN, ARG, 1 / two_pi, None, ALU.mult))
                link(nv.tensor_scalar(TRN, TRN, big, None, ALU.add))
                link(nv.tensor_scalar(TRN, TRN, -big, None, ALU.add))
                link(nv.scalar_tensor_tensor(ARG, TRN, -c1, ARG, ALU.mult, ALU.add))
                link(nv.scalar_tensor_tensor(ARG, TRN, -(two_pi - c1), ARG, ALU.mult, ALU.add))
                pi = float(np.nextafter(np.float32(math.pi), np.float32(0)))
                nv.tensor_scalar(ARG, ARG, pi, -pi, ALU.min, ALU.max).then_inc(f_arg, 1)

            def filters():
                dve.wait_ge(two_loaded, 7 * 16)
                nv.scalar_tensor_tensor(DELTA, DELTA, -1.0, DELTA, ALU.mult, ALU.max).then_inc(f_abs, 1)
                sine_argument(0)
                sine_argument(1)
                for i in range(8):
                    c, t = i // 2, i % 2
                    dve.wait_ge(f_h, i + 1)
                    dve.wait_ge(f_win, i + 1)
                    nv.scalar_tensor_tensor(FILT[:, t, c, :], WIN[:, i % 2, :], 0.05, PS[:, 4 + i % 2, :], ALU.add, ALU.mult).then_inc(f_filt, 1)
                dve.wait_ge(f_filt, 8)
                for o in range(2):
                    f, b = FILT[:, :, 2 * o, :], FILT[:, :, 2 * o + 1, :]
                    link(nv.tensor_tensor(f, f, b, ALU.add))
                    nv.scalar_tensor_tensor(b, b, -2.0, f, ALU.mult, ALU.add).then_inc(f_sum, 1)

            def conv(dst, src, w, b, lo, hi, blocks):
                tap = lambda i, j: p2[:, w + blocks * j + i:w + blocks * j + i + 1]
                u = lambda i: proj[:, src + i, :]
                for i in range(lo, hi):
                    ins = nv.tensor_scalar(dst[:, i, :], u(i), tap(i, 1), p2[:, b + i:b + i + 1], ALU.mult, ALU.add)
                link(ins)
                for i in range(lo, hi):
                    y = dst[:, i, 1:T]
                    ins = nv.scalar_tensor_tensor(y, u(i)[:, 0:T - 1], tap(i, 0), y, ALU.mult, ALU.add)
                link(ins)
                for i in range(lo, hi):
                    y = dst[:, i, 0:T - 1]
                    ins = nv.scalar_tensor_tensor(y, u(i)[:, 1:T], tap(i, 2), y, ALU.mult, ALU.add)
                if src == 0:
                    ins.then_inc(conv_ready, 1)
                else:
                    link(ins)

            def mlstm():
                f = G4[0:H2, 1::2, :]
                i_ = G4[0:H2, 0::2, :]
                lf, bb, aa, nm, emr, zer = (a[0:H2] for a in (LF, BB, AA, NM, EMR, ZER))
                dve.wait_ge(act2, 6)
                conv(QK2, 0, P2_CQW, P2_CQB, 0, 8, 8)
                dve.wait_ge(kf_ready, 8)
                nv.scalar_tensor_tensor(lf, f, -1.0, f, ALU.mult, ALU.max).then_inc(gate_rows, 1)
                dve.wait_ge(conv_ready, 1)
                link(nv.memset(zer, 0.0))
                dve.wait_ge(ln_rows, 2)
                link(nv.scalar_tensor_tensor(lf, f, 0.0, lf, ALU.min, ALU.subtract))
                link(nv.tensor_tensor_scan(bb[:, 0, :], zer[:, 0, :], lf[:, 0, :], 0.0, ALU.add, ALU.add))
                link(nv.tensor_tensor_scan(bb[:, 1, ::-1], zer[:, 0, :], lf[:, 1, ::-1], 0.0, ALU.add, ALU.add))
                link(nv.tensor_tensor(aa, i_, bb, ALU.subtract))
                link(nv.tensor_tensor_scan(nm[:, 0, :], zer[:, 0, :], aa[:, 0, :], NEG, ALU.add, ALU.max))
                nv.tensor_tensor_scan(nm[:, 1, ::-1], zer[:, 0, :], aa[:, 1, ::-1], NEG, ALU.add, ALU.max).then_inc(rows_ready, 1)
                dve.wait_ge(rows_ready, 1)
                link(nv.tensor_tensor(emr, bb, nm, ALU.add))
                nv.tensor_scalar(nm, nm, -1.0, None, ALU.mult).then_inc(rows_ready, 1)
                dve.wait_ge(rows_ready, 2)
                dve.wait_ge(m_out, 3)
                e1 = E2.rearrange("p d j t -> p (d j t)")
                for h in range(H2):
                    dve.wait_ge(m_em, h + 1)
                    for d in range(2):
                        for j in range(TT):
                            ins = nv.tensor_scalar(E2[:, d, j, :], PS[:, 3, T * d:T * (d + 1)], ACOL[:, d, j, h:h + 1], 0.0, ALU.add, ALU.min)
                    ins.then_inc(m_arg, 1)
                    dve.wait_ge(m_exp, h + 1)
                    link(nv.tensor_tensor(e1, e1, MASK2, ALU.mult))
                    dve.wait_ge(m_s, h + 1)
                    e3 = E2.rearrange("p d j t -> p d (j t)")
                    nv.scalar_tensor_tensor(e3, PS[:, 2, :].unsqueeze(1).broadcast_to([P, 2, 512]), DH2 ** -0.5, e3, ALU.mult, ALU.mult)\
                        .then_inc(m_w, 1)
                    lo, hi = max(4 * h - 2, 0), min(4 * h + 2, 12)
                    dve.wait_ge(act2, 8 + hi // 2)
                    conv(HX2, 16, P2_CHW, P2_CHB, lo, hi, 12)
                    dve.wait_ge(m_num, h + 1)
                    dve.wait_ge(m_emo, h + 1)
                    ems = EMS.rearrange("p a b -> p (a b)")
                    num = NUM.rearrange("p a b -> p (a b)")
                    link(nv.scalar_tensor_tensor(num, PS[:, 6, :], -1.0, ems, ALU.mult, ALU.max))
                    link(nv.tensor_tensor(num, PS[:, 6, :], num, ALU.max))
                    link(nv.reciprocal(num, num))
                    link(nv.tensor_tensor(num, PS[:, 5, :], num, ALU.mult))
                    nv.tensor_tensor(HS2[:, h, :], NUM[:, 0, :], NUM[:, 1, :], ALU.add).then_inc(m_h, 1)
                dve.wait_ge(m_h, H2)
                dve.wait_ge(act2, 16)
                group_norm(1, HS2, P2_MN, 0, proj[:, 12:16, :])

            def group_norm(n, x, gain, at, gate):
                nv.tensor_tensor(E2F, x, x, ALU.mult).then_inc(r_sq, 1)
                dve.wait_ge(r_std, n)
                link(nv.reciprocal(E2F, E2F))
                for b in range(4):
                    ins = nv.scalar_tensor_tensor(hT[:, at + b, :], x[:, b, :], p2[:, gain + b:gain + b + 1], E2F[:, b, :], ALU.mult, ALU.mult)
                if gate is not None:
                    link(ins)
                    ins = nv.tensor_tensor(hT[:, at:at + 4, :], hT[:, at:at + 4, :], gate, ALU.mult)
                ins.then_inc(cat_ready, 1)

            def hyena():
                z = HX2[:, 8:12, :]
                for o in range(2):
                    for kt in range(TT):
                        dve.wait_ge(u2_ready, TT * o + kt + 1)
                        x, f = PS[:, 2 + 2 * kt:4 + 2 * kt, :], KF[:, kt, o, :, :]
                        for n, (a, b) in enumerate(((0, 0), (1, 1), (0, 1), (1, 0))):
                            ins = nv.tensor_tensor(TMP[:, n, :], x[:, a, :], f[:, b, :], ALU.mult)
                        link(ins)
                        nv.tensor_tensor(YF[:, kt, 0, :], TMP[:, 0, :], TMP[:, 1, :], ALU.subtract)
                        nv.tensor_tensor(YF[:, kt, 1, :], TMP[:, 2, :], TMP[:, 3, :], ALU.add).then_inc(yf_ready, 1)
                        dve.wait_ge(yf_ready, TT * o + kt + 1)
                    dve.wait_ge(yt_ready, o + 1)
                    for b in range(4):
                        ins = nv.scalar_tensor_tensor(z[:, b, :], z[:, b, :], p2[:, P2_HBIAS + 4 * o + b:P2_HBIAS + 4 * o + b + 1],
                                                      PS[:, 6 + b // 2, T * (b % 2):T * (b % 2 + 1)], ALU.mult, ALU.add)
                    link(ins)
                    nv.tensor_tensor(z, z, HX2[:, 4 * o:4 * o + 4, :], ALU.mult).then_inc(z_ready2, 1)
                    dve.wait_ge(z_ready2, o + 1)
                group_norm(2, z, P2_HN, 4, None)

            def residual(n, signal, gate, bank):
                for b in range(2):
                    k = 2 * n + b
                    ins = nv.scalar_tensor_tensor(xT[:, k, :], PS[:, bank, T * b:T * (b + 1)], mod[:, gate + k:gate + k + 1], xT[:, k, :],
                                                  ALU.mult, ALU.add)
                ins.then_inc(signal, 1)

            def low_tokens(lo, hi):
                for i in range(lo, hi):
                    t, c = i // 2, slice(512 * (i % 2), 512 * (i % 2) + 512)
                    dve.wait_ge(tok2_out, i + 1)
                    nv.tensor_tensor(tok_low[:, t, c], PS[:, 4 + i, :], tok_high[:, t, c].bitcast(F32), ALU.subtract).then_inc(tok2_low, 1)

            def route():
                m, s = ST4[:, 0:TT], ST4[:, TT:2 * TT]
                wide = lambda a: a.unsqueeze(2).broadcast_to([P, TT, EXPERTS])
                dve.wait_ge(rt_logit, 1)
                lg = banks(2, 1, TT, EXPERTS)
                link(nv.tensor_reduce(m, lg, AX, ALU.max))
                nv.tensor_tensor(LOG, lg, wide(m), ALU.subtract).then_inc(rt_max, 1)
                low_tokens(0, 2)
                dve.wait_ge(rt_exp, 1)
                link(nv.tensor_reduce(s, LOG, AX, ALU.add))
                link(nv.reciprocal(s, s))
                nv.tensor_tensor(LOG, LOG, wide(s), ALU.mult).then_inc(rt_prob, 1)
                low_tokens(2, 4)
                dve.wait_ge(rt_tr, 1)
                link(nv.tensor_copy(AFF, PS[0:EXPERTS, 3, 0:T]))
                for g in range(CAP // 8):
                    v, ix = VAL[:, 8 * g:8 * g + 8], IDXU[:, 8 * g:8 * g + 8].bitcast(U32)
                    link(nv.max(v, AFF))
                    link(nv.max_index(ix, v, AFF))
                    link(nv.match_replace(AFF, v, AFF, -1.0))
                link(nv.tensor_copy(IDXF, IDXU.bitcast(U32)))
                for a, src in enumerate((IDXF, VAL)):
                    ins = nv.tensor_copy(REP[:, a, :, :], src.unsqueeze(1).broadcast_to([EXPERTS, 4, CAP]))
                    if a == 0:
                        link(ins)
                ins.then_inc(topk_done, 1)
                eye = ident[0:EXPERTS, 0:EXPERTS].unsqueeze(2).broadcast_to([EXPERTS, EXPERTS, CAP])
                nv.tensor_tensor(DIAG[0:EXPERTS, :].rearrange("p (e s) -> p e s", s=CAP), eye,
                                 IDXF.unsqueeze(1).broadcast_to([EXPERTS, EXPERTS, CAP]), ALU.mult).then_inc(diag_ready, 1)
                dve.wait_ge(row_ready, 1)
                nv.memset(ZERO, 0.0)
                for t in range(TT):
                    ins = nv.tensor_scalar(PICK[:, t, :], PS[:, 3, :], c2[:, D_TOK + t:D_TOK + t + 1], None, ALU.is_equal)
                    if t == 0:
                        link(ins)
                ins.then_inc(pick_ready, 1)
                dve.wait_ge(xs_out, KD)
                dve.wait_ge(ix_out, 1)

            def experts():
                iota = c2[:, D_IOTA:D_IOTA + T]
                with dve.Fori(0, EXPERTS) as e:
                    dve.wait_ge(expert_slots, EXPERT_SLOTS * e + 8)
                    nv.tensor_scalar(XSE.rearrange("p k s -> p (k s)"), XS[:, e, :, :].rearrange("p k s -> p (k s)"), 1.0, None, ALU.mult)\
                        .then_inc(xs_staged, 1)
                    dve.wait_ge(scattered, e + 1)
                    nv.tensor_scalar(GE, iota, IG[:, 0, bass.ts(e, 1)], IG[:, 1, bass.ts(e, 1)], ALU.is_equal, ALU.mult).then_inc(ge_ready, 1)
                    dve.wait_ge(expert_slots, EXPERT_SLOTS * e + EXPERT_SLOTS + 8)
                    dve.wait_ge(hs_ready, e + 1)
                    nv.tensor_tensor(HE, HSE, PS[:, 3, :], ALU.mult).then_inc(he_ready, 1)
                    dve.wait_ge(expert_slots, EXPERT_SLOTS * e + EXPERT_SLOTS + 12)
                    nv.tensor_copy(YE, PS[:, 5, :]).then_inc(ye_ready, 1)

            for n in range(4):
                square(n)
            dve.wait_ge(two_loaded, 16)
            link(nv.scalar_tensor_tensor(gs1, mod[:, 8:16], 1.0, p2[:, P2_GMIX:P2_GMIX + KD], ALU.add, ALU.mult))
            link(nv.scalar_tensor_tensor(gs2, mod[:, 32:40], 1.0, p2[:, P2_GFFN:P2_GFFN + KD], ALU.add, ALU.mult))
            norm(1, gs1, 0)
            filters()
            mlstm()
            hyena()
            for n in range(4):
                dve.wait_ge(block_done, BASE2 + 16 + n + 1)
                residual(n, dve2, 16, (16 + n) % 2)
                dve.wait_ge(dve2, n + 1)
                square(n)
            norm(2, gs2, 24)
            route()
            experts()
            dve.wait_ge(scattered, EXPERTS + 1)
            for n, b in enumerate((6, 7, 0, 1)):
                residual(n, moe_sum, 40, b)
                dve.wait_ge(moe_sum, n + 1)
                square(n)
            root(3)
            for k in range(KD):
                ins = nv.scalar_tensor_tensor(hT[:, k, :], xT[:, k, :], p2[:, P2_GFIN + k:P2_GFIN + k + 1], RSTD2, ALU.mult, ALU.mult)
            ins.then_inc(h2_ready, 1)

        block = ctx.enter_context(nc.Block())

        @block.sync
        def _(sp):
            def load(slot, pieces):
                for dst, src in pieces:
                    sp.dma_start(dst, src).then_inc(ring_full[slot], 16)

            def by_rows(w, slot, cols, place=None):
                place = ring[:, slot, :] if place is None else place
                n = w.shape[0] // P
                c = w.shape[1]
                v = w.rearrange("(k p) n -> p k n", p=P)
                r = place[:, 0:n * c].rearrange("p (k n) -> p k n", n=c)
                load(slot, [(r[:, 0:n // 2], v[:, 0:n // 2]), (r[:, n // 2:n], v[:, n // 2:n])])

            sp.wait_ge(const_loaded, 4 * 16)
            with sp.Fori(0, LAYERS) as l:
                for n in range(LAYER_SLOTS):
                    if n >= RING:
                        sp.wait_ge(block_done, START + LAYER_BLOCKS * l + SLOT_DONE[n - RING])
                    else:
                        sp.wait_ge(block_done, START + LAYER_BLOCKS * l - (RING - 1 - n))
                    sp.sem_inc(slot_freed, 1)
                    s = n % RING
                    if n in S_ADA:
                        by_rows(io["w_ada_2"][0].rearrange("d (l n) -> l d n", l=LAYERS)[l][:, 512 * S_ADA.index(n):512 * S_ADA.index(n) + 512], s, 512)
                    elif n < N_PROJ // 2:
                        by_rows(io["w_in"][l][:, IN_ORDER[n]:IN_ORDER[n] + 512], s, 512)
                    elif n < S_OUT:
                        by_rows(io[("w_attn_o", "w_rwkv_o", "w_ret_o")[S_MIX.index(n)]][l], s, D)
                    elif n < S_FFN:
                        by_rows(io["w_out"][l][:, 512 * (n - S_OUT):512 * (n - S_OUT + 1)], s, 512)
                    elif n < S_DOWN:
                        c = 256 * (n - S_FFN)
                        load(s, [(ring[:, s, 2048 * g:2048 * (g + 1)].rearrange("p (k n) -> p k n", n=256),
                                  io[("w_ffn_gate", "w_ffn_up")[g]][l][:, c:c + 256].rearrange("(k p) n -> p k n", p=P))
                                 for g in range(2)])
                    else:
                        c = P * (n - S_DOWN)
                        by_rows(io["w_ffn_down"][l][:, c:c + P], s, P)
            second_sync(sp, load, by_rows)

        @block.gpsimd
        def _(pool):
            pool.memset(bias[:, 0:1], EPS).then_inc(bias_set, 1)
            pool.memset(bias[:, 1:2], LNX_EPS).then_inc(bias_set, 1)
            pool.memset(bias[:, 2:3], 1.0).then_inc(bias_set, 1)
            def low_parts(lo, hi):
                for j in range(lo, hi):
                    n = SPLIT[j]
                    c = slice(width(n) // 2, width(n))
                    w = ring[:, n % RING, c]
                    pool.wait_ge(high_ready, j + 1)
                    pool.tensor_tensor(ring_low[:, n % RING, c], w, high(n)[:, c].bitcast(F32), ALU.subtract).then_inc(low_pool, 1)

            with pool.Fori(0, LAYERS) as l:
                low_parts(0, SPLIT_A)
                pool.wait_ge(oa_out, 3)
                pool.memset(w_(9216, 4096), 0.0).then_inc(gm_zero, 1)
                cos = con[:, C_COS:C_COS + T].unsqueeze(1).broadcast_to([P, HB, T])
                for n, at in enumerate((B_RQ, B_RK)):
                    x = proj[:, at:at + HB, :]
                    pool.wait_ge(rot_ready, n + 1)
                    pool.tensor_tensor(x, x, cos, ALU.mult).then_inc(pool_made, 1)
                pool.wait_ge(oc_out, 1)
                pool.tensor_tensor(GATED, proj[:, B_RQ:B_RQ + HB, :], proj[:, B_RG:B_RG + HB, :], ALU.mult).then_inc(pool_made, 1)
                low_parts(SPLIT_A, len(SPLIT))
                pool.wait_ge(layer_fin, 3)
                pool.sem_clear(layer_sems)
                pool.sem_inc(layer_go, 1)
            second_pool(pool)

        @block.tensor
        def _(pe):
            nt = nc.tensor

            def taken(q):
                if q >= 2:
                    pe.wait_ge(act_taken if BY_ACT[q - 2] else dve_taken, TAKEN[q - 2])

            def ada(l, n):
                q, s = Q_ADA[n], S_ADA[n] % RING
                pe.wait_ge(ring_full[s], full(l, S_ADA[n]))
                taken(q)
                for k in range(KD):
                    j = 32 * (k % 4)
                    mm = nt.matmul(PS[j:j + 32, q % 2, :], cond[:, k, 32 - n:64 - n], ring[:, s, 512 * k:512 * (k + 1)],
                                   start=(k < 4), stop=(k >= 4))
                mm.then_inc(block_done, 1)

            def ada_columns():
                taken(Q_COLS)
                pe.wait_ge(dve_taken, TAKEN[Q_ADA[-1]])
                for b in range(4):
                    mm = nt.matmul(PS[:, Q_COLS % 2, N_ADA * b:N_ADA * (b + 1)], mod_rows[:, P * b:P * (b + 1)], con[:, C_SEL:C_SEL + N_ADA],
                                   start=True, stop=True)
                mm.then_inc(block_done, 1)

            def product(q, weight, moving, kn, n_blocks=2):
                taken(q)
                for b in range(n_blocks):
                    for k in range(kn):
                        mm = nt.matmul(PS[:, q % 2, T * b:T * (b + 1)], weight(b, k), moving(k), start=(k == 0), stop=(k == kn - 1))
                mm.then_inc(block_done, 1)

            def split_product(q, n, weight, high_x, low_x, kn, n_blocks=2, low_at=None):
                j = SPLIT.index(n)
                pe.wait_ge(low_dve, j + 1)
                pe.wait_ge(low_pool, j + 1)
                taken(q)
                h, w = high(n), ring_low[:, n % RING, :]
                for b in range(n_blocks):
                    out = PS[:, q % 2, T * b:T * (b + 1)]
                    for k in range(kn):
                        c = weight(b, k)
                        nt.matmul(out, h[:, c:c + P], high_x[:, k, :], start=(k == 0), stop=False)
                        nt.matmul(out, w[:, c:c + P], high_x[:, k, :], start=False, stop=False)
                    if b == 0 and low_at is not None:
                        pe.wait_ge(h_ready, low_at)
                    for k in range(kn):
                        c = weight(b, k)
                        mm = nt.matmul(out, h[:, c:c + P], low_x[:, k, :], start=False, stop=(k == kn - 1))
                mm.then_inc(block_done, 1)

            def norm_sums(n):
                for k in range(KD):
                    if k % 2 == 0:
                        pe.wait_ge(sq_ready, 4 * (n - 1) + k // 2 + 1)
                    mm = nt.matmul(PS[:, 2, 0:T], ones, SQ[:, k, :], start=(k == 0), stop=(k == KD - 1))
                mm.then_inc(ss_ready, 1)

            def project(l, lo, hi):
                for q in range(lo, hi):
                    s, half = q // 2 % RING, q % 2
                    if half == 0:
                        pe.wait_ge(ring_full[s], full(l, q // 2))
                    product(q, lambda b, k: ring[:, s, 512 * k + P * (2 * half + b):512 * k + P * (2 * half + b + 1)],
                            lambda k: hT[:, k, :], KD)

            def split_project(lo, hi):
                for q in range(lo, hi):
                    split_product(q, q // 2, lambda b, k: 512 * k + P * (2 * (q % 2) + b), XH_A, XL_A, KD, low_at=2 if q == 0 else None)

            def head_sums(bank, src, signal):
                for n in range(2):
                    mm = nt.matmul(PS[:, bank + n, :], bd, src[:, 2 * n:2 * n + 2, :].rearrange("p a b -> p (a b)"), start=True, stop=True)
                mm.then_inc(signal, 1)

            def lora_products():
                pe.wait_ge(lora_in, 2)
                for b in range(HB):
                    mm = nt.matmul(PS[:, 2 + b // 2, T * (b % 2):T * (b % 2 + 1)], lora[0:64, P * b:P * (b + 1)],
                                   proj[0:64, B_LORA, :], start=True, stop=True)
                mm.then_inc(lora_done, 1)
                for b in range(HB):
                    mm = nt.matmul(PS[:, 4 + b // 2, T * (b % 2):T * (b % 2 + 1)], lora[64:128, P * b:P * (b + 1)],
                                   proj[64:128, B_LORA, :], start=True, stop=True)
                mm.then_inc(lora_done, 1)
                for b in range(HB):
                    mm = nt.matmul(PS[:, 6 + b // 2, T * (b % 2):T * (b % 2 + 1)], lora[:, 512 + P * b:512 + P * (b + 1)],
                                   proj[:, B_GD, :], start=True, stop=True)
                mm.then_inc(lora_done, 1)

            def rwkv_prep():
                pe.wait_ge(kk_sq, 1)
                pe.wait_ge(lora_out, 4)
                head_sums(2, X3, kk_ss)
                pe.wait_ge(lora_out, 10)
                for t in range(TT):
                    for b in range(HB):
                        mm = nt.transpose(PS[:, 4 + t, P * b:P * (b + 1)], proj[:, B_V + b, P * t:P * (t + 1)], ident)
                mm.then_inc(tok_ready, 1)

            def rwkv_decayed():
                pe.wait_ge(gram_in, 1)
                for n, src in enumerate((AT, KK)):
                    for b in range(HB):
                        mm = nt.transpose(PS[:, 6 + n, P * b:P * (b + 1)], src[:, b, 0:P], ident)
                mm.then_inc(tok_ready, 1)
                pe.wait_ge(kk_std, 1)
                pe.wait_ge(bonus_in, 1)
                head_sums(2, Y, bonus_ss)

            def rwkv_chunk(l, t):
                cols = slice(P * t, P * (t + 1))
                if t == 0:
                    pe.wait_ge(tok_out, 4)
                    pe.wait_ge(oa_out, 3)
                else:
                    pe.wait_ge(y_out, 1)
                    pe.wait_ge(st_ready, 1)
                for h in range(HEADS):
                    bk = 2 + h % 2 + 2 * (h // 2 % 2)
                    if h >= 4:
                        pe.wait_ge(gram_taken, 8 * t + h - 3)
                    o, b = hrow(h), h // 2
                    nt.matmul(PS[:, bk, 0:P], AR[o, b, t, 0, :], AT[o, b, cols], start=True, stop=True)
                    nt.matmul(PS[:, bk, P:2 * P], AT[o, b, cols], AR[o, b, t, 1, :], start=True, stop=True)
                    nt.matmul(PS[:, bk, 2 * P:4 * P], KK[o, b, cols], AR[o, b, t, :, :].rearrange("p a b -> p (a b)"),
                              start=True, stop=True).then_inc(gram_ready, 1)
                for lev in range(LEVELS):
                    for half in range(2):
                        pe.wait_ge(qt_ready, t * (2 * LEVELS + 1) + (2 * lev + half if lev else 1))
                        if lev == 0:
                            pe.wait_ge(gram_taken, 8 * t + 4 * (half + 1))
                        for u in range(4 * half, 4 * half + 4):
                            out, q = PS[:, 6 + half, P * (u % 4):P * (u % 4 + 1)], QT[:, u, 0, :]
                            if lev:
                                out, q = every_other(out, lev, 1), every_other(q, lev, 1)
                            mm = nt.matmul(out, GM[:, u, 0:P], q, start=True, stop=True)
                        mm.then_inc(w1_ready, 1)
                    if lev in ADA_AT[t]:
                        ada(l, ADA_AT[t][lev])
                    if lev == COLS_AT[t]:
                        ada_columns()
                    for half in range(2):
                        i = (t * LEVELS + lev) * 2 + half
                        pe.wait_ge(w1_masked, i + 1)
                        for u in range(4 * half, 4 * half + 4):
                            bk, c = 2 + 2 * half + u % 4 // 2, 2 * P * (u % 2)
                            nt.matmul(every_other(PS[:, bk, c:c + P], lev, 1), QT[:, u, 1, :], every_other(W1S[:, u, :], lev, 1),
                                      start=True, stop=True)
                            mm = nt.matmul(every_other(PS[:, bk, c + P:c + 2 * P], lev, 0), W1S[:, u, :], every_other(QT[:, u, 1, :], lev, 0),
                                           start=True, stop=True)
                        mm.then_inc(dq_ready, 1)
                pe.wait_ge(qt_ready, (t + 1) * (2 * LEVELS + 1))
                for h in [0, 2, 4, 6, 1, 3, 5, 7]:
                    out = PS[:, 6 + h % 2, HD * (h // 2):HD * (h // 2 + 1)]
                    if t:
                        nt.matmul(out, AR[hrow(h), h // 2, t, 0, :], ST[hrow(h), h // 2, :], start=True, stop=False)
                    mm = nt.matmul(out, GM[:, h, 2 * P:3 * P], VTOK[:, t, HD * h:HD * (h + 1)], start=(t == 0), stop=True)
                mm.then_inc(rhs_ready, 1)
                mix(l, 0, 2 * t, 2 * t + 1)
                pe.wait_ge(rhs_out, 2 * (t + 1))
                for h in range(HEADS):
                    mm = nt.matmul(PS[:, 2, HD * h:HD * (h + 1)], QT[:, h, 0, :], RHS[:, h, :], start=True, stop=True)
                mm.then_inc(u_ready, 1)
                mix(l, 0, 2 * t + 1, 2 * t + 2)
                pe.wait_ge(u_out, t + 1)
                for h in range(HEADS):
                    out = PS[hrow(h), 3, P * (h // 2):P * (h // 2 + 1)]
                    nt.matmul(out, U[:, h, :], GM[:, h, P:2 * P], start=True, stop=False)
                    mm = nt.matmul(out, VTOK[:, t, HD * h:HD * (h + 1)], GM[:, h, 3 * P:4 * P], start=False, stop=(t == 0))
                    if t:
                        mm = nt.matmul(out, ST[hrow(h), h // 2, :], AR[hrow(h), h // 2, t, 1, :], start=False, stop=True)
                mm.then_inc(y_ready, 1)
                if t == 0:
                    for h in range(HEADS):
                        out = PS[hrow(h), 5, HD * (h // 2):HD * (h // 2 + 1)]
                        nt.matmul(out, BKT[:, 0, HD * h:HD * (h + 1)], U[:, h, :], start=True, stop=False)
                        mm = nt.matmul(out, BKT[:, 1, HD * h:HD * (h + 1)], VTOK[:, 0, HD * h:HD * (h + 1)], start=False, stop=True)
                    mm.then_inc(s_ready, 1)

            def attention(l):
                pe.wait_ge(att_sq, 2)
                pe.wait_ge(bonus_out, 1)
                head_sums(2, ATS[:, 0:HB, :], att_ss)
                nt.matmul(PS[:, 4, 0:T], bd, ATS[:, HB, :], start=True, stop=True).then_inc(att_ss, 1)
                pe.wait_ge(tok_out, 4)
                for t in range(TT):
                    mm = nt.transpose(PS[:, 6, P * t:P * (t + 1)], proj[:, B_AV, P * t:P * (t + 1)], ident)
                mm.then_inc(att_tr, 1)
                project(l, 20, 22)
                pe.wait_ge(att_qk, 2)
                for kv in range(2):
                    mm = nt.matmul(PS[:, 5, T * kv:T * (kv + 1)], con[:, C_DUP + P * kv:C_DUP + P * (kv + 1)], proj[:, B_AK, :],
                                   start=True, stop=True)
                mm.then_inc(att_tr, 1)
                pe.wait_ge(att_kv, 2)
                for r, (t, heads) in enumerate(ROUNDS):
                    w = P * (t + 1)
                    if r:
                        pe.wait_ge(oa_out, r)
                    for n, h in enumerate(heads):
                        at = n * w
                        mm = nt.matmul(PS[:, 2 + at // 512, at % 512:at % 512 + w], proj[hrow(h), B_AQ + h // 2, P * t:P * (t + 1)],
                                       KDUP[hrow(h), h // 4, 0:w], start=True, stop=True)
                    mm.then_inc(sc_ready, 1)
                    project(l, *BESIDE_SOFTMAX[r])
                    pe.wait_ge(p_ready, r + 1)
                    for n in range(8):
                        mm = nt.transpose(PS[:, 6 + n // 4, P * (n % 4):P * (n % 4 + 1)], SCO[:, P * n:P * (n + 1)], ident)
                    mm.then_inc(pt_ready, 1)
                    project(l, *BESIDE_COPY[r])
                    pe.wait_ge(pt_out, r + 1)
                    for n, h in enumerate(heads):
                        kv = h // 4
                        for j in range(t + 1):
                            mm = nt.matmul(PS[hrow(h), 4, P * (h // 2):P * (h // 2 + 1)], VATT[:, j, HD * kv:HD * (kv + 1)],
                                           PT[:, n * (t + 1) + j, :], start=(j == 0), stop=(j == t))
                    mm.then_inc(oa_ready, 1)

            def rwkv_norm_and_retention(l):
                def rotate(n, at):
                    for b in range(2):
                        mm = nt.matmul(PS[:, 2 + 2 * n + b, :], perm, proj[:, at + 2 * b:at + 2 * b + 2, :].rearrange("p a b -> p (a b)"),
                                       start=True, stop=True)
                    mm.then_inc(rot_ready, 1)

                pe.wait_ge(y_out, 2)
                head_sums(4, Y, ln_ss)
                rotate(0, B_RQ)
                pe.wait_ge(ln_in, 1)
                head_sums(6, X1, ln_ss)
                rotate(1, B_RK)
                pe.wait_ge(ln_std, 1)
                for t in range(TT):
                    for b in range(HB):
                        mm = nt.transpose(PS[:, 6 + t, P * b:P * (b + 1)], proj[:, B_RV + b, P * t:P * (t + 1)], ident)
                mm.then_inc(vr_ready, 1)
                pe.wait_ge(rot_out, 2)
                for h in range(HEADS):
                    o, b, bk = hrow(h), h // 2, 2 + h % 2 + 2 * (h // 2 % 2)
                    if h >= 4:
                        pe.wait_ge(rs_out, h - 3)
                    nt.matmul(PS[:, bk, 0:T], proj[o, B_RK + b, 0:P], proj[o, B_RQ + b, :], start=True, stop=True)
                    nt.matmul(PS[:, bk, T:T + P], proj[o, B_RK + b, P:T], proj[o, B_RQ + b, P:T], start=True, stop=True)\
                        .then_inc(rs_ready, 1)
                pe.wait_ge(vr_out, 2)
                for h in range(HEADS):
                    pe.wait_ge(rs_out, h + 1)
                    o, b = hrow(h), h // 2
                    bk, c = 6 + b // 2, T * (b % 2)
                    nt.matmul(PS[o, bk, c:c + T], VRET[:, 0, HD * h:HD * (h + 1)], SM[:, h, 0:T], start=True, stop=False)
                    mm = nt.matmul(PS[o, bk, c + P:c + T], VRET[:, 1, HD * h:HD * (h + 1)], SM[:, h, T:T + P], start=False, stop=True)
                mm.then_inc(oc_psum, 1)
                mix(l, 1, 0, 2)
                pe.wait_ge(oc_sq, 1)
                head_sums(2, XR, oc_ss)
                mix(l, 1, 2, 4)

            def mix(l, br, lo, hi):
                src, at, ready = ((proj, B_AQ, oa_out), (Y, 0, ob_ready), (proj, B_RQ, oc_ready))[br]
                s = S_MIX[br] % RING
                if lo == 0:
                    pe.wait_ge(ready, 3 if br == 0 else 1)
                    pe.wait_ge(ring_full[s], full(l, S_MIX[br]))
                for i in range(lo, hi):
                    product(Q_MIX[br][i], lambda b, k: ring[:, s, D * k + P * (2 * i + b):D * k + P * (2 * i + b + 1)],
                            lambda k: src[:, at + k, :], HB)

            def out(l):
                pe.wait_ge(h_ready, 3)
                for n in range(2):
                    for i in range(2):
                        split_product(Q_OUT + 2 * n + i, S_OUT + n, lambda b, k: 512 * k + P * (2 * i + b), XH_F, hT_low, KD)

            def ffn(l):
                pe.wait_ge(h_ready, 4)
                for n in range(N_FFN // 2):
                    for g in range(2):
                        split_product(Q_FFN + 2 * n + g, S_FFN + n, lambda b, k: 2048 * g + 256 * k + P * b, XH_F, hT_low, KD,
                                      low_at=5 if n + g == 0 else None)
                pe.wait_ge(h_ready, 6)
                for n in range(N_DOWN):
                    split_product(Q_DOWN + n, S_DOWN + n, lambda b, k: P * k, HID_H, HID_low, FB, 1)

            pe.sem_inc(block_done, START)
            pe.wait_ge(const_loaded, 4 * 16)
            with pe.Fori(0, LAYERS) as l:
                norm_sums(1)
                pe.wait_ge(h_ready, 1)
                split_project(0, 10)
                lora_products()
                split_project(10, 12)
                rwkv_prep()
                split_project(12, 2 * SPLIT_A)
                project(l, 2 * SPLIT_A, 18)
                rwkv_decayed()
                project(l, 18, 20)
                attention(l)
                project(l, 29, 30)
                rwkv_chunk(l, 0)
                rwkv_chunk(l, 1)
                rwkv_norm_and_retention(l)
                mix(l, 2, 0, 4)
                out(l)
                norm_sums(2)
                ffn(l)
                pe.wait_ge(dve_taken, TAKEN[LAYER_BLOCKS - 1])
                pe.sem_inc(layer_fin, 1)
                pe.wait_ge(layer_go, l + 1)
                pe.sem_inc(layer_joined, 1)
            second_tensor(pe)

        @block.scalar
        def _(act):
            na = nc.scalar
            def proj_out(l, lo, hi):
                for q in range(lo, hi):
                    act.wait_ge(block_done, done(l, q))
                    f = ACT.Copy
                    if 2 * q >= B_GATE:
                        f = ACT.Sigmoid
                    elif 2 * q >= B_RG:
                        f = ACT.Silu
                    na.activation(proj[:, 2 * q:2 * q + 2, :].rearrange("p a b -> p (a b)"), PS[:, q % 2, :], f).then_inc(act_taken, 1)

            def high_weights(l, *slots):
                for n in slots:
                    act.wait_ge(ring_full[n % RING], full(l, n))
                    if n - 2 in SPLIT:
                        act.wait_ge(block_done, done(l, SLOT_DONE[n - 2] - 1))
                    w = slice(0, width(n))
                    na.activation(high(n)[:, w], ring[:, n % RING, w], ACT.Copy).then_inc(high_ready, 1)

            def norm_root(n):
                act.wait_ge(ss_ready, n)
                na.activation(STD, PS[:, 2, 0:T], ACT.Sqrt, bias=epsc, scale=1.0 / D).then_inc(std_ready, 1)

            def lora_inputs():
                act.wait_ge(z_ready, 1)
                na.activation(proj[0:64, B_LORA, :], proj[0:64, B_LORA, :], ACT.Tanh).then_inc(lora_in, 1)
                na.activation(proj[:, B_GD, :], proj[:, B_GD, :], ACT.Sigmoid).then_inc(lora_in, 1)

            def lora_outputs():
                for n, (dst, col) in enumerate(((X1, PL_W0), (AT, PL_A0))):
                    act.wait_ge(lora_done, n + 1)
                    for b in range(HB):
                        na.activation(dst[:, b, :], PS[:, 2 + 2 * n + b // 2, T * (b % 2):T * (b % 2 + 1)], ACT.Sigmoid,
                                      bias=par[:, col + b:col + b + 1]).then_inc(lora_out, 1)
                act.wait_ge(lora_done, 3)
                for n in range(2):
                    na.activation(GT[:, 2 * n:2 * n + 2, :].rearrange("p a b -> p (a b)"), PS[:, 6 + n, :], ACT.Copy).then_inc(lora_out, 1)

            def rwkv_prep():
                act.wait_ge(kk_ss, 1)
                na.activation(Y[:, :, :].rearrange("p a b -> p (a b)"), banks(2, 2), ACT.Sqrt).then_inc(kk_std, 1)
                act.wait_ge(tok_ready, 1)
                for t in range(TT):
                    na.activation(VTOK[:, t, :], PS[:, 4 + t, :], ACT.Copy).then_inc(tok_out, 1)

            def rwkv_exponentials():
                act.wait_ge(cum_ready, 2)
                na.activation(X1[:, :, :], X1[:, :, :], ACT.Exp, scale=-KAPPA).then_inc(exps_ready, 1)
                na.activation(X3[:, :, :], X2[:, :, :], ACT.Exp, scale=-KAPPA).then_inc(exps_ready, 1)
                act.wait_ge(exps_ready, 2)
                na.activation(X2[:, :, :], X2[:, :, :], ACT.Exp, scale=KAPPA).then_inc(exps_ready, 1)
                na.activation(MIDE, MID[:, :, 1], ACT.Exp, scale=-KAPPA).then_inc(exps_ready, 1)

            def rwkv_decayed():
                act.wait_ge(tok_ready, 2)
                for n in range(2):
                    na.activation(BKT[:, n, :], PS[:, 6 + n, :], ACT.Copy).then_inc(tok_out, 1)

            def rwkv_chunk(t):
                act.wait_ge(rhs_ready, t + 1)
                for odd in range(2):
                    na.activation(RHS[:, odd::2, :], banks(6 + odd, 1, HB, HD), ACT.Copy).then_inc(rhs_out, 1)
                act.wait_ge(u_ready, t + 1)
                na.activation(U[:, :, :].rearrange("p a b -> p (a b)"), PS[:, 2, :], ACT.Copy).then_inc(u_out, 1)
                act.wait_ge(y_ready, t + 1)
                na.activation(Y[:, :, P * t:P * (t + 1)], banks(3, 1, HB, P), ACT.Copy).then_inc(y_out, 1)

            def rwkv_norm():
                act.wait_ge(y_ready, 2)
                act.dma_start(w_(9216, HEADS * 3 * P), io["decay"]).then_inc(dec_loaded, 16)
                act.wait_ge(ln_ss, 2)
                na.activation(X2[:, :, :].rearrange("p a b -> p (a b)"), banks(6, 2), ACT.Sqrt, bias=lnxc, scale=1.0 / HD).then_inc(ln_std, 1)

            def attention(l):
                act.wait_ge(att_ss, 2)
                na.activation(ATS[:, 0:HB, :].rearrange("p a b -> p (a b)"), banks(2, 2), ACT.Sqrt, bias=epsc, scale=1.0 / HD).then_inc(att_std, 1)
                na.activation(ATS[:, HB, :], PS[:, 4, 0:T], ACT.Sqrt, bias=epsc, scale=1.0 / HD).then_inc(att_std, 1)
                act.wait_ge(att_tr, 1)
                na.activation(VATT[:, :, :].rearrange("p a b -> p (a b)"), PS[:, 6, 0:T], ACT.Copy).then_inc(att_kv, 1)
                proj_out(l, 20, 22)
                act.wait_ge(att_tr, 2)
                na.activation(KDUP[:, :, :].rearrange("p a b -> p (a b)"), PS[:, 5, :], ACT.Copy).then_inc(att_kv, 1)
                for r, (t, heads) in enumerate(ROUNDS):
                    act.wait_ge(sc_max, r + 1)
                    na.activation(SCO, SCO, ACT.Exp).then_inc(sc_exp, 1)
                    na.activation(SK[:, 0:len(heads)], SK[:, 0:len(heads)], ACT.Exp).then_inc(sc_exp, 1)
                    proj_out(l, *BESIDE_SOFTMAX[r])
                    act.wait_ge(pt_ready, r + 1)
                    na.activation(PT[:, :, :].rearrange("p a b -> p (a b)"), banks(6, 2), ACT.Copy).then_inc(pt_out, 1)
                    proj_out(l, *BESIDE_COPY[r])
                    act.wait_ge(oa_ready, r + 1)
                    b0, b1 = (0, 4) if t == 0 else (2 * (r - 1), 2 * r)
                    na.activation(proj[:, B_AQ + b0:B_AQ + b1, P * t:P * (t + 1)],
                                  PS[:, 4, P * b0:P * b1].rearrange("p (a b) -> p a b", b=P), ACT.Copy).then_inc(oa_out, 1)

            def retention():
                act.wait_ge(vr_ready, 1)
                for t in range(TT):
                    na.activation(VRET[:, t, :], PS[:, 6 + t, :], ACT.Copy).then_inc(vr_out, 1)
                act.wait_ge(oc_psum, 1)
                na.activation(proj[:, B_RQ:B_RQ + HB, :].rearrange("p a b -> p (a b)"), banks(6, 2), ACT.Copy).then_inc(oc_out, 1)
                act.wait_ge(oc_ss, 1)
                na.activation(XR[:, :, :].rearrange("p a b -> p (a b)"), banks(2, 2), ACT.Sqrt, bias=epsc, scale=1.0 / HD).then_inc(oc_std, 1)

            def ffn(l):
                act.wait_ge(h_ready, 4)
                act.dma_start(par[:, :], io["layer_params"][1:][l]).then_inc(par_loaded, 16)
                act.dma_start(lora[:, :], io["layer_lora"][1:][l]).then_inc(par_loaded, 16)
                for n in range(N_FFN // 2):
                    act.wait_ge(block_done, done(l, Q_FFN + 2 * n))
                    if n >= 2:
                        act.wait_ge(dve_taken, TAKEN[Q_FFN + 2 * n - 3])
                    na.activation(SILU[:, n % 2, :], PS[:, Q_FFN % 2, :], ACT.Silu).then_inc(act_taken, 1)
                    high_weights(l, S_FFN + 2 + n)
                high_weights(l, *range(S_DOWN + 2, LAYER_SLOTS))

            act.dma_start(con[:, :], io["constants"]).then_inc(const_loaded, 16)
            act.dma_start(xT[:, :, :], io["xT"]).then_inc(const_loaded, 16)
            act.dma_start(cond[:, :, :], io["cond"]).then_inc(const_loaded, 16)
            act.dma_start(mod[:, :], io["ada_bias"]).then_inc(const_loaded, 16)
            act.dma_start(par[:, :], io["layer_params"][0]).then_inc(par_loaded, 16)
            act.dma_start(lora[:, :], io["layer_lora"][0]).then_inc(par_loaded, 16)
            act.dma_start(p2, io["params_2"]).then_inc(two_loaded, 16)
            act.wait_ge(bias_set, 3)
            with act.Fori(0, LAYERS) as l:
                high_weights(l, 0)
                norm_root(1)
                high_weights(l, 1, 2)
                proj_out(l, 0, 3)
                high_weights(l, 3)
                proj_out(l, 3, 5)
                high_weights(l, 4)
                proj_out(l, 5, 8)
                high_weights(l, 5)
                lora_inputs()
                proj_out(l, 8, 10)
                high_weights(l, 6)
                lora_outputs()
                proj_out(l, 10, 12)
                rwkv_prep()
                high_weights(l, 7)
                proj_out(l, 12, 14)
                rwkv_exponentials()
                proj_out(l, 14, 18)
                rwkv_decayed()
                proj_out(l, 18, 20)
                attention(l)
                proj_out(l, 29, 30)
                rwkv_chunk(0)
                rwkv_chunk(1)
                rwkv_norm()
                retention()
                act.wait_ge(block_done, done(l, Q_MIX[1][-1]))
                act.wait_ge(oc_ready, 1)
                high_weights(l, S_OUT, S_OUT + 1, S_FFN)
                norm_root(2)
                high_weights(l, S_FFN + 1)
                ffn(l)
                act.wait_ge(act_taken, TAKEN[Q_DOWN - 2])
                act.sem_inc(layer_fin, 1)
                act.wait_ge(layer_go, l + 1)
                act.sem_inc(layer_joined, 1)
            second_scalar(act)

        @block.vector
        def _(dve):
            nv = nc.vector
            count = [0]

            def link(ins):
                count[0] += 1
                ins.then_inc(vec_order, 1)
                dve.wait_ge(vec_order, count[0])

            def low_weights(n):
                c = slice(0, width(n) // 2)
                w = ring[:, n % RING, c]
                dve.wait_ge(high_ready, SPLIT.index(n) + 1)
                nv.tensor_tensor(ring_low[:, n % RING, c], w, high(n)[:, c].bitcast(F32), ALU.subtract).then_inc(low_dve, 1)

            def high_part(h, x):
                return nv.tensor_copy(h, x)

            def low_part(low, x, h):
                return nv.tensor_tensor(low, x, h.bitcast(F32), ALU.subtract)

            def square(n):
                x = slice(2 * n, 2 * n + 2)
                nv.tensor_tensor(SQ[:, x, :], xT[:, x, :], xT[:, x, :], ALU.mult).then_inc(sq_ready, 1)

            def norm(l, n, gain, high_x, low_x, ready):
                if n == 1:
                    low_weights(0)
                dve.wait_ge(std_ready, n)
                link(nv.reciprocal(RSTD, STD))
                if n == 1:
                    dve.wait_ge(par_loaded, 32 * l + 32)
                for k in range(KD):
                    ins = nv.scalar_tensor_tensor(hT[:, k, :], xT[:, k, :], par[:, gain + k:gain + k + 1], RSTD, ALU.mult, ALU.mult)
                link(ins)
                high_part(high_x[:, :, :], hT[:, :, :]).then_inc(h_ready, 1)
                dve.wait_ge(h_ready, ready)
                low_part(low_x[:, :, :], hT[:, :, :], high_x[:, :, :]).then_inc(h_ready, 1)

            def rwkv_mix():
                dve.wait_ge(act_taken, 8)
                raw = proj[:, B_R:B_R + RW_BLOCKS, :]
                nv.tensor_tensor(SHIFT[:, :, 1:T], raw[:, :, 0:T - 1], raw[:, :, 1:T], ALU.subtract)
                link(nv.tensor_scalar(SHIFT[:, :, 0:1], raw[:, :, 0:1], -1.0, None, ALU.mult))
                for b in range(RW_BLOCKS):
                    ins = nv.scalar_tensor_tensor(raw[:, b, :], SHIFT[:, b, :], par[:, PL_MU + b:PL_MU + b + 1], raw[:, b, :],
                                                  ALU.mult, ALU.add)
                ins.then_inc(z_ready, 1)

            r, k, v = (proj[:, b:b + HB, :] for b in (B_R, B_K, B_V))

            def rwkv_prep():
                dve.wait_ge(z_ready, 1)
                for b in range(HB):
                    ins = nv.tensor_scalar(KK[:, b, :], k[:, b, :], par[:, PL_KK + b:PL_KK + b + 1], None, ALU.mult)
                link(ins)
                nv.tensor_tensor(X3, KK, KK, ALU.mult).then_inc(kk_sq, 1)
                low_weights(6)
                dve.wait_ge(lora_out, 8)
                for b in range(HB):
                    for t in range(TT):
                        c = slice(P * t, P * (t + 1))
                        ins = nv.tensor_tensor_scan(X2[:, b, c], ones, X1[:, b, c], 0.0, ALU.mult, ALU.add)
                link(ins)
                by_chunk = lambda a: a.rearrange("p b (t n) -> p (b t) n", n=P)
                x2c = by_chunk(X2)
                mid = small[:, 0:8]
                link(nv.tensor_copy(mid, x2c[:, :, P // 2 - 1]))
                nv.tensor_tensor(x2c, x2c, mid.unsqueeze(2).broadcast_to([P, 8, P]), ALU.subtract).then_inc(cum_ready, 1)
                dve.wait_ge(cum_ready, 1)
                nv.tensor_tensor(X1, X2, X1, ALU.subtract).then_inc(cum_ready, 1)
                low_weights(7)
                dve.wait_ge(kk_std, 1)
                link(nv.tensor_scalar(Y, Y, 1e-12, None, ALU.max))
                link(nv.reciprocal(Y, Y))
                link(nv.tensor_tensor(KK, KK, Y, ALU.mult))
                for b in range(HB):
                    ins = nv.tensor_scalar(Y[:, b, :], AT[:, b, :], -1.0, par[:, PL_KA + b:PL_KA + b + 1], ALU.add, ALU.mult)
                link(ins)
                link(nv.scalar_tensor_tensor(k, Y, 1.0, k, ALU.add, ALU.mult))
                link(nv.tensor_tensor(AT, KK, AT, ALU.mult))
                dve.wait_ge(exps_ready, 4)
                arv = AR.rearrange("p b t s n -> p (b t) s n")
                nv.tensor_tensor(arv[:, :, 1, :], by_chunk(r), by_chunk(X3), ALU.mult)
                nv.scalar_tensor_tensor(arv[:, :, 0, :], by_chunk(KK), -1.0, by_chunk(X1), ALU.mult, ALU.mult)
                nv.tensor_tensor(AT, AT, X2, ALU.mult)
                link(nv.tensor_tensor(SC, X3[:, :, P - 1], MIDE, ALU.mult))
                nv.tensor_tensor(KK, k, X2, ALU.mult).then_inc(gram_in, 1)
                for b in range(HB):
                    ins = nv.scalar_tensor_tensor(Y[:, b, :], r[:, b, :], par[:, PL_RK + b:PL_RK + b + 1], k[:, b, :], ALU.mult, ALU.mult)
                ins.then_inc(bonus_in, 1)

            def rwkv_chunk(l, t):
                dve.wait_ge(gm_zero, 1)
                dve.wait_ge(gram_in, 1)
                if t:
                    dve.wait_ge(y_ready, 1)
                    dve.wait_ge(s_ready, 1)
                else:
                    dve.wait_ge(bonus_in, 1)
                nv.tensor_copy(QT.rearrange("p h s n -> p (h s) n"), ident.unsqueeze(1).broadcast_to([P, 2 * HEADS, P])).then_inc(qt_ready, 1)
                mask = con[:, C_GRAM:C_GRAM + 512].bitcast(U32)
                for h in range(HEADS):
                    dve.wait_ge(gram_ready, 8 * t + h + 1)
                    nv.copy_predicated(GM[:, h, :], mask, PS[:, 2 + h % 2 + 2 * (h // 2 % 2), :]).then_inc(gram_taken, 1)
                dve.wait_ge(qt_ready, t * (2 * LEVELS + 1) + 1)
                for lev in range(LEVELS):
                    lm = con[:, C_LVL + P * lev:C_LVL + P * (lev + 1)]
                    for half in range(2):
                        i = (t * LEVELS + lev) * 2 + half
                        u = slice(4 * half, 4 * half + 4)
                        dve.wait_ge(w1_ready, i + 1)
                        nv.tensor_tensor(W1S[:, u, :], banks(6 + half, 1, 4, P), lm.unsqueeze(1).broadcast_to([P, 4, P]), ALU.mult)\
                            .then_inc(w1_masked, 1)
                    if lev in ADA_AT[t]:
                        n = ADA_AT[t][lev]
                        dve.wait_ge(block_done, done(l, Q_ADA[n]))
                        rows = PS[:, Q_ADA[n] % 2, :]
                        if n == 0:
                            nv.tensor_copy(mod_rows[:, :], rows).then_inc(dve_taken, 1)
                        else:
                            dve.wait_ge(dve_taken, TAKEN[Q_ADA[n] - 1])
                            nv.tensor_tensor(mod_rows[:, :], rows, mod_rows[:, :], ALU.add).then_inc(dve_taken, 1)
                    if lev == COLS_AT[t]:
                        dve.wait_ge(block_done, done(l, Q_COLS))
                        m = MOD2[:, l, :, :]
                        nv.tensor_tensor(m, PS[:, Q_COLS % 2, 0:4 * N_ADA].rearrange("p (n b) -> p n b", b=N_ADA), m, ALU.add).then_inc(dve_taken, 1)
                    for half in range(2):
                        i = (t * LEVELS + lev) * 2 + half
                        u = slice(4 * half, 4 * half + 4)
                        dve.wait_ge(dq_ready, i + 1)
                        add = banks(2 + 2 * half, 2, 4, 2 * P)
                        for side in range(2):
                            q = every_other(QT[:, u, side, :], lev, 1 - side)
                            ins = nv.tensor_tensor(q, q, every_other(add[:, :, P * side:P * (side + 1)], lev, 1 - side), ALU.add)
                        ins.then_inc(qt_ready, 1)
                mix(l, 0, 2 * t, 2 * t + 2)
                if t == 0:
                    dve.wait_ge(s_ready, 1)
                    nv.tensor_tensor(ST, banks(5, 1, HB, HD), SC.unsqueeze(2).broadcast_to([P, HB, HD]), ALU.mult).then_inc(st_ready, 1)

            def attention(l):
                q, kk = proj[:, B_AQ:B_AQ + HB, :], proj[:, B_AK, :]
                dve.wait_ge(act_taken, 10)
                dve.wait_ge(block_done, done(l, 2 * SPLIT_A - 1))
                nv.tensor_tensor(ATS[:, 0:HB, :], q, q, ALU.mult).then_inc(att_sq, 1)
                nv.tensor_tensor(ATS[:, HB, :], kk, kk, ALU.mult).then_inc(att_sq, 1)
                dve.wait_ge(bonus_ss, 1)
                nv.tensor_tensor(r, banks(2, 2, HB, T), v, ALU.mult).then_inc(bonus_out, 1)
                dve.wait_ge(bonus_out, 1)
                dve.wait_ge(lora_out, 10)
                for b in range(HB):
                    ins = nv.scalar_tensor_tensor(r[:, b, :], r[:, b, :], par[:, PL_LB + b:PL_LB + b + 1], GT[:, b, :], ALU.add, ALU.mult)
                link(ins)
                for b in range(HB):
                    ins = nv.tensor_scalar(GT[:, b, :], GT[:, b, :], par[:, PL_LG + b:PL_LG + b + 1], None, ALU.mult)
                link(ins)
                dve.wait_ge(att_std, 2)
                link(nv.reciprocal(ATS, ATS))
                nv.scalar_tensor_tensor(q, q, par[:, PL_QN:PL_QN + 1], ATS[:, 0:HB, :], ALU.mult, ALU.mult).then_inc(att_qk, 1)
                nv.scalar_tensor_tensor(kk, kk, par[:, PL_KN:PL_KN + 1], ATS[:, HB, :], ALU.mult, ALU.mult).then_inc(att_qk, 1)
                at = 0
                for rnd, (t, heads) in enumerate(ROUNDS):
                    n, w = len(heads), P * (t + 1)
                    s = SCO.rearrange("p (a b) -> p a b", b=w)
                    wide = lambda a: a[:, 0:n].unsqueeze(2).broadcast_to([P, n, w])
                    mask = con[:, C_BAND:C_BAND + w] if t else con[:, C_CAUSAL:C_CAUSAL + P]
                    sink = par[:, PL_SINK + at:PL_SINK + at + n]
                    at += n
                    dve.wait_ge(sc_ready, rnd + 1)
                    if rnd:
                        dve.wait_ge(pt_ready, rnd)
                    link(nv.scalar_tensor_tensor(s, banks(2, 2, n, w), HD ** -0.5, mask.unsqueeze(1).broadcast_to([P, n, w]), ALU.mult, ALU.add))
                    link(nv.tensor_reduce(MX[:, 0:n], s, AX, ALU.max))
                    link(nv.tensor_tensor(MM[:, 0:n], MX[:, 0:n], sink, ALU.max))
                    link(nv.tensor_tensor(s, s, wide(MM), ALU.subtract))
                    nv.tensor_tensor(SK[:, 0:n], sink, MM[:, 0:n], ALU.subtract).then_inc(sc_max, 1)
                    dve.wait_ge(sc_exp, 2 * (rnd + 1))
                    link(nv.tensor_reduce(SUM[:, 0:n], s, AX, ALU.add))
                    link(nv.tensor_tensor(SUM[:, 0:n], SUM[:, 0:n], SK[:, 0:n], ALU.add))
                    link(nv.reciprocal(SUM[:, 0:n], SUM[:, 0:n]))
                    nv.tensor_tensor(s, s, wide(SUM), ALU.mult).then_inc(p_ready, 1)

            def rwkv_norm_and_retention(l):
                dve.wait_ge(ln_ss, 1)
                dve.wait_ge(y_out, 2)
                link(nv.scalar_tensor_tensor(Y, banks(4, 2, HB, T), -1.0 / HD, Y, ALU.mult, ALU.add))
                nv.tensor_tensor(X1, Y, Y, ALU.mult).then_inc(ln_in, 1)
                sin = con[:, C_SIN:C_SIN + T].unsqueeze(1).broadcast_to([P, HB, T])
                dve.wait_ge(act_taken, 18)
                for n, at in enumerate((B_RQ, B_RK)):
                    x = proj[:, at:at + HB, :]
                    dve.wait_ge(rot_ready, n + 1)
                    link(nv.tensor_tensor(XR, banks(2 + 2 * n, 2, HB, T), sin, ALU.mult))
                    dve.wait_ge(pool_made, n + 1)
                    nv.tensor_tensor(x, x, XR, ALU.add).then_inc(rot_out, 1)
                    dve.wait_ge(rot_out, n + 1)
                nv.tensor_tensor(Y, Y, GT, ALU.mult)
                dve.wait_ge(ln_std, 1)
                link(nv.reciprocal(X2, X2))
                link(nv.tensor_tensor(Y, Y, X2, ALU.mult))
                nv.tensor_tensor(Y, Y, r, ALU.add).then_inc(ob_ready, 1)
                dve.wait_ge(dec_loaded, 16)
                for h in range(HEADS):
                    dve.wait_ge(rs_ready, h + 1)
                    nv.tensor_tensor(SM[:, h, :], PS[:, 2 + h % 2 + 2 * (h // 2 % 2), 0:3 * P], DEC[:, h, :], ALU.mult).then_inc(rs_out, 1)
                o = proj[:, B_RQ:B_RQ + HB, :]
                mix(l, 1, 0, 1)
                dve.wait_ge(oc_out, 1)
                nv.tensor_tensor(XR, o, o, ALU.mult).then_inc(oc_sq, 1)
                mix(l, 1, 1, 2)
                dve.wait_ge(oc_std, 1)
                link(nv.reciprocal(XR, XR))
                dve.wait_ge(pool_made, 3)
                nv.tensor_tensor(o, GATED, XR, ALU.mult).then_inc(oc_ready, 1)
                mix(l, 1, 2, 4)

            def mix(l, br, lo, hi):
                for i in range(lo, hi):
                    q = Q_MIX[br][i]
                    gate = proj[:, B_GATE + KD * br + 2 * i:B_GATE + KD * br + 2 * i + 2, :]
                    out = hT[:, 2 * i:2 * i + 2, :]
                    dve.wait_ge(block_done, done(l, q))
                    ps = banks(q % 2, 1, 2, T)
                    if br == 0:
                        nv.tensor_tensor(out, ps, gate, ALU.mult).then_inc(dve_taken, 1)
                    else:
                        link(nv.tensor_tensor(gate, ps, gate, ALU.mult))
                        if i == 0:
                            dve.wait_ge(dve_taken, TAKEN[q - 1])
                        nv.tensor_tensor(out, out, gate, ALU.add).then_inc(dve_taken, 1)
                    if br == 2:
                        dve.wait_ge(dve_taken, TAKEN[q])
                        h = XH_F[:, 2 * i:2 * i + 2, :]
                        link(high_part(h, out))
                        ins = low_part(hT_low[:, 2 * i:2 * i + 2, :], out, h)
                        if i == 3:
                            ins.then_inc(h_ready, 1)
                        if i in (0, 3):
                            low_weights(S_OUT + i // 3)

            def residual(l, q0, n, blocks, next_slots):
                for i in range(n):
                    dve.wait_ge(block_done, done(l, q0 + i))
                    x = xT[:, blocks * i:blocks * (i + 1), :]
                    nv.tensor_tensor(x, x, banks((q0 + i) % 2, 1, blocks, T), ALU.add).then_inc(dve_taken, 1)
                    if blocks == 2:
                        dve.wait_ge(dve_taken, TAKEN[q0 + i])
                        square(i)
                    if i in next_slots:
                        low_weights(next_slots[i])
                dve.wait_ge(dve_taken, TAKEN[q0 + n - 1])

            def ffn(l):
                for n in range(N_FFN // 2):
                    dve.wait_ge(block_done, done(l, Q_FFN + 2 * n + 1))
                    dve.wait_ge(act_taken, TAKEN[Q_FFN + 2 * n])
                    x, h = HID[:, 2 * n:2 * n + 2, :], HID_H[:, 2 * n:2 * n + 2, :]
                    nv.tensor_tensor(x, banks((Q_FFN + 1) % 2, 1, 2, T), SILU[:, n % 2, :].rearrange("p (a b) -> p a b", b=T),
                                     ALU.mult).then_inc(dve_taken, 1)
                    dve.wait_ge(dve_taken, TAKEN[Q_FFN + 2 * n + 1])
                    link(high_part(h, x))
                    ins = low_part(HID_low[:, 2 * n:2 * n + 2, :], x, h)
                    if n == N_FFN // 2 - 1:
                        ins.then_inc(h_ready, 1)
                    low_weights(S_FFN + 2 + n)

            dve.wait_ge(const_loaded, 4 * 16)
            with dve.Fori(0, LAYERS) as l:
                for n in range(4):
                    square(n)
                norm(l, 1, PL_G1, XH_A, XL_A, 1)
                for n in range(1, 5):
                    low_weights(n)
                rwkv_mix()
                low_weights(5)
                rwkv_prep()
                attention(l)
                rwkv_chunk(l, 0)
                rwkv_chunk(l, 1)
                rwkv_norm_and_retention(l)
                mix(l, 2, 0, 4)
                residual(l, Q_OUT, N_OUT, 2, {1: S_FFN})
                norm(l, 2, PL_G2, XH_F, hT_low, 4)
                low_weights(S_FFN + 1)
                ffn(l)
                residual(l, Q_DOWN, N_DOWN, 1, {i: S_DOWN + 2 + i for i in range(N_DOWN - 2)})
                dve.sem_inc(layer_fin, 1)
                dve.wait_ge(layer_go, l + 1)
                dve.sem_inc(layer_joined, 1)
            second_vector(dve)


_NATURAL = ["w_ada_2", "w_in", "w_attn_o", "w_rwkv_o", "w_ret_o", "w_out", "w_ffn_gate", "w_ffn_up", "w_ffn_down",
            "w_in_2", "w_out_2", "hy_w1_2", "hy_w2_2", "hy_w3_2", "hy_deltas_2", "w_gate_2", "w_up_2", "w_down_2"]


def kernel(**inputs):
    import concourse.bacc as bacc
    from concourse.bass_utils import run_bass_kernel_spmd

    a = {n: np.asarray(v) for n, v in inputs.items()}
    arrays = {n: np.ascontiguousarray(a[n]) for n in _NATURAL}
    blocks = lambda m: np.ascontiguousarray(m.reshape(KD, P, -1).transpose(1, 0, 2))
    one_more = lambda layers: np.stack(layers + [np.zeros_like(layers[0])])
    arrays["xT"] = blocks(a["x"][0].T)
    cond = np.zeros((P, KD, 64), a["c_2"].dtype)
    cond[:, :, 32] = a["c_2"].reshape(KD, P).T
    arrays["cond"] = cond
    arrays["ada_bias"] = columns(a["b_ada_2"][0])
    arrays["router"] = blocks(a["w_router_2"][0])
    arrays["layer_params"] = one_more([pack_layer(a, l) for l in range(LAYERS)])
    arrays["layer_lora"] = one_more([pack_lora(a, l) for l in range(LAYERS)])
    arrays["params_2"] = pack_second(a)
    arrays["constants"], arrays["decay"] = layer_constants()
    arrays["constants_2"] = second_constants()

    nc = bacc.Bacc("TRN2", target_bir_lowering=False, num_devices=1)
    io = {}
    for n, v in arrays.items():
        v = arrays[n] = np.ascontiguousarray(v)
        io[n] = nc.dram_tensor(f"in_{n}", v.shape, mybir.dt.from_np(v.dtype), kind="ExternalInput").ap()
    io["yT"] = nc.dram_tensor("out_yT", (D, T), F32, kind="ExternalOutput").ap()
    build(nc, io)
    r = run_bass_kernel_spmd(nc, [{f"in_{n}": v for n, v in arrays.items()}], core_ids=[0])
    return np.ascontiguousarray(r.results[0]["out_yT"].T)[None]
```
